# Optimizing a Trainium2 kernel written in Bass

```python
import math
import jax, jax.numpy as jnp
from jax import lax
import numpy as np

D_MODEL = 1024
BATCH = 1
SEQ = 512
DEPTH = 2

HEAD_DIM = 64
N_MEM = 256
MEM_HEADS = 4
MEM_WIDTH = MEM_HEADS * HEAD_DIM
RWKV_HEADS = 12
RWKV_WIDTH = RWKV_HEADS * HEAD_DIM
DECAY_LORA = 64
AAA_LORA = 64
GATE_LORA = 128
SHIFT_WIDTH = 3 * RWKV_WIDTH + DECAY_LORA + AAA_LORA + GATE_LORA
A_IN_WIDTH = SHIFT_WIDTH + MEM_WIDTH
A_OUT_WIDTH = RWKV_WIDTH + MEM_WIDTH
DIL_GROUPS = ((128, 1), (512, 4), (2048, 16))
DIL_HEADS_PER_GROUP = 4
DIL_HEADS = DIL_HEADS_PER_GROUP * len(DIL_GROUPS)
DIL_WIDTH = DIL_HEADS * HEAD_DIM
DIL_BLOCK = 128
B_IN_WIDTH = DIL_WIDTH + MEM_WIDTH
B_OUT_WIDTH = DIL_HEADS_PER_GROUP * HEAD_DIM + MEM_WIDTH
D_FF = 2816
CONV_WIDTH = 3
ROPE_THETA = 10000.0
RMS_EPS = 1e-6
LNX_EPS = 64e-5
NEG_INF = -1e30
N_A = DEPTH // 2
N_B = DEPTH - N_A

kernel_name = "yoco_rwkv7_dilated_memory_convffn"

def f32(a):
    return a.astype(jnp.float32)

def rmsnorm(x, g):
    xf = f32(x)
    return xf * lax.rsqrt(jnp.mean(xf * xf, axis=-1, keepdims=True) + RMS_EPS) * f32(g)

def rope_tables(T):
    inv = ROPE_THETA ** (-jnp.arange(0, HEAD_DIM, 2, dtype=jnp.float32) / HEAD_DIM)
    ang = jnp.arange(T, dtype=jnp.float32)[:, None] * inv[None, :]
    return jnp.cos(ang)[:, None, :], jnp.sin(ang)[:, None, :]

def apply_rope(z, cos, sin):
    half = HEAD_DIM // 2
    z1, z2 = z[..., :half], z[..., half:]
    return jnp.concatenate([z1 * cos - z2 * sin, z2 * cos + z1 * sin], axis=-1)

def rwkv7_time_mix(p, mu, w0, w2, a0, a2, g2, k_k, k_a, r_k, lnx_w, lnx_b):
    B, T, _ = p.shape
    prev = jnp.pad(p[:, :-1], ((0, 0), (1, 0), (0, 0)))
    xs = p + (prev - p) * f32(mu)
    cuts = np.cumsum([RWKV_WIDTH, RWKV_WIDTH, RWKV_WIDTH, DECAY_LORA, AAA_LORA]).tolist()
    r, k, v, wd, ad, gd = jnp.split(xs, cuts, axis=-1)
    w_log = -jax.nn.softplus(-(f32(w0) + jnp.tanh(wd) @ f32(w2))) - 0.5
    decay = jnp.exp(-jnp.exp(w_log))
    a = jax.nn.sigmoid(f32(a0) + ad @ f32(a2))
    g = jax.nn.sigmoid(gd) @ f32(g2)
    heads = lambda z: z.reshape(B, T, RWKV_HEADS, HEAD_DIM)
    kk = heads(k * f32(k_k))
    kk = kk / jnp.maximum(jnp.linalg.norm(kk, axis=-1, keepdims=True), 1e-12)
    k = k * (1.0 + (a - 1.0) * f32(k_a))
    r_h, k_h, v_h, w_h, a_h = heads(r), heads(k), heads(v), heads(decay), heads(a)

    def step(S, inp):
        r_t, w_t, k_t, v_t, kk_t, a_t = inp
        sa = jnp.einsum('bhvk,bhk->bhv', S, -kk_t)
        S = (S * w_t[:, :, None, :] + sa[..., None] * (kk_t * a_t)[:, :, None, :]
             + v_t[..., None] * k_t[:, :, None, :])
        return S, jnp.einsum('bhvk,bhk->bhv', S, r_t)

    seq = tuple(jnp.moveaxis(z, 1, 0) for z in (r_h, w_h, k_h, v_h, kk, a_h))
    S0 = jnp.zeros((B, RWKV_HEADS, HEAD_DIM, HEAD_DIM), jnp.float32)
    _, ys = lax.scan(step, S0, seq)
    y = jnp.moveaxis(ys, 0, 1)
    m = jnp.mean(y, axis=-1, keepdims=True)
    var = jnp.mean((y - m) ** 2, axis=-1, keepdims=True)
    y = ((y - m) * lax.rsqrt(var + LNX_EPS)).reshape(B, T, RWKV_WIDTH) * f32(lnx_w) + f32(lnx_b)
    bonus = (jnp.sum(r_h * k_h * f32(r_k), axis=-1, keepdims=True) * v_h).reshape(B, T, RWKV_WIDTH)
    return (y + bonus) * g

def dilated_group_attention(q, k, v, window, dilation):
    B, T, H, Dh = q.shape
    back = window // dilation
    span = dilation * DIL_BLOCK
    Tp = ((T + span - 1) // span) * span
    U = Tp // dilation
    nb = U // DIL_BLOCK

    def to_blocks(z):
        z = jnp.pad(z, ((0, 0), (0, Tp - T), (0, 0), (0, 0)))
        z = z.reshape(B, U, dilation, H, Dh).transpose(0, 3, 2, 1, 4)
        return z.reshape(B, H, dilation, nb, DIL_BLOCK, Dh)

    def with_prev(z):
        prev = jnp.pad(z, ((0, 0), (0, 0), (0, 0), (1, 0), (0, 0), (0, 0)))[:, :, :, :-1]
        return jnp.concatenate([prev, z], axis=4)

    qb = to_blocks(q)
    kw, vw = with_prev(to_blocks(k)), with_prev(to_blocks(v))
    s = jnp.einsum('bhrnid,bhrnjd->bhrnij', qb, kw) / math.sqrt(Dh)
    i = jnp.arange(DIL_BLOCK)[:, None]
    jj = jnp.arange(2 * DIL_BLOCK)[None, :]
    dist = DIL_BLOCK + i - jj
    band = (dist >= 0) & (dist <= back)
    valid = band[None] & ((jnp.arange(nb) > 0)[:, None, None] | (jj >= DIL_BLOCK)[None])
    s = jnp.where(valid, s, NEG_INF)
    mx = jnp.max(s, axis=-1, keepdims=True)
    pr = jnp.exp(s - mx)
    den = jnp.sum(pr, axis=-1, keepdims=True)
    o = jnp.einsum('bhrnij,bhrnjd->bhrnid', pr, vw) / den
    lse = (mx + jnp.log(den))[..., 0]
    o = o.reshape(B, H, dilation, U, Dh).transpose(0, 3, 2, 1, 4).reshape(B, Tp, H, Dh)[:, :T]
    lse = lse.reshape(B, H, dilation, U).transpose(0, 3, 2, 1).reshape(B, Tp, H)[:, :T]
    return o, lse

def dilated_attention(q, k, v):
    B, T = q.shape[:2]
    outs, lses = [], []
    for gi, (win, dil) in enumerate(DIL_GROUPS):
        hs = slice(gi * DIL_HEADS_PER_GROUP, (gi + 1) * DIL_HEADS_PER_GROUP)
        o, l = dilated_group_attention(q[:, :, hs], k[:, :, hs], v[:, :, hs], win, dil)
        outs.append(o)
        lses.append(l)
    wgt = jax.nn.softmax(jnp.stack(lses, axis=0), axis=0)
    o = jnp.sum(wgt[..., None] * jnp.stack(outs, axis=0), axis=0)
    return o.reshape(B, T, DIL_HEADS_PER_GROUP * HEAD_DIM)

def memory_attention(q, mem, norm_g, w_kv, q_norm, k_norm):
    B, T, _ = q.shape
    M = mem.shape[1]
    kv = f32(rmsnorm(mem, norm_g).astype(mem.dtype) @ w_kv)
    k = rmsnorm(kv[..., :MEM_WIDTH].reshape(B, M, MEM_HEADS, HEAD_DIM), k_norm)
    v = kv[..., MEM_WIDTH:].reshape(B, M, MEM_HEADS, HEAD_DIM)
    qh = rmsnorm(q.reshape(B, T, MEM_HEADS, HEAD_DIM), q_norm)
    s = jnp.einsum('bthd,bmhd->bhtm', qh, k) / math.sqrt(HEAD_DIM)
    p = jax.nn.softmax(s, axis=-1)
    return jnp.einsum('bhtm,bmhd->bthd', p, v).reshape(B, T, MEM_WIDTH)

def conv_ffn(x, g, w_up, conv_w, conv_b, w_down):
    T = x.shape[1]
    u = f32(rmsnorm(x, g).astype(x.dtype) @ w_up)
    up = jnp.pad(u, ((0, 0), (CONV_WIDTH - 1, 0), (0, 0)))
    c = f32(conv_b) + sum(f32(conv_w[j]) * up[:, j:j + T] for j in range(CONV_WIDTH))
    gate, val = jnp.split(c, 2, axis=-1)
    z = jax.nn.silu(gate) * val
    return z.astype(x.dtype) @ w_down

def setup_inputs(seed: int = 0) -> dict:
    key = jax.random.key(seed)
    ks = iter(jax.random.split(key, 40))
    D = D_MODEL

    def nrm(shape, scale):
        return scale * jax.random.normal(next(ks), shape, jnp.float32)

    def unif(shape, lo, hi):
        return jax.random.uniform(next(ks), shape, jnp.float32, lo, hi)

    def gain(shape):
        return 1.0 + nrm(shape, 0.02)

    return {
        "x": nrm((BATCH, SEQ, D), 1.0),
        "mem": nrm((BATCH, N_MEM, D), 1.0),
        "attn_norm": gain((DEPTH, D)),
        "a_w_in": nrm((N_A, D, A_IN_WIDTH), D ** -0.5),
        "a_mu": unif((N_A, SHIFT_WIDTH), 0.0, 1.0),
        "a_w0": unif((N_A, RWKV_WIDTH), -5.0, 0.0),
        "a_w2": nrm((N_A, DECAY_LORA, RWKV_WIDTH), 0.5 * DECAY_LORA ** -0.5),
        "a_a0": nrm((N_A, RWKV_WIDTH), 0.5),
        "a_a2": nrm((N_A, AAA_LORA, RWKV_WIDTH), AAA_LORA ** -0.5),
        "a_g2": nrm((N_A, GATE_LORA, RWKV_WIDTH), GATE_LORA ** -0.5),
        "a_k_k": 0.85 + nrm((N_A, RWKV_WIDTH), 0.05),
        "a_k_a": 1.0 + nrm((N_A, RWKV_WIDTH), 0.05),
        "a_r_k": nrm((N_A, RWKV_HEADS, HEAD_DIM), 0.1),
        "a_lnx_w": gain((N_A, RWKV_WIDTH)),
        "a_lnx_b": nrm((N_A, RWKV_WIDTH), 0.02),
        "a_w_out": nrm((N_A, A_OUT_WIDTH, D), A_OUT_WIDTH ** -0.5),
        "kv_norm": gain((D,)),
        "kv_w": nrm((D, 2 * DIL_WIDTH), D ** -0.5),
        "kv_k_norm": gain((HEAD_DIM,)),
        "b_w_in": nrm((N_B, D, B_IN_WIDTH), D ** -0.5),
        "b_q_norm": gain((N_B, HEAD_DIM)),
        "b_w_out": nrm((N_B, B_OUT_WIDTH, D), B_OUT_WIDTH ** -0.5),
        "mem_norm": gain((DEPTH, D)),
        "mem_w_kv": nrm((DEPTH, D, 2 * MEM_WIDTH), D ** -0.5),
        "mem_q_norm": gain((DEPTH, HEAD_DIM)),
        "mem_k_norm": gain((DEPTH, HEAD_DIM)),
        "ffn_norm": gain((DEPTH, D)),
        "ffn_w_up": nrm((DEPTH, D, 2 * D_FF), D ** -0.5),
        "ffn_conv_w": nrm((DEPTH, CONV_WIDTH, 2 * D_FF), CONV_WIDTH ** -0.5),
        "ffn_conv_b": nrm((DEPTH, 2 * D_FF), 0.02),
        "ffn_w_down": nrm((DEPTH, D_FF, D), D_FF ** -0.5),
    }

def reference(x, mem, attn_norm, a_w_in, a_mu, a_w0, a_w2, a_a0, a_a2, a_g2, a_k_k, a_k_a,
              a_r_k, a_lnx_w, a_lnx_b, a_w_out, kv_norm, kv_w, kv_k_norm, b_w_in, b_q_norm,
              b_w_out, mem_norm, mem_w_kv, mem_q_norm, mem_k_norm, ffn_norm, ffn_w_up,
              ffn_conv_w, ffn_conv_b, ffn_w_down):
    B, T, _ = x.shape
    cos, sin = rope_tables(T)
    k_sh = v_sh = None
    for i in range(DEPTH):
        h = rmsnorm(x, attn_norm[i]).astype(x.dtype)
        if i < N_A:
            j = i
            p = f32(h @ a_w_in[j])
            y_mix = rwkv7_time_mix(p[..., :SHIFT_WIDTH], a_mu[j], a_w0[j], a_w2[j], a_a0[j],
                                   a_a2[j], a_g2[j], a_k_k[j], a_k_a[j], a_r_k[j],
                                   a_lnx_w[j], a_lnx_b[j])
            q_mem = p[..., SHIFT_WIDTH:]
            w_out = a_w_out[j]
        else:
            j = i - N_A
            if j == 0:
                kvp = f32(rmsnorm(x, kv_norm).astype(x.dtype) @ kv_w)
                k_sh = apply_rope(rmsnorm(kvp[..., :DIL_WIDTH].reshape(B, T, DIL_HEADS, HEAD_DIM),
                                          kv_k_norm), cos, sin)
                v_sh = kvp[..., DIL_WIDTH:].reshape(B, T, DIL_HEADS, HEAD_DIM)
            p = f32(h @ b_w_in[j])
            q = apply_rope(rmsnorm(p[..., :DIL_WIDTH].reshape(B, T, DIL_HEADS, HEAD_DIM),
                                   b_q_norm[j]), cos, sin)
            y_mix = dilated_attention(q, k_sh, v_sh)
            q_mem = p[..., DIL_WIDTH:]
            w_out = b_w_out[j]
        y_mem = memory_attention(q_mem, mem, mem_norm[i], mem_w_kv[i], mem_q_norm[i], mem_k_norm[i])
        y = jnp.concatenate([y_mix, y_mem], axis=-1).astype(x.dtype)
        x = x + y @ w_out
        x = x + conv_ffn(x, ffn_norm[i], ffn_w_up[i], ffn_conv_w[i], ffn_conv_b[i], ffn_w_down[i])
    return x


_drawn_inputs = setup_inputs


def setup_inputs(seed=0):
    import zlib

    import numpy as np

    out = dict(_drawn_inputs(seed))
    spreads = {}
    factors = {'attn_norm': 2.718,
     'a_w2': 3.531,
     'a_k_k': 3.132,
     'a_lnx_w': 5.206,
     'a_lnx_b': 5.376,
     'kv_norm': 8.0,
     'kv_k_norm': 8.0,
     'b_q_norm': 8.0,
     'mem_norm': 8.0,
     'mem_q_norm': 8.0,
     'mem_k_norm': 8.0,
     'ffn_norm': 2.939,
     'ffn_conv_b': 2.906}
    for name, (base, spread) in spreads.items():
        noise = np.random.default_rng([zlib.crc32(name.encode()), seed]).standard_normal(out[name].shape)
        drawn = base * np.exp(spread * noise) if base else spread * noise
        out[name] = __import__('jax').numpy.asarray(drawn.astype(out[name].dtype))
    for name, factor in factors.items():
        out[name] = (out[name] * factor).astype(out[name].dtype)
    return out
```

```python
from contextlib import ExitStack

import numpy as np

import concourse.bass as bass
from concourse import mybir

F32 = mybir.dt.float32
ALU = mybir.AluOpType
ACT = mybir.ActivationFunctionType
AX = mybir.AxisListType

P = 128
T = 512
D = 1024
KD = D // P
HD = 64
NMEM = 256
MEMH = 4
PAIRS = 6
CHUNK = 128
NCH = T // CHUNK
PAD = CHUNK + 1
LEVELS = 6
ADDS = 4 * LEVELS - 2
FF = 2816
FT = FF // P
RES = 4
SLOTS = 4
SLOTW = FT // 2 * P
TILEW = KD * P
LNX_EPS = 64e-5
RMS_EPS = 1e-6
DECAY = -float(np.exp(-0.5))
NPAR = 10
MUK, MUR, MUV, PW0, PA0, KKP, KAP, RKP, LNW, LNB = range(NPAR)
N_LORA, N_QM0, N_OUTA, N_UP0, N_DOWN0, N_K, N_Q, N_QM1, N_V = 0, 2, 4, 12, 56, 72, 78, 84, 86
N_OUTB, N_UP1, N_DOWN1, N_END = 92, 96, 140, 156
U_MK, U_QM0, U_K, U_Q, U_QM1, U_END = 0, 4, 6, 12, 18, 20
C_ID, C_ONE, C_BLK, C_ROT, C_TRI, C_LEV = 0, 128, 256, 384, 512, 768
C_RESET = C_LEV + (LEVELS + 2) * P
C_END = C_RESET + NCH * PAD
G_ATTN0, G_ATTN1, G_KV, G_FFN0, G_FFN1, G_MEM0, G_MEM1 = range(0, 56, 8)
G_KN, G_QN, G_MQ0, G_MQ1, G_MK0, G_MK1, MU_WA, MU_G = range(56, 64)
G_CONV = 64
G_PAIR = G_CONV + 2 * 2 * FT * 4
G_END = G_PAIR + PAIRS * NPAR
ARENA = 26700


def rounds(eng, n, body):
    body(0, True)
    with eng.Fori(1, n) as i:
        body(i, False)


def trunk(nc, xT, memT, consts, params, ropes, masks, w_small, w_mem, w_pairs, w_ring, outT):
    ctx = ExitStack()
    with ctx:
        def sb(name, shape):
            return ctx.enter_context(nc.sbuf_tensor(name, shape, F32))

        made = {}

        def sem(name):
            if name not in made:
                made[name] = ctx.enter_context(nc.semaphore(name))
            return made[name]

        x = sb("x", [P, KD, T])
        h = sb("h", [P, KD, T])
        y = sb("y", [P, KD, T])
        ring = sb("ring", [P, SLOTS, SLOTW])
        cst = sb("cst", [P, C_END])
        par = sb("par", [P, G_END])
        derived = sb("derived", [P, PAIRS * NPAR + 2])
        rstd = sb("rstd", [P, T])
        mem_k = sb("mem_k", [P, 2, 2, 2, NMEM])
        mem_v = sb("mem_v", [P, 2, 2, MEMH * HD])
        stat = sb("stat", [P, 32])
        epsb = sb("epsb", [P, 2])
        arena = sb("arena", [P, ARENA])

        ident = cst[:, C_ID:C_ID + P]
        ones = cst[:, C_ONE:C_ONE + P]
        blk = cst[:, C_BLK:C_BLK + P]
        rot = cst[:, C_ROT:C_ROT + P]
        tri = cst[:, C_TRI:C_TRI + 2 * P]
        reset = cst[:, C_RESET:C_RESET + NCH * PAD]
        rms_eps, lnx_eps = epsb[:, 0:1], epsb[:, 1:2]

        def level(v):
            return cst[:, C_LEV + v * P:C_LEV + (v + 1) * P]

        def col(i):
            return par[:, i:i + 1]

        def pcol(j, k):
            return par[:, bass.ds(NPAR * j + (G_PAIR + k), 1)]

        def dcol(j, k):
            return derived[:, bass.ds(NPAR * j + k, 1)]

        at = [0]

        def part(*shape):
            n = int(np.prod(shape))
            a = arena[:, at[0]:at[0] + n]
            at[0] += n
            assert at[0] <= ARENA, at[0]
            if len(shape) == 2:
                a = a.rearrange("p (a b) -> p a b", b=shape[1])
            if len(shape) == 3:
                a = a.rearrange("p (a b c) -> p a b c", b=shape[1], c=shape[2])
            return a

        lora_w, lora_a = part(T), part(T)
        sig_g = part(T)
        ws = part(2, P)
        kx, rx, vx, aa = part(T), part(T), part(T), part(T)
        lw, cc = part(NCH, PAD), part(NCH, PAD)
        e_pos, e_neg = part(NCH, PAD), part(NCH, PAD)
        rw_late = at[0]
        kk, kkr, sc1, sc2 = part(T), part(T), part(T), part(T)
        fa, bb, rrk = part(T), part(T), part(T)
        Bf, Kf = part(NCH, P), part(NCH, P)
        bonus, gate, ysb = part(T), part(T), part(T)
        Btok, Ktok = part(NCH, P), part(NCH, P)
        BG, KG = part(NCH, 4, P), part(NCH, 4, P)
        X, XT, CT, Y1 = part(2, NCH, P), part(2, NCH, P), part(2, NCH, P), part(2, NCH, P)
        Usb = part(P)
        Sf = part(P)
        fS = part(4)
        AR = part(NCH, 4, P)
        Vp = part(NCH * 2 * P + P)
        SAp = part(3 * P)
        S = part(P)

        at[0] = rw_late
        hn_a = (part(2, T), part(2, T), part(2, T))
        qm_a = part(2, T)
        memx, memh, mem_rs = part(KD, NMEM), part(KD, NMEM), part(NMEM)
        wmem = part(KD, 2 * MEMH * HD)
        at[0] = rw_late + 8 * T
        qs_a, pm_a, pt_a = part(2, P), part(MEMH, NMEM), part(2, MEMH, T)
        at[0] = 0
        z = part(FT, T)
        conv = part(4, T)
        silu = part(2, T)
        at[0] = 0
        h2 = part(KD, T)
        kp = part(12, T)
        cosT, sinT = part(T), part(T)
        rope_b = at[0]
        hz, t1 = part(2, T), part(2, T)
        qT = part(6, T)
        vtok = part(RES, 6 * P)
        qm_b = part(2, T)
        hn_b = (part(2, T), part(2, T), part(2, T))
        pr, pT = part(2, 6 * P), part(2, 6 * P)
        at[0] = rope_b
        sm = part(2, 6 * P)
        at[0] = 0
        mask0, mask12 = part(RES, T), part(2 * P)
        qS, vS = part(6, P), part(T)
        assert at[0] <= KD * T
        at[0] = 0
        qs_b, pm_b, pt_b = part(2, P), part(MEMH, NMEM), part(2, MEMH, T)

        bank = [ctx.enter_context(nc.psum_tensor(f"bank{i}", [P, T], F32)) for i in range(8)]
        mem_attn = [dict(q=qm_a, qs=qs_a, p=pm_a, pt=pt_a, y=6), dict(q=qm_b, qs=qs_b, p=pm_b, pt=pt_b, y=2)]
        landed = [sem(f"landed{i}") for i in range(SLOTS)]
        used = sem("ring_used")

        def flat(a):
            return a.rearrange("p a b -> p (a b)")

        def diag(a, base=0):
            return a[:, base:base + 3 * P].rearrange("p (h w) -> p h w", w=3 * HD)[:, :, 0:HD]

        def by_residue(a):
            return a.rearrange("p (u r) -> p r u", r=RES)

        def heads_of(u):
            raw, sq, rs = hn_b if u >= U_K else hn_a
            n = NMEM if u < U_QM0 else T
            return raw[:, u % 2, 0:n], sq[:, u % 2, 0:n], rs[:, u % 2, 0:n], n

        block = ctx.enter_context(nc.Block())

        @block.sync
        def _(sp):
            sp.dma_start(memx, memT).then_inc(sem("mem_in"), 16)
            sp.dma_start(cst[:, :], consts).then_inc(sem("const_in"), 16)
            sp.dma_start(par[:, :], params).then_inc(sem("par_in"), 16)
            sp.dma_start(wmem, w_mem[0]).then_inc(sem("wmem_in"), 16)
            sp.dma_start(x[:, :, :], xT).then_inc(sem("x_in"), 16)

            def ring_tile(n, i, wide=False):
                w = SLOTW if wide else TILEW
                sp.dma_start(ring[:, i, 0:w], w_ring[bass.ds(n, 1), :, 0:w].rearrange("a p w -> (a p) w"))\
                  .then_inc(landed[i], 16)

            for n in range(SLOTS):
                ring_tile(n, n)
            sp.wait_ge(sem("mv_mm"), 2)
            sp.dma_start(wmem, w_mem[1]).then_inc(sem("wmem_in"), 16)
            sp.dma_start(ws, w_small[0].rearrange("p (a m) -> p a m", m=P)).then_inc(sem("ws_in"), 16)
            sp.wait_ge(used, N_OUTA)
            for i in range(3):
                sp.dma_start(ring[:, i, 0:TILEW], w_pairs[0, i]).then_inc(sem(f"wp_in{i}"), 16)
            with sp.Fori(1, PAIRS) as j:
                for i, name in enumerate(("k_mm", "r_mm", "v_mm")):
                    sp.wait_ge(sem(name), j)
                    sp.dma_start(ring[:, i, 0:TILEW],
                                 w_pairs[bass.ds(j, 1), i, :, :].rearrange("a p w -> (a p) w"))\
                      .then_inc(sem(f"wp_in{i}"), 16)
                sp.wait_ge(sem("g_mm"), j)
                sp.dma_start(ws, w_small[bass.ds(j, 1)].rearrange("a p (b m) -> (a p) b m", m=P))\
                  .then_inc(sem("ws_in"), 16)
            for n, name in zip(range(N_OUTA, N_OUTA + SLOTS), ("k_mm", "r_mm", "v_mm", "v_mm")):
                sp.wait_ge(sem(name), PAIRS)
                ring_tile(n, n % SLOTS)

            def stream(n0, n1):
                for n in range(n0, n1):
                    sp.wait_ge(used, n - SLOTS + 1)
                    ring_tile(n, n % SLOTS)

            def stream_loop(n0, n1, wide=False):
                with sp.Fori(0, (n1 - n0) // SLOTS) as i:
                    for b in range(SLOTS):
                        sp.wait_ge(used, SLOTS * i + (n0 + b - SLOTS + 1))
                        ring_tile(SLOTS * i + (n0 + b), b, wide)

            stream(N_OUTA + SLOTS, N_UP0)
            stream_loop(N_UP0, N_DOWN0)
            stream_loop(N_DOWN0, N_K, wide=True)
            stream(N_K, N_K + SLOTS)
            sp.wait_ge(sem("x_up"), 2 * KD)
            sp.dma_start(cosT, ropes[0]).then_inc(sem("rope_in"), 16)
            sp.dma_start(sinT, ropes[1]).then_inc(sem("rope_in"), 16)
            stream(N_K + SLOTS, N_OUTB)
            sp.wait_ge(used, N_V)
            sp.dma_start(mask0, masks[:, 0:RES * T].rearrange("p (r t) -> p r t", t=T)).then_inc(sem("mask_in"), 16)
            sp.dma_start(mask12, masks[:, RES * T:RES * T + 2 * P]).then_inc(sem("mask_in"), 16)
            stream(N_OUTB, N_UP1)
            stream_loop(N_UP1, N_DOWN1)
            stream_loop(N_DOWN1, N_END, wide=True)
            for m in range(KD):
                sp.wait_ge(sem("x_up"), 3 * KD + m + 1)
                sp.dma_start(outT[m], x[:, m, :]).then_inc(sem("out"), 16)
            sp.wait_ge(sem("out"), 16 * KD)

        @block.tensor
        def _(pe):
            def mm(out, lhsT, rhs, first=True, last=True):
                return nc.tensor.matmul(out, lhsT, rhs, start=first, stop=last, skip_group_check=True)

            def head_sum(u):
                _, sq, _, n = heads_of(u)
                pe.wait_ge(sem("hn_sqd"), u + 1)
                if u >= 2:
                    pe.wait_ge(sem("hn_sd"), u - 1)
                mm(bank[2 + u % 2][:, 0:n], blk, sq).then_inc(sem("hn_ss"), 1)

            def rope_turn(u):
                pe.wait_ge(sem("hn_done"), u + 1)
                if u >= U_K + 2:
                    pe.wait_ge(sem("rope_done"), u - U_K - 1)
                mm(bank[4 + u % 2][:, :], rot, hz[:, u % 2, :]).then_inc(sem("rope_mm"), 1)

            def ring_product(out, slot, rhs, kn, base=0, ready=None):
                for k in range(kn):
                    if ready:
                        pe.wait_ge(sem(ready[0]), ready[1] + k)
                    i = mm(out, ring[:, slot, base + k * P:base + (k + 1) * P], rhs(k), k == 0, k == kn - 1)
                return i

            def head_tile(u, n, src, h_at=None):
                pe.wait_ge(landed[n % SLOTS], 16 * (n // SLOTS + 1))
                if u >= 2:
                    pe.wait_ge(sem("hn_sqd"), u - 1)
                ring_product(bank[u % 2][:, :], n % SLOTS, lambda k: src[:, k, :], KD,
                             ready=("h_ready", h_at + 1) if h_at is not None else None).then_inc(used, 1)

            pe.wait_ge(sem("const_in"), 16)
            for k in range(KD):
                pe.wait_ge(sem("msq"), k + 1)
                q = mm(bank[6][:, 0:NMEM], ones, memh[:, k, :], k == 0, k == KD - 1)
            q.then_inc(sem("mem_ss"), 1)
            for k in range(KD):
                pe.wait_ge(sem("xsq"), k + 1)
                q = mm(bank[7][:, :], ones, h[:, k, :], k == 0, k == KD - 1)
            q.then_inc(sem("x_ss"), 1)
            for l in range(2):
                pe.wait_ge(sem("wmem_in"), 16 * (l + 1))
                for i in range(2):
                    u = U_MK + 2 * l + i
                    if u >= 2:
                        pe.wait_ge(sem("hn_sqd"), u - 1)
                    for k in range(KD):
                        pe.wait_ge(sem("memh"), l * KD + k + 1)
                        q = mm(bank[u % 2][:, 0:NMEM], wmem[:, k, i * P:(i + 1) * P], memh[:, k, :], k == 0, k == KD - 1)
                    q.then_inc(sem("mk_mm"), 1)
                for i in range(2):
                    if l:
                        pe.wait_ge(sem("mv_out"), i + 1)
                    for k in range(KD):
                        q = mm(bank[4 + i][:, 0:NMEM], memh[:, k, i * P:(i + 1) * P],
                               wmem[:, k, 2 * P:4 * P], k == 0, k == KD - 1)
                    q.then_inc(sem("mv_mm"), 1)
                for i in range(2):
                    head_sum(U_MK + 2 * l + i)

            pe.wait_ge(sem("mv_out"), 4)
            for i in range(2):
                n = N_LORA + i
                pe.wait_ge(landed[n], 16)
                ring_product(bank[4 + i][:, :], n, lambda k: h[:, k, :], KD, ready=("h_ready", 1)).then_inc(used, 1)
            for i in range(2):
                head_tile(U_QM0 + i, N_QM0 + i, h)
            for i in range(2):
                head_sum(U_QM0 + i)
            pe.wait_ge(sem("lora_x"), 2)

            def memory_attention(l):
                m = mem_attn[l]

                def token_tile(c, first):
                    g = 4 * l + c
                    pe.wait_ge(sem("ma_qs"), g + 1)
                    if not first:
                        pe.wait_ge(sem("ma_exp"), 4 * g)
                    for i in range(2):
                        mm(bank[i][:, :], m["qs"][:, i, :], mem_k[:, l, i, :, :].rearrange("p h t -> p (h t)"))\
                            .then_inc(sem("ma_sc"), 1)
                    pe.wait_ge(sem("ma_pn"), g + 1)
                    if not first:
                        pe.wait_ge(sem("ma_pt"), 2 * g)
                    for t in range(2):
                        for hh in range(MEMH):
                            q = nc.tensor.transpose(bank[2 + t][:, hh * P:(hh + 1) * P],
                                                    m["p"][:, hh, t * P:(t + 1) * P], ident)
                        q.then_inc(sem("ma_tr"), 1)

                rounds(pe, RES, token_tile)
                pe.wait_ge(sem("ma_pt"), 8 * l + 8)
                for hh in range(MEMH):
                    r = HD * (hh % 2)
                    for t in range(2):
                        q = mm(bank[4 + hh // 2][r:r + HD, :], mem_v[:, l, t, hh * HD:(hh + 1) * HD],
                               m["pt"][:, t, hh, :], t == 0, t == 1)
                    if hh % 2:
                        q.then_inc(sem("ma_o"), 1)

            memory_attention(0)

            def chain(j, c, hop):
                if hop == 0:
                    if c == 0:
                        pe.wait_ge(sem("dx_add"), ADDS * (j + 1))
                        pe.wait_ge(sem("v_tok"), j + 1)
                    else:
                        pe.wait_ge(sem("s_up"), 3 * j + c)
                    for hh in range(2):
                        o = bank[4][:, hh * P:(hh + 1) * P]
                        if c:
                            mm(o, AR[:, c, 2 * hh, :], S, True, False)
                        q = mm(o, KG[:, c, 2 * hh, :], diag(Vp, 2 * P * c), c == 0, True)
                    q.then_inc(sem("u_mm"), 1)
                elif hop == 1:
                    pe.wait_ge(sem("u_sb"), NCH * j + c + 1)
                    for hh in range(2):
                        q = mm(bank[4][:, hh * P:(hh + 1) * P], XT[:, hh, c, :], Usb)
                    q.then_inc(sem("sa_mm"), 1)
                else:
                    pe.wait_ge(sem("sa_sb"), NCH * j + c + 1)
                    o = bank[7][:, c * P:(c + 1) * P]
                    if c < NCH - 1:
                        q = mm(bank[5][:, 0:P], Btok[:, c, :], diag(SAp), True, False)
                        q = mm(bank[5][:, 0:P], Ktok[:, c, :], diag(Vp, 2 * P * c), False, True)
                    if c:
                        mm(o, S, AR[:, c, 1, :], True, False)
                        q = mm(o, S, AR[:, c, 3, :], False, False)
                    if c < NCH - 1:
                        q.then_inc(sem("st_mm"), 1)
                    for hh in range(2):
                        mm(o, SAp[:, hh * P:(hh + 1) * P], BG[:, c, 2 * hh + 1, :], c == 0 and hh == 0, False)
                        q = mm(o, Vp[:, 2 * P * c + hh * P:2 * P * c + (hh + 1) * P], KG[:, c, 2 * hh + 1, :],
                               False, hh == 1)
                    q.then_inc(sem("y_mm"), 1)

            def to_tokens(src, sig):
                for c in range(NCH):
                    q = nc.tensor.transpose(bank[5][:, c * P:(c + 1) * P], src[:, c * P:(c + 1) * P], ident)
                q.then_inc(sem(sig), 1)

            def mean_of(j):
                pe.wait_ge(sem("y_sb"), j + 1)
                mm(bank[6][:, :], blk, ysb).then_inc(sem("mean_mm"), 1)

            def variance_of(j):
                pe.wait_ge(sem("y_sq"), j + 1)
                mm(bank[7][:, :], blk, sc1).then_inc(sem("var_mm"), 1)

            def pair(j, first):
                pe.wait_ge(sem("ws_in"), 16 * (j + 1))
                if not first:
                    pe.wait_ge(sem("g_sb"), j)
                mm(bank[0][:, :], ws[:, 0, :], lora_w).then_inc(sem("w_mm"), 1)
                if not first:
                    pe.wait_ge(sem("bonus"), j)
                mm(bank[1][:, :], ws[:, 0, :], lora_a).then_inc(sem("a_mm"), 1)
                for g in range(12):
                    if not first:
                        chain(j - 1, g // 3, g % 3)
                    if g == 8:
                        pe.wait_ge(sem("kk_sq"), j + 1)
                        mm(bank[0][:, :], blk, sc1).then_inc(sem("kkss_mm"), 1)
                    t, b = g // 4, (0, 1, 1)[g // 4]
                    if g % 4 == 0:
                        pe.wait_ge(sem(f"wp_in{t}"), 16 * (j + 1))
                        pe.wait_ge(sem(("w_sig", "a_sig", "r_x")[t]), j + 1)
                    for k in (2 * (g % 4), 2 * (g % 4) + 1):
                        q = mm(bank[b][:, :], ring[:, t, k * P:(k + 1) * P], h[:, k, :], k == 0, k == KD - 1)
                    if g % 4 == 3:
                        q.then_inc(sem(("k_mm", "r_mm", "v_mm")[t]), 1)
                pe.wait_ge(sem("v_x"), j + 1)
                to_tokens(vx, "vt_mm")
                if not first:
                    mean_of(j - 1)
                pe.wait_ge(sem("kf"), j + 1)
                pe.wait_ge(sem("v_tok"), j + 1)
                to_tokens(flat(Kf), "kt_mm")
                pe.wait_ge(sem("bf"), j + 1)
                pe.wait_ge(sem("k_tok"), j + 1)
                to_tokens(flat(Bf), "bt_mm")
                if not first:
                    variance_of(j - 1)
                pe.wait_ge(sem("ar"), j + 1)
                for c in range(NCH):
                    if c:
                        pe.wait_ge(sem("kg_ev"), NCH * j + c)
                    mm(bank[2][:, :], Kf[:, c, :], flat(AR[:, c, :, :])).then_inc(sem("kg_mm"), 1)
                    if c:
                        pe.wait_ge(sem("bg_ev"), NCH * j + c)
                    mm(bank[3][:, :], Bf[:, c, :], flat(AR[:, c, :, :])).then_inc(sem("bg_mm"), 1)
                    if c:
                        pe.wait_ge(sem("x_l1"), NCH * j + c)
                    for hh in range(2):
                        q = mm(bank[4][:, hh * P:(hh + 1) * P], AR[:, c, 2 * hh, :], Bf[:, c, :])
                    q.then_inc(sem("m_mm"), 1)
                pe.wait_ge(sem("rk"), j + 1)
                mm(bank[1][:, :], blk, rrk).then_inc(sem("bonus_mm"), 1)
                pe.wait_ge(sem("kk_sd"), j + 1)
                mm(bank[0][:, :], ws[:, 1, :], sig_g).then_inc(sem("g_mm"), 1)
                pe.wait_ge(sem("kg_ev"), NCH * j + NCH)
                pe.wait_ge(sem("b_tok"), j + 1)
                if not first:
                    pe.wait_ge(sem("y_sd"), j)
                for v in range(LEVELS):
                    for hh in range(2):
                        pe.wait_ge(sem("ct"), 2 * LEVELS * j + (2 * v + hh + 1))
                        if v == 0:
                            pe.wait_ge(sem("x_one"), 4 * j + (2 * hh + 2))
                        else:
                            pe.wait_ge(sem("dx_add"), ADDS * j + (4 * (v - 1) + 2 * hh + 2))
                        for c in range(NCH):
                            q = mm(bank[2 + hh][:, c * P:(c + 1) * P], CT[:, hh, c, :], X[:, hh, c, :])
                        q.then_inc(sem("y1_mm"), 1)
                    for hh in range(2):
                        pe.wait_ge(sem("y1_sb"), 2 * LEVELS * j + (2 * v + hh + 1))
                        if v < LEVELS - 1:
                            for c in range(NCH):
                                mm(bank[4 + 2 * hh][:, c * P:(c + 1) * P], XT[:, hh, c, :], Y1[:, hh, c, :])
                        for c in range(NCH):
                            q = mm(bank[5 + 2 * hh][:, c * P:(c + 1) * P], Y1[:, hh, c, :], XT[:, hh, c, :])
                        q.then_inc(sem("dx_mm"), 1)

            pe.wait_ge(sem("lora_in"), 3)
            pe.wait_ge(sem("ma_y"), 2)
            rounds(pe, PAIRS, pair)
            for g in range(12):
                chain(PAIRS - 1, g // 3, g % 3)
            mean_of(PAIRS - 1)
            variance_of(PAIRS - 1)

            def out_product(e, n0, tiles, kn, per_slot):
                for m in range(KD):
                    n, b = n0 + m // per_slot, m % per_slot
                    pe.wait_ge(landed[n % SLOTS], 16 * (n // SLOTS + 1))
                    if m >= 2 or e:
                        pe.wait_ge(sem("x_up"), KD * e + m - 1)
                    q = ring_product(bank[m % 2][:, :], n % SLOTS, lambda k: y[:, k, :], kn, base=b * kn * P)
                    q.then_inc(used if b == per_slot - 1 else sem("out_half"), 1)
                    if m:
                        square_sum(e, m - 1, m == 1)

            def square_sum(e, m, first=False, last=False):
                pe.wait_ge(sem("xsq"), KD * (e + 1) + m + 1)
                return mm(bank[7][:, :], ones, h[:, bass.ds(m, 1), :].rearrange("p a t -> p (a t)"), first, last)

            pe.wait_ge(sem("y_out"), PAIRS)
            out_product(0, N_OUTA, KD, KD, 1)
            square_sum(0, KD - 1, last=True).then_inc(sem("x_ss"), 1)

            def mlp(l, n0, n1, h_at):
                def up(i, first):
                    for b in range(2):
                        if not (first and l == 0):
                            pe.wait_ge(sem("conv_done"), 2 * i + (FT * l + b - 1))
                        for s in range(2):
                            pe.wait_ge(landed[2 * b + s], 16 * (i + (n0 // SLOTS + 1)))
                            ring_product(bank[2 * b + s][:, :], 2 * b + s, lambda k: h[:, k, :], KD,
                                         ready=("h_ready", h_at + 1) if first else None).then_inc(used, 1)

                rounds(pe, FT // 2, up)

                def down(i, first):
                    for b in range(2):
                        if not (first and b == 0):
                            pe.wait_ge(sem("x_up"), 2 * i + (KD * (2 * l + 1) + b - 1))
                        for s in range(2):
                            pe.wait_ge(landed[2 * b + s], 16 * (i + (n1 // SLOTS + 1)))
                            for k in range(FT // 2):
                                kz = s * (FT // 2) + k
                                if first and b == 0:
                                    pe.wait_ge(sem("z"), FT * l + kz + 1)
                                q = mm(bank[4 + b][:, :], ring[:, 2 * b + s, k * P:(k + 1) * P], z[:, kz, :],
                                       kz == 0, kz == FT - 1)
                            q.then_inc(used, 1)
                        if l == 0 and not (first and b == 0):
                            square_sum(1, 2 * i + (b - 1), first)

                rounds(pe, KD // 2, down)
                if l == 0:
                    square_sum(1, KD - 1, last=True).then_inc(sem("x_ss"), 1)

            mlp(0, N_UP0, N_DOWN0, KD)

            pe.wait_ge(sem("kp_zero"), 1)
            for u in range(U_K, U_END + 2):
                if u < U_END:
                    n = N_K + u - U_K
                    head_tile(u, n, h if u < U_Q else h2,
                              2 * KD if u == U_K else 3 * KD if u == U_Q else None)
                if U_K < u <= U_END:
                    head_sum(u - 1)
                if U_K + 2 <= u < U_QM1 + 2:
                    rope_turn(u - 2)
            for i in range(6):
                n = N_V + i
                pe.wait_ge(landed[n % SLOTS], 16 * (n // SLOTS + 1))
                if i >= 2:
                    pe.wait_ge(sem("v_ev"), i - 1)
                for r in range(RES):
                    for k in range(KD):
                        q = mm(bank[6 + i % 2][:, r * P:(r + 1) * P], by_residue(h[:, k, :])[:, r, :],
                               ring[:, n % SLOTS, k * P:(k + 1) * P], k == 0, k == KD - 1)
                q.then_inc(used, 1)

            pe.wait_ge(sem("rope_done"), 12)
            pe.wait_ge(sem("v_ev"), 6)

            def residue(r, first):
                pe.wait_ge(sem("da_stage"), r + 1)
                rs = bass.ds(r * P, P)

                def scores(s):
                    if not (first and s < 2):
                        pe.wait_ge(sem("da_sm"), 4 * r + (s - 1))
                    b = 2 * (s % 2)
                    mm(bank[b][:, :], qS[:, s // 2, :], kp[:, s, :])
                    mm(bank[b + 1][:, 0:P], qS[:, 2 + s // 2, :], kp[:, SLOTS + s, rs])
                    mm(bank[b + 1][:, P:2 * P], qS[:, 4 + s // 2, :], kp[:, 2 * SLOTS + s, rs])\
                        .then_inc(sem("da_sc"), 1)

                scores(0)
                for s in range(4):
                    if s < 3:
                        scores(s + 1)
                    pe.wait_ge(sem("da_pn"), 4 * r + s + 1)
                    if not (first and s == 0):
                        pe.wait_ge(sem("da_pt"), 4 * r + s)
                    for q in range(6):
                        i = nc.tensor.transpose(bank[4 + q // 4][:, (q % 4) * P:(q % 4 + 1) * P],
                                                pr[:, s % 2, q * P:(q + 1) * P], ident)
                    i.then_inc(sem("da_tr"), 1)
                    pe.wait_ge(sem("da_pt"), 4 * r + s + 1)
                    o = bank[6 + s // 2][HD * (s % 2):HD * (s % 2) + HD, 0:P]
                    if not first:
                        pe.wait_ge(sem("da_y"), 4 * r + (s - 3))
                    for q in range(6):
                        v = vtok[:, q, s * HD:(s + 1) * HD] if q < RES else vS[:, ((q - RES) * 4 + s) * HD:((q - RES) * 4 + s + 1) * HD]
                        i = mm(o, v, pT[:, s % 2, q * P:(q + 1) * P], q == 0, q == 5)
                    i.then_inc(sem("da_o"), 1)

            rounds(pe, RES, residue)
            pe.wait_ge(sem("da_y"), 4 * RES)
            memory_attention(1)
            pe.wait_ge(sem("ma_y"), 4)
            out_product(2, N_OUTB, KD, 4, 2)
            square_sum(2, KD - 1, last=True).then_inc(sem("x_ss"), 1)
            mlp(1, N_UP1, N_DOWN1, 4 * KD)

        @block.scalar
        def _(act):
            def root(out, in_, count, eps):
                return nc.scalar.activation(out, in_, ACT.Sqrt, bias=eps, scale=1.0 / count)

            def copy(out, in_):
                return nc.scalar.activation(out, in_, ACT.Copy)

            act.wait_ge(sem("mem_in"), 16)
            for k in range(KD):
                nc.scalar.activation(memh[:, k, :], memx[:, k, :], ACT.Square).then_inc(sem("msq"), 1)
            act.wait_ge(sem("x_in"), 16)
            for k in range(KD):
                nc.scalar.activation(h[:, k, :], x[:, k, :], ACT.Square).then_inc(sem("xsq"), 1)
            act.wait_ge(sem("eps"), 2)
            act.wait_ge(sem("mem_ss"), 1)
            root(mem_rs, bank[6][:, 0:NMEM], D, rms_eps).then_inc(sem("mem_sd"), 1)

            def stream_root(e):
                act.wait_ge(sem("x_ss"), e + 1)
                root(rstd[:, :], bank[7][:, :], D, rms_eps).then_inc(sem("x_sd"), 1)

            stream_root(0)

            def head_out(u):
                raw, sq, _, n = heads_of(u)
                if u < U_QM0:
                    act.wait_ge(sem("mk_mm"), u + 1)
                else:
                    act.wait_ge(used, (N_QM0 + u - U_QM0 if u < U_K else N_K + u - U_K) + 1)
                if u >= 2:
                    act.wait_ge(sem("hn_done"), u - 1)
                    act.wait_ge(sem("hn_ss"), u - 1)
                copy(raw, bank[u % 2][:, 0:n]).then_inc(sem("hn_raw"), 1)
                nc.scalar.activation(sq, bank[u % 2][:, 0:n], ACT.Square).then_inc(sem("hn_sqd"), 1)

            def head_root(u):
                _, _, rs, n = heads_of(u)
                act.wait_ge(sem("hn_ss"), u + 1)
                if u >= 2:
                    act.wait_ge(sem("hn_done"), u - 1)
                if u >= U_K + 2:
                    act.wait_ge(sem("rope_done"), u - U_K - 1)
                root(rs, bank[2 + u % 2][:, 0:n], HD, rms_eps).then_inc(sem("hn_sd"), 1)

            for l in range(2):
                for i in range(2):
                    head_out(2 * l + i)
                for i in range(2):
                    act.wait_ge(sem("mv_mm"), 2 * l + i + 1)
                    copy(mem_v[:, l, i, :], bank[4 + i][:, 0:NMEM]).then_inc(sem("mv_out"), 1)
                for i in range(2):
                    head_root(2 * l + i)

            act.wait_ge(sem("derived"), 2)
            for i, dst in enumerate((kx, rx)):
                act.wait_ge(used, N_LORA + i + 1)
                nc.scalar.activation(dst, bank[4 + i][:, :], ACT.Identity,
                                     scale=derived[:, PAIRS * NPAR + i:PAIRS * NPAR + i + 1]).then_inc(sem("lora_own"), 1)
            for i in range(2):
                head_out(U_QM0 + i)
            for i in range(2):
                head_root(U_QM0 + i)
            act.wait_ge(sem("lora_x"), 2)
            act.wait_ge(sem("zeroed"), 2)
            nc.scalar.activation(lora_w[0:HD], kx[0:HD], ACT.Tanh).then_inc(sem("lora_in"), 1)
            copy(lora_a[HD:P], kx[HD:P]).then_inc(sem("lora_in"), 1)
            nc.scalar.activation(sig_g, rx, ACT.Sigmoid).then_inc(sem("lora_in"), 1)

            def memory_attention(l):
                m = mem_attn[l]

                def token_tile(c, first):
                    g = 4 * l + c
                    if not first:
                        act.wait_ge(sem("ma_tr"), 2 * g)
                    for i in range(2):
                        act.wait_ge(sem("ma_nb"), 2 * g + i + 1)
                        for hh in range(2):
                            k = 2 * i + hh
                            nc.scalar.activation(m["p"][:, k, :], bank[i][:, hh * NMEM:(hh + 1) * NMEM], ACT.Exp,
                                                 bias=stat[:, 4 + k:5 + k], scale=HD ** -0.5,
                                                 accum_out=stat[:, 8 + k:9 + k]).then_inc(sem("ma_exp"), 1)
                    for t in range(2):
                        act.wait_ge(sem("ma_tr"), 2 * g + t + 1)
                        copy(m["pt"][:, t, :, bass.ds(c * P, P)], bank[2 + t][:, :].rearrange("p (h t) -> p h t", t=P))\
                            .then_inc(sem("ma_pt"), 1)

                rounds(act, RES, token_tile)
                for i in range(2):
                    act.wait_ge(sem("ma_o"), 2 * l + i + 1)
                    copy(y[:, m["y"] + i, :], bank[4 + i][:, :]).then_inc(sem("ma_y"), 1)

            memory_attention(0)

            def bchunks(a):
                return a.rearrange("p (c t) -> p c t", t=CHUNK)

            def hop_u(j, c):
                act.wait_ge(sem("u_mm"), NCH * j + c + 1)
                copy(Usb.rearrange("p (h w) -> p h w", w=HD), diag(bank[4])).then_inc(sem("u_sb"), 1)

            def hop_sa(j, c):
                act.wait_ge(sem("sa_mm"), NCH * j + c + 1)
                copy(diag(SAp), diag(bank[4])).then_inc(sem("sa_sb"), 1)

            def y_read(j):
                act.wait_ge(sem("y_mm"), NCH * (j + 1))
                copy(ysb, bank[7][:, :]).then_inc(sem("y_sb"), 1)

            def y_square(j):
                act.wait_ge(sem("yc"), j + 1)
                nc.scalar.activation(sc1, ysb, ACT.Square).then_inc(sem("y_sq"), 1)

            def y_root(j):
                act.wait_ge(sem("var_mm"), j + 1)
                root(sc2, bank[7][:, :], HD, lnx_eps).then_inc(sem("y_sd"), 1)

            def y_affine(j):
                act.wait_ge(sem("yn"), j + 1)
                nc.scalar.activation(ysb, ysb, ACT.Identity, scale=pcol(j, LNW), bias=pcol(j, LNB))\
                    .then_inc(sem("y_ln"), 1)

            def own_part(dst, b, j, k, sig):
                nc.scalar.activation(dst, bank[b][:, :], ACT.Identity, scale=dcol(j, k)).then_inc(sem(sig), 1)

            def pair(j, first):
                act.wait_ge(sem("w_mm"), j + 1)
                nc.scalar.activation(lw[:, :, 1:], bchunks(bank[0][:, :]), ACT.Sigmoid, bias=pcol(j, PW0))\
                    .then_inc(sem("w_sig"), 1)
                act.wait_ge(sem("a_mm"), j + 1)
                nc.scalar.activation(aa, bank[1][:, :], ACT.Sigmoid, bias=pcol(j, PA0)).then_inc(sem("a_sig"), 1)
                act.wait_ge(sem("a_sig"), j + 1)
                nc.scalar.activation(fa, aa, ACT.Identity, scale=pcol(j, KAP), bias=dcol(j, KAP)).then_inc(sem("fa"), 1)
                if not first:
                    hop_u(j - 1, 0)
                    hop_sa(j - 1, 0)
                act.wait_ge(sem("cc"), j + 1)
                nc.scalar.activation(e_pos, cc, ACT.Exp, scale=DECAY).then_inc(sem("e_pos"), 1)
                nc.scalar.activation(e_neg, cc, ACT.Exp, scale=-DECAY).then_inc(sem("e_neg"), 1)
                if not first:
                    hop_u(j - 1, 1)
                act.wait_ge(sem("k_mm"), j + 1)
                own_part(kx, 0, j, MUK, "k_own")
                if not first:
                    hop_sa(j - 1, 1)
                    hop_u(j - 1, 2)
                act.wait_ge(sem("k_x"), j + 1)
                nc.scalar.activation(kkr, kx, ACT.Identity, scale=pcol(j, KKP)).then_inc(sem("kkr"), 1)
                act.wait_ge(sem("kkr"), j + 1)
                nc.scalar.activation(sc1, kkr, ACT.Square).then_inc(sem("kk_sq"), 1)
                if not first:
                    hop_sa(j - 1, 2)
                act.wait_ge(sem("r_mm"), j + 1)
                own_part(rx, 1, j, MUR, "r_own")
                act.wait_ge(sem("kkss_mm"), j + 1)
                nc.scalar.activation(sc2, bank[0][:, :], ACT.Sqrt).then_inc(sem("kk_sd"), 1)
                if not first:
                    hop_u(j - 1, 3)
                    hop_sa(j - 1, 3)
                act.wait_ge(sem("v_mm"), j + 1)
                own_part(vx, 1, j, MUV, "v_own")
                if not first:
                    y_read(j - 1)
                act.wait_ge(sem("vt_mm"), j + 1)
                v_to_tokens()
                act.wait_ge(sem("kt_mm"), j + 1)
                copy(flat(Ktok), bank[5][:, :]).then_inc(sem("k_tok"), 1)
                if not first:
                    y_square(j - 1)
                act.wait_ge(sem("bt_mm"), j + 1)
                copy(flat(Btok), bank[5][:, :]).then_inc(sem("b_tok"), 1)
                if not first:
                    act.wait_ge(sem("kk_n"), j + 1)
                    y_root(j - 1)
                    y_affine(j - 1)
                    act.wait_ge(sem("y_out"), j)
                act.wait_ge(sem("g_mm"), j + 1)
                copy(gate, bank[0][:, :]).then_inc(sem("g_sb"), 1)
                for i in range(2 * LEVELS):
                    act.wait_ge(sem("y1_mm"), 2 * LEVELS * j + i + 1)
                    copy(flat(Y1[:, i % 2, :, :]), bank[2 + i % 2][:, :]).then_inc(sem("y1_sb"), 1)

            def v_to_tokens():
                for hh in range(2):
                    dst = Vp[:, 0:NCH * 2 * P].rearrange("p (c w) -> p c w", w=2 * P)[:, :, 3 * HD * hh:3 * HD * hh + HD]
                    src = bank[5][:, :].rearrange("p (c w) -> p c w", w=P)[:, :, HD * hh:HD * (hh + 1)]
                    q = copy(dst, src)
                q.then_inc(sem("v_tok"), 1)

            act.wait_ge(sem("rw_zero"), 1)
            rounds(act, PAIRS, pair)
            j = PAIRS - 1
            for c in range(NCH):
                hop_u(j, c)
                hop_sa(j, c)
            y_read(j)
            y_square(j)
            y_root(j)
            y_affine(j)

            def squares(e):
                for m in range(KD):
                    act.wait_ge(sem("x_up"), KD * e + m + 1)
                    nc.scalar.activation(h[:, m, :], x[:, m, :], ACT.Square).then_inc(sem("xsq"), 1)

            squares(0)
            stream_root(1)

            def mlp(l, n0):
                def up(i, first):
                    for b in range(2):
                        jj = 2 * i + (FT * l + b)
                        if not (first and l == 0):
                            act.wait_ge(sem("z"), jj - 1)
                        for s in range(2):
                            act.wait_ge(used, 4 * i + (n0 + 2 * b + s + 1))
                            nc.scalar.activation(conv[:, 2 * b + s, :], bank[2 * b + s][:, :], ACT.Identity,
                                                 scale=tap(l, 2 * (2 * i + b) + s, 2), bias=tap(l, 2 * (2 * i + b) + s, 3))\
                                .then_inc(sem("conv_own"), 1)
                        act.wait_ge(sem("conv_gate"), jj + 1)
                        nc.scalar.activation(silu[:, b, :], conv[:, 2 * b, :], ACT.Silu).then_inc(sem("silu"), 1)

                rounds(act, FT // 2, up)

            def tap(l, tile, k):
                return par[:, bass.ds(4 * tile + (G_CONV + l * 2 * FT * 4 + k), 1)]

            mlp(0, N_UP0)
            squares(1)
            stream_root(2)
            for u in range(U_K, U_END + 1):
                if u < U_END:
                    head_out(u)
                if u > U_K:
                    head_root(u - 1)
            for i in range(6):
                act.wait_ge(used, N_V + i + 1)
                copy(vtok[:, :, i * P:(i + 1) * P], bank[6 + i % 2][:, :].rearrange("p (r f) -> p r f", f=P))\
                    .then_inc(sem("v_ev"), 1)

            def residue(r, first):
                def exps(s):
                    g = 4 * r + s
                    act.wait_ge(sem("da_nb"), g + 1)
                    if not (first and s < 2):
                        act.wait_ge(sem("da_tr"), g - 1)
                    nc.scalar.activation(pr[:, s % 2, :], sm[:, s % 2, :], ACT.Exp, bias=stat[:, 18 + s % 2:19 + s % 2],
                                         scale=HD ** -0.5, accum_out=stat[:, 20 + s % 2:21 + s % 2]).then_inc(sem("da_exp"), 1)

                exps(0)
                for s in range(4):
                    g = 4 * r + s
                    if s < 3:
                        exps(s + 1)
                    act.wait_ge(sem("da_tr"), g + 1)
                    if not (first and s < 2):
                        act.wait_ge(sem("da_o"), g - 1)
                    copy(pT[:, s % 2, 0:T], bank[4][:, :])
                    copy(pT[:, s % 2, T:6 * P], bank[5][:, 0:2 * P]).then_inc(sem("da_pt"), 1)
                    act.wait_ge(sem("da_o"), g + 1)
                    hs = slice(HD * (s % 2), HD * (s % 2) + HD)
                    copy(by_residue(y[:, s // 2, :])[hs, bass.ds(r, 1), :],
                         bank[6 + s // 2][hs, 0:P].unsqueeze(1)).then_inc(sem("da_y"), 1)

            rounds(act, RES, residue)
            memory_attention(1)
            squares(2)
            stream_root(3)
            mlp(1, N_UP1)

        @block.vector
        def _(dve):
            V = nc.vector
            V.memset(epsb[:, 0:1], RMS_EPS).then_inc(sem("eps"), 1)
            V.memset(epsb[:, 1:2], LNX_EPS).then_inc(sem("eps"), 1)
            dve.wait_ge(sem("par_in"), 16)
            V.tensor_scalar(derived[:, 0:PAIRS * NPAR], par[:, G_PAIR:G_END], -1.0, 1.0, ALU.mult, ALU.add)\
                .then_inc(sem("derived"), 1)
            V.tensor_scalar(derived[:, PAIRS * NPAR:PAIRS * NPAR + 2], par[:, MU_WA:MU_WA + 2], -1.0, 1.0, ALU.mult, ALU.add)\
                .then_inc(sem("derived"), 1)

            dve.wait_ge(sem("mem_sd"), 1)
            V.reciprocal(mem_rs, mem_rs).then_inc(sem("mem_rc"), 1)
            dve.wait_ge(sem("mem_rc"), 1)
            dve.wait_ge(sem("zeroed"), 2)

            def scaled(dst, src, gain, by, sig):
                return V.scalar_tensor_tensor(out=dst, in0=src, scalar=gain, in1=by, op0=ALU.mult, op1=ALU.mult)\
                    .then_inc(sem(sig), 1)

            def stream_rstd(e):
                dve.wait_ge(sem("x_sd"), e + 1)
                V.reciprocal(rstd[:, :], rstd[:, :]).then_inc(sem("x_rc"), 1)
                dve.wait_ge(sem("x_rc"), e + 1)

            def stream_norm(dst, gain):
                for k in range(KD):
                    scaled(dst[:, k, :], x[:, k, :], col(gain + k), rstd[:, :], "h_ready")

            def head_norm(u, gain):
                raw, _, rs, n = heads_of(u)
                dve.wait_ge(sem("hn_sd"), u + 1)
                V.reciprocal(rs, rs).then_inc(sem("hn_rc"), 1)
                dve.wait_ge(sem("hn_rc"), u + 1)
                if u < U_QM0:
                    l, i = u // 2, u % 2
                    for hh in range(2):
                        hs = slice(HD * hh, HD * hh + HD)
                        q = V.scalar_tensor_tensor(out=mem_k[hs, l, i, hh, :], in0=raw[hs], scalar=par[hs, gain:gain + 1],
                                                   in1=rs[hs], op0=ALU.mult, op1=ALU.mult)
                    q.then_inc(sem("hn_done"), 1)
                    return
                dst = qm_a[:, u % 2, :] if u < U_K else hz[:, u % 2, :] if u < U_QM1 else qm_b[:, u % 2, :]
                scaled(dst, raw, col(gain), rs, "hn_done")

            for k in range(KD):
                scaled(memh[:, k, :], memx[:, k, :], col(G_MEM0 + k), mem_rs, "memh")
            stream_rstd(0)
            stream_norm(h, G_ATTN0)
            for i in range(2):
                head_norm(i, G_MK0)
            dve.wait_ge(sem("mv_mm"), 2)
            for k in range(KD):
                scaled(memh[:, k, :], memx[:, k, :], col(G_MEM1 + k), mem_rs, "memh")
            for i in range(2):
                head_norm(2 + i, G_MK1)

            def shifted(dst, src, mu, sig):
                V.scalar_tensor_tensor(out=dst[:, 1:T], in0=src[:, 0:T - 1], scalar=mu, in1=dst[:, 1:T],
                                       op0=ALU.mult, op1=ALU.add).then_inc(sem(sig), 1)

            for i, dst in enumerate((kx, rx)):
                dve.wait_ge(sem("lora_own"), i + 1)
                shifted(dst, bank[4 + i], col(MU_WA + i), "lora_x")
            for i in range(2):
                head_norm(U_QM0 + i, G_MQ0)

            def memory_attention(l):
                m = mem_attn[l]

                def token_tile(c, first):
                    g = 4 * l + c
                    for i in range(2):
                        dve.wait_ge(sem("ma_sc"), 2 * g + i + 1)
                        V.tensor_reduce(stat[:, 2 * i:2 * i + 2], bank[i][:, :].rearrange("p (h t) -> p h t", t=NMEM),
                                        AX.X, ALU.max).then_inc(sem("ma_mx"), 1)
                        dve.wait_ge(sem("ma_mx"), 2 * g + i + 1)
                        V.tensor_scalar(stat[:, 4 + 2 * i:6 + 2 * i], stat[:, 2 * i:2 * i + 2], -HD ** -0.5, None, ALU.mult)\
                            .then_inc(sem("ma_nb"), 1)
                    dve.wait_ge(sem("ma_exp"), 4 * g + 4)
                    V.reciprocal(stat[:, 12:16], stat[:, 8:12]).then_inc(sem("ma_rd"), 1)
                    dve.wait_ge(sem("ma_rd"), g + 1)
                    V.tensor_tensor(m["p"], m["p"], stat[:, 12:16].unsqueeze(2).to_broadcast([P, MEMH, NMEM]), ALU.mult)\
                        .then_inc(sem("ma_pn"), 1)

                rounds(dve, RES, token_tile)

            memory_attention(0)

            def halves():
                return (slice(0, HD), 0), (slice(HD, P), 1)

            def state(j, c):
                if c:
                    dve.wait_ge(sem("s_up"), 3 * j + c)
                    V.tensor_scalar(Sf, S, fS[:, c:c + 1], None, ALU.mult).then_inc(sem("sf"), 1)
                dve.wait_ge(sem("st_mm"), 3 * j + c + 1)
                dve.wait_ge(sem("fs"), j + 1)
                if c:
                    dve.wait_ge(sem("sf"), 2 * j + c)
                for hs, hh in halves():
                    cs = slice(HD * hh, HD * hh + HD)
                    if c == 0:
                        q = V.tensor_scalar(S[hs, cs], bank[5][hs, cs], fS[hs, 0:1], None, ALU.mult)
                    else:
                        q = V.scalar_tensor_tensor(out=S[hs, cs], in0=bank[5][hs, cs], scalar=fS[hs, c:c + 1],
                                                   in1=Sf[hs, cs], op0=ALU.mult, op1=ALU.add)
                q.then_inc(sem("s_up"), 1)

            def centre(j):
                dve.wait_ge(sem("mean_mm"), j + 1)
                V.scalar_tensor_tensor(out=ysb, in0=bank[6][:, :], scalar=-1.0 / HD, in1=ysb, op0=ALU.mult, op1=ALU.add)\
                    .then_inc(sem("yc"), 1)

            def finish(j):
                dve.wait_ge(sem("y_sd"), j + 1)
                V.reciprocal(sc2, sc2).then_inc(sem("y_rc"), 1)
                dve.wait_ge(sem("y_rc"), j + 1)
                V.tensor_tensor(ysb, ysb, sc2, ALU.mult).then_inc(sem("yn"), 1)
                dve.wait_ge(sem("y_ln"), j + 1)
                V.tensor_tensor(ysb, ysb, bonus, ALU.add).then_inc(sem("y_b"), 1)
                dve.wait_ge(sem("y_b"), j + 1)
                V.tensor_tensor(y[:, bass.ds(j, 1), :], ysb.unsqueeze(1), gate.unsqueeze(1), ALU.mult)\
                    .then_inc(sem("y_out"), 1)

            def pair(j, first):
                dve.wait_ge(sem("w_sig"), j + 1)
                V.tensor_tensor_scan(flat(lw), reset, flat(lw), 0.0, ALU.mult, ALU.add).then_inc(sem("cum"), 1)
                dve.wait_ge(sem("cum"), j + 1)
                V.tensor_tensor(cc, lw, lw[:, :, CHUNK // 2:CHUNK // 2 + 1].to_broadcast([P, NCH, PAD]), ALU.subtract)\
                    .then_inc(sem("cc"), 1)
                if not first:
                    state(j - 1, 0)
                dve.wait_ge(sem("k_own"), j + 1)
                shifted(kx, bank[0], pcol(j, MUK), "k_x")
                if not first:
                    state(j - 1, 1)
                dve.wait_ge(sem("fa"), j + 1)
                dve.wait_ge(sem("kkr"), j + 1)
                dve.wait_ge(sem("k_x"), j + 1)
                V.tensor_tensor(kx, kx, fa, ALU.mult).then_inc(sem("k2"), 1)
                dve.wait_ge(sem("r_own"), j + 1)
                shifted(rx, bank[1], pcol(j, MUR), "r_x")
                if not first:
                    state(j - 1, 2)
                dve.wait_ge(sem("r_x"), j + 1)
                dve.wait_ge(sem("k2"), j + 1)
                V.scalar_tensor_tensor(out=rrk, in0=rx, scalar=pcol(j, RKP), in1=kx, op0=ALU.mult, op1=ALU.mult)\
                    .then_inc(sem("rk"), 1)
                dve.wait_ge(sem("e_neg"), j + 1)
                V.tensor_tensor(Kf, kx.rearrange("p (c t) -> p c t", t=P), e_neg[:, :, 1:], ALU.mult).then_inc(sem("kf"), 1)
                dve.wait_ge(sem("kk_sd"), j + 1)
                V.tensor_scalar(sc2, sc2, 1e-12, None, ALU.max).then_inc(sem("kk_mx"), 1)
                dve.wait_ge(sem("kk_mx"), j + 1)
                V.reciprocal(sc2, sc2).then_inc(sem("kk_rc"), 1)
                dve.wait_ge(sem("kk_rc"), j + 1)
                V.tensor_tensor(kk, kkr, sc2, ALU.mult).then_inc(sem("kk_n"), 1)
                dve.wait_ge(sem("v_own"), j + 1)
                shifted(vx, bank[1], pcol(j, MUV), "v_x")
                dve.wait_ge(sem("bb"), j + 1)
                V.tensor_tensor(Bf, bb.rearrange("p (c t) -> p c t", t=P), e_neg[:, :, 1:], ALU.mult).then_inc(sem("bf"), 1)
                if not first:
                    dve.wait_ge(sem("y_mm"), NCH * j)
                    centre(j - 1)
                dve.wait_ge(sem("r_x"), j + 1)
                for hs, hh in halves():
                    V.scalar_tensor_tensor(out=AR[hs, :, 2 * hh, :], in0=kk[hs].rearrange("p (c t) -> p c t", t=P),
                                           scalar=-1.0, in1=e_pos[hs, :, 0:CHUNK], op0=ALU.mult, op1=ALU.mult)
                    q = V.tensor_tensor(AR[hs, :, 2 * hh + 1, :], rx[hs].rearrange("p (c t) -> p c t", t=P),
                                        e_pos[hs, :, 1:], ALU.mult)
                q.then_inc(sem("ar"), 1)
                tri2 = tri.unsqueeze(1).to_broadcast([P, 2, 2 * P])
                for c in range(NCH):
                    for G, b, n in ((KG, 2, "kg"), (BG, 3, "bg")):
                        dve.wait_ge(sem(n + "_mm"), NCH * j + c + 1)
                        V.tensor_tensor(flat(G[:, c, :, :]).rearrange("p (h w) -> p h w", w=2 * P),
                                        bank[b][:, :].rearrange("p (h w) -> p h w", w=2 * P), tri2, ALU.mult)\
                            .then_inc(sem(n + "_ev"), 1)
                    dve.wait_ge(sem("m_mm"), NCH * j + c + 1)
                    V.tensor_tensor(X[:, :, c, :], bank[4][:, 0:2 * P].rearrange("p (h t) -> p h t", t=P),
                                    level(LEVELS + 1).unsqueeze(1).to_broadcast([P, 2, P]), ALU.mult).then_inc(sem("x_l1"), 1)
                if not first:
                    finish(j - 1)
                dve.wait_ge(sem("bonus_mm"), j + 1)
                V.tensor_tensor(bonus, bank[1][:, :], vx, ALU.mult).then_inc(sem("bonus"), 1)
                for v in range(LEVELS):
                    for hh in range(2):
                        dve.wait_ge(sem("dx_mm"), 2 * LEVELS * j + (2 * v + hh + 1))
                        dve.wait_ge(sem("x_one"), 4 * j + 2 * hh + 2)
                        if v:
                            dve.wait_ge(sem("dx_add"), ADDS * j + (4 * (v - 1) + 2 * hh + 2))
                        if v < LEVELS - 1:
                            xf = flat(X[:, hh, :, :])
                            V.tensor_tensor(xf, bank[4 + 2 * hh][:, :], xf, ALU.add).then_inc(sem("dx_add"), 1)
                        xf = flat(XT[:, hh, :, :])
                        V.tensor_tensor(xf, bank[5 + 2 * hh][:, :], xf, ALU.add).then_inc(sem("dx_add"), 1)

            dve.wait_ge(sem("rw_zero"), 1)
            rounds(dve, PAIRS, pair)
            for c in range(NCH - 1):
                state(PAIRS - 1, c)
            centre(PAIRS - 1)
            finish(PAIRS - 1)

            def residual(n0, b0, slots):
                for m in range(KD):
                    if slots < 1 and m % 2 == 0:
                        dve.wait_ge(sem("out_half"), m // 2 + 1)
                    else:
                        dve.wait_ge(used, n0 + int(slots * (m + 1)))
                    V.tensor_tensor(x[:, m, :], bank[b0 + m % 2][:, :], x[:, m, :], ALU.add).then_inc(sem("x_up"), 1)

            residual(N_OUTA, 0, 1)
            stream_rstd(1)
            stream_norm(h, G_FFN0)

            def tap(l, tile, k):
                return par[:, bass.ds(4 * tile + (G_CONV + l * 2 * FT * 4 + k), 1)]

            def mlp(l):
                def up(i, first):
                    for b in range(2):
                        jj = 2 * i + (FT * l + b)
                        for lag in (1, 2):
                            for s in range(2):
                                c = conv[:, 2 * b + s, :]
                                if lag == 1:
                                    dve.wait_ge(sem("conv_own"), 2 * jj + s + 1)
                                else:
                                    dve.wait_ge(sem("conv_one"), 2 * jj + s + 1)
                                q = V.scalar_tensor_tensor(out=c[:, lag:T], in0=bank[2 * b + s][:, 0:T - lag],
                                                           scalar=tap(l, 2 * (2 * i + b) + s, 2 - lag), in1=c[:, lag:T],
                                                           op0=ALU.mult, op1=ALU.add)
                                q.then_inc(sem("conv_one" if lag == 1 else ("conv_gate", "conv_done")[s]), 1)

                rounds(dve, FT // 2, up)

            mlp(0)
            residual(N_DOWN0, 4, 2)
            stream_rstd(2)
            stream_norm(h, G_KV)
            stream_norm(h2, G_ATTN1)

            def turn(u):
                v = u - U_K
                dve.wait_ge(sem("rope_mm"), v + 1)
                dve.wait_ge(sem("rope_in"), 32)
                rz = hn_b[2][:, u % 2, :]
                V.tensor_tensor(rz, bank[4 + u % 2][:, :], sinT, ALU.mult).then_inc(sem("rope_sin"), 1)
                dve.wait_ge(sem("rope_sin"), v + 1)
                dve.wait_ge(sem("rope_cos"), v + 1)
                if u < U_Q:
                    for hs, hh in halves():
                        q = V.tensor_tensor(kp[hs, 2 * v + hh, :].rearrange("p (r u) -> p r u", r=RES),
                                            by_residue(t1[hs, u % 2, :]), by_residue(rz[hs]), ALU.add)
                else:
                    q = V.tensor_tensor(qT[:, v - 6, :].rearrange("p (r u) -> p r u", r=RES),
                                        by_residue(t1[:, u % 2, :]), by_residue(rz), ALU.add)
                q.then_inc(sem("rope_done"), 1)

            dve.wait_ge(sem("kp_zero"), 1)
            for u in range(U_K, U_END + 2):
                if U_K + 2 <= u < U_QM1 + 2:
                    turn(u - 2)
                if U_K < u <= U_END:
                    head_norm(u - 1, G_KN if u - 1 < U_Q else G_QN if u - 1 < U_QM1 else G_MQ1)

            def residue(r, first):
                for s in range(4):
                    g, b = 4 * r + s, s % 2
                    dve.wait_ge(sem("da_sc"), g + 1)
                    if not (first and s < 2):
                        dve.wait_ge(sem("da_exp"), g - 1)
                    V.tensor_tensor(sm[:, b, 0:T].unsqueeze(1), bank[2 * b][:, :].unsqueeze(1), mask0[:, bass.ds(r, 1), :], ALU.add)
                    V.tensor_tensor(sm[:, b, T:6 * P], bank[2 * b + 1][:, 0:2 * P], mask12, ALU.add).then_inc(sem("da_sm"), 1)
                    dve.wait_ge(sem("da_sm"), g + 1)
                    V.tensor_reduce(stat[:, 16 + b:17 + b], sm[:, b, :], AX.X, ALU.max).then_inc(sem("da_mx"), 1)
                    dve.wait_ge(sem("da_mx"), g + 1)
                    V.tensor_scalar(stat[:, 18 + b:19 + b], stat[:, 16 + b:17 + b], -HD ** -0.5, None, ALU.mult)\
                        .then_inc(sem("da_nb"), 1)
                    dve.wait_ge(sem("da_exp"), g + 1)
                    V.reciprocal(stat[:, 22 + b:23 + b], stat[:, 20 + b:21 + b]).then_inc(sem("da_rd"), 1)
                    dve.wait_ge(sem("da_rd"), g + 1)
                    V.tensor_scalar(pr[:, b, :], pr[:, b, :], stat[:, 22 + b:23 + b], None, ALU.mult).then_inc(sem("da_pn"), 1)

            dve.wait_ge(sem("mask_in"), 32)
            rounds(dve, RES, residue)
            memory_attention(1)
            residual(N_OUTB, 0, 0.5)
            stream_rstd(3)
            stream_norm(h, G_FFN1)
            mlp(1)
            residual(N_DOWN1, 4, 2)

        @block.gpsimd
        def _(pool):
            G = nc.gpsimd

            G.memset(mem_k[:, :, :, :, :], 0.0).then_inc(sem("zeroed"), 1)
            G.memset(arena[:, 0:2 * T], 0.0).then_inc(sem("zeroed"), 1)

            def memory_attention(l):
                m = mem_attn[l]

                def token_tile(c, first):
                    g = 4 * l + c
                    if not first:
                        pool.wait_ge(sem("ma_sc"), 2 * g)
                    G.tensor_copy(m["qs"], m["q"][:, :, bass.ds(c * P, P)]).then_inc(sem("ma_qs"), 1)

                pool.wait_ge(sem("hn_done"), (U_K, U_END)[l])
                rounds(pool, RES, token_tile)

            memory_attention(0)
            pool.wait_ge(sem("ma_y"), 2)
            G.memset(flat(lw)[:, 0:NCH * PAD:PAD], 0.0)
            G.memset(AR, 0.0)
            G.memset(Vp, 0.0)
            G.memset(SAp, 0.0)
            G.memset(S, 0.0).then_inc(sem("rw_zero"), 1)

            def pair(j, first):
                pool.wait_ge(sem("kk_n"), j + 1)
                G.tensor_tensor(bb, kk, aa, ALU.mult).then_inc(sem("bb"), 1)
                pool.wait_ge(sem("e_neg"), j + 1)
                if not first:
                    pool.wait_ge(sem("s_up"), 3 * j)
                G.tensor_tensor(fS[:, 0:NCH - 1].unsqueeze(2), e_pos[:, 0:NCH - 1, CHUNK:PAD], e_neg[:, 1:NCH, 0:1], ALU.mult)\
                    .then_inc(sem("fs"), 1)
                pool.wait_ge(sem("x_l1"), NCH * (j + 1))
                for hh in range(2):
                    G.tensor_tensor(XT[:, hh, :, :], BG[:, :, 2 * hh, :], level_t(0), ALU.mult).then_inc(sem("xt_l1"), 1)
                    G.tensor_tensor(X[:, hh, :, :], X[:, hh, :, :], idb, ALU.add).then_inc(sem("x_one"), 1)
                    pool.wait_ge(sem("xt_l1"), 2 * j + hh + 1)
                    G.tensor_tensor(XT[:, hh, :, :], XT[:, hh, :, :], idb, ALU.add).then_inc(sem("x_one"), 1)
                    masked_c(j, 0, hh)
                for v in range(1, LEVELS):
                    for hh in range(2):
                        masked_c(j, v, hh)

            idb = ident.unsqueeze(1).to_broadcast([P, NCH, P])

            def level_t(v):
                return level(v).unsqueeze(1).to_broadcast([P, NCH, P])

            def masked_c(j, v, hh):
                if v:
                    pool.wait_ge(sem("y1_mm"), 2 * LEVELS * j + (2 * (v - 1) + hh + 1))
                G.tensor_tensor(CT[:, hh, :, :], BG[:, :, 2 * hh, :], level_t(v + 1), ALU.mult).then_inc(sem("ct"), 1)

            rounds(pool, PAIRS, pair)

            def mlp(l):
                def up(i, first):
                    for b in range(2):
                        jj = 2 * i + (FT * l + b)
                        pool.wait_ge(sem("silu"), jj + 1)
                        pool.wait_ge(sem("conv_done"), jj + 1)
                        G.tensor_tensor(z[:, bass.ds(2 * i + b, 1), :], silu[:, b, :].unsqueeze(1),
                                        conv[:, 2 * b + 1, :].unsqueeze(1), ALU.mult).then_inc(sem("z"), 1)

                rounds(pool, FT // 2, up)

            mlp(0)
            pool.wait_ge(sem("x_up"), 2 * KD)
            G.memset(flat(kp), 0.0).then_inc(sem("kp_zero"), 1)
            pool.wait_ge(sem("rope_in"), 32)
            for u in range(U_K, U_QM1):
                pool.wait_ge(sem("hn_done"), u + 1)
                if u >= U_K + 2:
                    pool.wait_ge(sem("rope_done"), u - U_K - 1)
                G.tensor_tensor(t1[:, u % 2, :], hz[:, u % 2, :], cosT, ALU.mult).then_inc(sem("rope_cos"), 1)

            def residue(r, first):
                if not first:
                    pool.wait_ge(sem("da_o"), 4 * r)
                G.tensor_copy(qS, qT[:, :, bass.ds(r * P, P)])
                G.tensor_copy(vS.unsqueeze(1), vtok[:, bass.ds(r, 1), 2 * P:6 * P]).then_inc(sem("da_stage"), 1)

            pool.wait_ge(used, N_OUTB)
            pool.wait_ge(sem("v_ev"), 6)
            pool.wait_ge(sem("rope_done"), 12)
            rounds(pool, RES, residue)
            pool.wait_ge(sem("da_y"), 4 * RES)
            memory_attention(1)
            mlp(1)


def shape_constants():
    i = np.arange(P)
    cst = np.zeros((P, C_END), np.float32)
    cst[:, C_ID:C_ID + P] = np.eye(P)
    cst[:, C_ONE:C_ONE + P] = 1
    cst[:, C_BLK:C_BLK + P] = i[:, None] // HD == i[None] // HD
    half = HD // 2
    turn = np.zeros((P, P), np.float32)
    for m in range(P):
        if m % HD < half:
            turn[m + half, m] = -1
        else:
            turn[m - half, m] = 1
    cst[:, C_ROT:C_ROT + P] = turn
    s, t = i[:, None], i[None]
    cst[:, C_TRI:C_TRI + P] = s < t
    cst[:, C_TRI + P:C_TRI + 2 * P] = s <= t
    for v in range(LEVELS + 1):
        b = 1 << v
        cst[:, C_LEV + v * P:C_LEV + (v + 1) * P] = (s // b + 1 == t // b) & (t // b % 2 == 1)
    cst[:, C_LEV + (LEVELS + 1) * P:C_RESET] = cst[:, C_LEV:C_LEV + P].T
    cst[:, C_RESET:C_END] = np.tile((np.arange(PAD) > 0).astype(np.float32), NCH)
    inv = (10000.0 ** (-np.arange(0, HD, 2, dtype=np.float32) / np.float32(HD))).astype(np.float32)
    ang = np.arange(T, dtype=np.float32)[:, None] * inv[None, :]
    rope = np.stack([np.tile(f(ang).T, (4, 1)) for f in (np.cos, np.sin)]).astype(np.float32)
    tok = np.arange(T).reshape(P, RES).T
    keys = tok.reshape(-1)
    masks = np.zeros((P, RES * T + 2 * P), np.float32)
    for r in range(RES):
        dist = tok[r][:, None] - keys[None]
        masks[:, r * T:(r + 1) * T] = np.where((dist >= 0) & (dist <= 128), 0, -1e30)
    d = i[:, None] - i[None]
    masks[:, RES * T:RES * T + P] = np.where(d >= 0, 0, -1e30)
    masks[:, RES * T + P:] = np.where((d >= 0) & (d % 4 == 0), 0, -1e30)
    return cst, rope, masks


def tiles_of(w):
    k, n = w.shape
    return w.reshape(k // P, P, n // P, P).transpose(2, 1, 0, 3).reshape(n // P, P, k)


def columns(v):
    return v.reshape(-1, P).T


def kernel(**inputs):
    import concourse.bacc as _bacc
    from concourse.bass_utils import run_bass_kernel_spmd as _run

    a = {k: np.asarray(v) for k, v in inputs.items()}
    f32 = np.float32
    cst, rope, masks = shape_constants()
    W = PAIRS * P

    w_in = tiles_of(a["a_w_in"][0])
    w_pairs = np.stack([np.stack([w_in[6 + j], w_in[j], w_in[12 + j]]) for j in range(PAIRS)])
    w_small = np.zeros((PAIRS, P, 2 * P), f32)
    for j in range(PAIRS):
        js = slice(j * P, (j + 1) * P)
        w_small[j, 0:HD, 0:P] = a["a_w2"][0][:, js]
        w_small[j, HD:P, 0:P] = a["a_a2"][0][:, js]
        w_small[j, :, P:2 * P] = a["a_g2"][0][:, js]

    w_ring = np.zeros((N_END, P, SLOTW), f32)
    w_ring[N_LORA:N_LORA + 2, :, 0:TILEW] = w_in[18:20]
    w_ring[N_QM0:N_QM0 + 2, :, 0:TILEW] = w_in[20:22]
    w_ring[N_OUTA:N_OUTA + KD, :, 0:TILEW] = tiles_of(a["a_w_out"][0])
    kv = tiles_of(a["kv_w"])
    w_ring[N_K:N_K + 6, :, 0:TILEW] = kv[0:6]
    w_ring[N_V:N_V + 6, :, 0:TILEW] = kv[6:12]
    b_in = tiles_of(a["b_w_in"][0])
    w_ring[N_Q:N_Q + 8, :, 0:TILEW] = b_in
    out_b = tiles_of(a["b_w_out"][0])
    w_ring[N_OUTB:N_OUTB + 4, :, 0:TILEW] = out_b.reshape(4, 2, P, 4 * P).transpose(0, 2, 1, 3).reshape(4, P, TILEW)
    for l, (up, down) in enumerate(((N_UP0, N_DOWN0), (N_UP1, N_DOWN1))):
        u = tiles_of(a["ffn_w_up"][l])
        w_ring[up:up + 2 * FT:2, :, 0:TILEW] = u[0:FT]
        w_ring[up + 1:up + 2 * FT:2, :, 0:TILEW] = u[FT:2 * FT]
        dn = tiles_of(a["ffn_w_down"][l])
        w_ring[down:down + 2 * KD] = dn.reshape(KD, P, 2, SLOTW).transpose(0, 2, 1, 3).reshape(2 * KD, P, SLOTW)
    w_mem = np.ascontiguousarray(a["mem_w_kv"].reshape(2, KD, P, 2 * MEMH * HD).transpose(0, 2, 1, 3))

    par = np.zeros((P, G_END), f32)
    for l in range(2):
        par[:, (G_ATTN0, G_ATTN1)[l]:][:, 0:KD] = columns(a["attn_norm"][l])
        par[:, (G_FFN0, G_FFN1)[l]:][:, 0:KD] = columns(a["ffn_norm"][l])
        par[:, (G_MEM0, G_MEM1)[l]:][:, 0:KD] = columns(a["mem_norm"][l])
        par[:, (G_MQ0, G_MQ1)[l]] = np.tile(a["mem_q_norm"][l], 2)
        par[:, (G_MK0, G_MK1)[l]] = np.tile(a["mem_k_norm"][l], 2)
        taps = np.concatenate([a["ffn_conv_w"][l], a["ffn_conv_b"][l][None]])
        taps = taps.reshape(4, 2, FT, P).transpose(3, 2, 1, 0)
        par[:, G_CONV + l * 2 * FT * 4:][:, 0:2 * FT * 4] = taps.reshape(P, -1)
    par[:, G_KV:G_KV + KD] = columns(a["kv_norm"])
    par[:, G_KN] = np.tile(a["kv_k_norm"], 2)
    par[:, G_QN] = np.tile(a["b_q_norm"][0], 2)
    mu = a["a_mu"][0]
    par[:, MU_WA] = mu[3 * W:3 * W + P]
    par[:, MU_G] = mu[3 * W + P:3 * W + 2 * P]
    per_pair = (mu[W:2 * W], mu[0:W], mu[2 * W:3 * W], a["a_w0"][0], a["a_a0"][0], a["a_k_k"][0], a["a_k_a"][0],
                a["a_r_k"][0].reshape(-1), a["a_lnx_w"][0], a["a_lnx_b"][0])
    par[:, G_PAIR:G_END] = np.stack([columns(v) for v in per_pair], axis=2).reshape(P, -1)

    arrays = {
        "xT": np.ascontiguousarray(a["x"][0].T.reshape(KD, P, T).transpose(1, 0, 2)),
        "memT": np.ascontiguousarray(a["mem"][0].T.reshape(KD, P, NMEM).transpose(1, 0, 2)),
        "consts": cst, "params": par, "ropes": rope, "masks": masks, "w_small": w_small, "w_mem": w_mem,
        "w_pairs": w_pairs, "w_ring": w_ring,
    }
    nc = _bacc.Bacc("TRN2", target_bir_lowering=False, num_devices=1)
    args = [nc.dram_tensor(k, v.shape, mybir.dt.from_np(v.dtype), kind="ExternalInput").ap() for k, v in arrays.items()]
    args.append(nc.dram_tensor("outT", [KD, P, T], F32, kind="ExternalOutput").ap())
    trunk(nc, *args)
    r = _run(nc, [arrays], core_ids=[0])
    return np.ascontiguousarray(r.results[0]["outT"].reshape(D, T).T).reshape(1, T, D)
```

```python
from contextlib import ExitStack

import numpy as np

import concourse.bass as bass
from concourse import mybir

F32 = mybir.dt.float32
F32R = mybir.dt.float32r
ALU = mybir.AluOpType
ACT = mybir.ActivationFunctionType
AX = mybir.AxisListType

P = 128
HP = P // 2
T = 512
D = 1024
KD = D // P
HD = 64
NMEM = 256
MEMH = 4
PAIRS = 6
CHUNK = 128
NCH = T // CHUNK
PAD = CHUNK + 1
LEVELS = 6
ADDS = 4 * LEVELS - 2
MASKS = 2 * LEVELS - 1
FF = 2816
FT = FF // P
RES = 4
SLOTS = 4
SLOTW = FT // 2 * P
TILEW = KD * P
LNX_EPS = 64e-5
RMS_EPS = 1e-6
DECAY = -float(np.exp(-0.5))
NPAR = 10
MUK, MUR, MUV, PW0, PA0, KKP, KAP, RKP, LNW, LNB = range(NPAR)
N_LORA, N_QM0, N_OUTA, N_MLP0, N_K, N_V, N_Q, N_QM1, N_OUTB, N_MLP1, N_END = 0, 2, 4, 12, 72, 78, 84, 90, 92, 96, 156
HALF = FT // 2
UPS = 2 * HALF
U_MK, U_QM0, U_K, U_Q, U_QM1, U_END = 0, 4, 6, 12, 18, 20
C_ID, C_ONE, C_BLK, C_ROT, C_TRI, C_LEV = 0, 128, 256, 384, 512, 768
C_RESET = C_LEV + (LEVELS + 2) * P
C_END = C_RESET + NCH * PAD
G_ATTN0, G_ATTN1, G_KV, G_FFN0, G_FFN1, G_MEM0, G_MEM1 = range(0, 56, 8)
G_KN, G_QN, G_MQ0, G_MQ1, G_MK0, G_MK1, MU_WA, MU_G = range(56, 64)
G_CONV = 64
G_PAIR = G_CONV + 2 * 2 * FT * 4
G_END = G_PAIR + PAIRS * NPAR
ARENA = 26320


def mlp_tiles(l, half):
    n = (N_MLP0, N_MLP1)[l] + half * (UPS + KD)
    return n, n + UPS


def width(n):
    down = any(mlp_tiles(l, f)[1] <= n < mlp_tiles(l, f)[1] + KD for l in range(2) for f in range(2))
    return SLOTW if down else TILEW


def mlp_pairs(eng, step):
    step(0, 0)
    with eng.Fori(0, (HALF - 3) // 2) as i:
        step(2 * i + 1, 1)
        step(2 * i + 2, 2)
    for p in range(HALF - 2, HALF):
        step(p, p)


def rounds(eng, n, body):
    body(0, True)
    with eng.Fori(1, n) as i:
        body(i, False)


def four_rounds(eng, body):
    body(0, True, False)
    with eng.Fori(1, RES - 1) as r:
        body(r, False, False)
    body(RES - 1, False, True)


def trunk(nc, xT, memT, consts, params, ropes, masks, w_small, w_mem, w_pairs, w_ring, outT):
    ctx = ExitStack()
    with ctx:
        def sb(name, shape):
            return ctx.enter_context(nc.sbuf_tensor(name, shape, F32))

        made = {}

        def sem(name):
            if name not in made:
                made[name] = ctx.enter_context(nc.semaphore(name))
            return made[name]

        x = sb("x", [P, KD, T])
        y = sb("y", [P, KD, T])
        ring = sb("ring", [P, SLOTS, SLOTW])
        cst = sb("cst", [P, C_END])
        par = sb("par", [P, G_END])
        derived = sb("derived", [P, PAIRS * NPAR + 2])
        rstd = sb("rstd", [P, T])
        mem_k = sb("mem_k", [P, 2, 2, 2, NMEM])
        mem_v = sb("mem_v", [P, 2, 2, MEMH * HD])
        stat = sb("stat", [P, 32])
        epsb = sb("epsb", [P, 2])

        def tensor(group, name, shape, dt=F32):
            return group.enter_context(nc.sbuf_tensor(name, shape, dt))

        with ExitStack() as rwkv_layer:
            h = tensor(rwkv_layer, "h", [P, KD, T])
            arena = tensor(rwkv_layer, "arena", [P, ARENA])
        w_hi = tensor(ctx, "w_hi", [P, 2, SLOTW], F32R)
        w_lo = tensor(ctx, "w_lo", [P, 2, SLOTW], F32R)
        with ExitStack() as mlp_layer:
            in_hi = tensor(mlp_layer, "in_hi", [P, KD, T], F32R)
            in_lo = tensor(mlp_layer, "in_lo", [P, KD, T], F32R)
            in_raw = tensor(mlp_layer, "in_raw", [P, 2, T])
            z_hi = tensor(mlp_layer, "z_hi", [P, HALF, T], F32R)
            z_lo = tensor(mlp_layer, "z_lo", [P, HALF, T], F32R)
            z_raw = tensor(mlp_layer, "z_raw", [P, 2, T])
            conv = tensor(mlp_layer, "conv", [P, 4, T])
            silu = tensor(mlp_layer, "silu", [P, 2, T])
        with ExitStack() as dilated_layer:
            kp = tensor(dilated_layer, "kp", [P, 12, T])
            qT = tensor(dilated_layer, "qT", [P, 6, T])
            vtok = tensor(dilated_layer, "vtok", [P, RES, 6 * P])
            qm_b = tensor(dilated_layer, "qm_b", [P, 2, T])
            with ExitStack() as projections:
                rope = tensor(projections, "rope", [P, 2, T])
                b_hi = tensor(projections, "b_hi", [P, KD, T], F32R)
                b_lo = tensor(projections, "b_lo", [P, KD, T], F32R)
                b_raw = tensor(projections, "b_raw", [P, 2, T])
                hz = tensor(projections, "hz", [P, 2, T])
                t1 = tensor(projections, "t1", [P, 2, T])
            with ExitStack() as attention:
                mask0 = tensor(attention, "mask0", [P, RES, T])
                mask12 = tensor(attention, "mask12", [P, 2 * P])
                qS = tensor(attention, "qS", [P, 6, P])
                vS = tensor(attention, "vS", [P, T])
                sm = tensor(attention, "sm", [P, 2, 6 * P])
                pr = tensor(attention, "pr", [P, 2, 6 * P])
                pT = tensor(attention, "pT", [P, 2, 6 * P])
            with ExitStack() as memory:
                qs_b = tensor(memory, "qs_b", [P, 2, P])
                pm_b = tensor(memory, "pm_b", [P, MEMH, NMEM])
                pt_b = tensor(memory, "pt_b", [P, 2, MEMH, T])
        cosT, sinT = rope[:, 0, :], rope[:, 1, :]

        ident = cst[:, C_ID:C_ID + P]
        ones = cst[:, C_ONE:C_ONE + P]
        blk = cst[:, C_BLK:C_BLK + P]
        rot = cst[:, C_ROT:C_ROT + P]
        tri = cst[:, C_TRI:C_TRI + 2 * P]
        reset = cst[:, C_RESET:C_RESET + NCH * PAD]
        rms_eps, lnx_eps = epsb[:, 0:1], epsb[:, 1:2]

        def level(v):
            return cst[:, C_LEV + v * P:C_LEV + (v + 1) * P]

        def col(i):
            return par[:, i:i + 1]

        def pcol(j, k):
            return par[:, bass.ds(NPAR * j + (G_PAIR + k), 1)]

        def dcol(j, k):
            return derived[:, bass.ds(NPAR * j + k, 1)]

        at = [0]

        def part(*shape):
            n = int(np.prod(shape))
            a = arena[:, at[0]:at[0] + n]
            at[0] += n
            assert at[0] <= ARENA, at[0]
            if len(shape) == 2:
                a = a.rearrange("p (a b) -> p a b", b=shape[1])
            if len(shape) == 3:
                a = a.rearrange("p (a b c) -> p a b c", b=shape[1], c=shape[2])
            return a

        lora_w, lora_a = part(T), part(T)
        sig_g = part(T)
        ws = part(2, P)
        kx, rx, vx, aa = part(T), part(T), part(T), part(T)
        lw, cc = part(NCH, PAD), part(NCH, PAD)
        e_pos, e_neg = part(NCH, PAD), part(NCH, PAD)
        rw_late = at[0]
        kk, kkr, sc1, sc2 = part(T), part(T), part(T), part(T)
        fa, bb, rrk = part(T), part(T), part(T)
        Bf, Kf = part(NCH, P), part(NCH, P)
        bonus, gate, ysb = part(T), part(T), part(T)
        Btok, Ktok = part(NCH, P), part(NCH, P)
        BG, KG = part(NCH, 4, P), part(NCH, 4, P)
        X, XT, CT, Y1 = part(2, NCH, P), part(2, NCH, P), part(2, NCH, P), part(2, NCH, P)
        Usb = part(P)
        Sf = part(P)
        fS = part(4)
        AR = part(NCH, 4, P)
        Vp = part(NCH * 2 * P + P)
        SAp = part(3 * P)
        S = part(P)

        at[0] = rw_late
        hn_a = (part(2, T), part(2, T), part(2, T))
        qm_a = part(2, T)
        memx, memh, mem_rs = part(KD, NMEM), part(KD, NMEM), part(NMEM)
        wmem = part(KD, 2 * MEMH * HD)
        at[0] = rw_late + 8 * T
        qs_a, pm_a, pt_a = part(2, P), part(MEMH, NMEM), part(2, MEMH, T)
        bank = [ctx.enter_context(nc.psum_tensor(f"bank{i}", [P, T], F32)) for i in range(8)]
        mem_attn = [dict(q=qm_a, qs=qs_a, p=pm_a, pt=pt_a, y=6), dict(q=qm_b, qs=qs_b[:, :, :], p=pm_b[:, :, :], pt=pt_b[:, :, :, :], y=2)]
        landed = [sem(f"landed{i}") for i in range(SLOTS)]
        used = sem("ring_used")

        def flat(a):
            return a.rearrange("p a b -> p (a b)")

        def blocks(a, v, odd):
            return a.rearrange("p (n w b) -> p n w b", w=2, b=2 << v)[:, :, odd, :]

        def diag(a, base=0):
            return a[:, base:base + 3 * P].rearrange("p (h w) -> p h w", w=3 * HD)[:, :, 0:HD]

        def by_residue(a):
            return a.rearrange("p (u r) -> p r u", r=RES)

        def unit(s):
            return U_K + s if s < 6 else U_K + s - 6

        def heads_of(u):
            raw, sq, rs = (hz, y[:, 0:2, :], y[:, 2:4, :]) if u >= U_K else hn_a
            n = NMEM if u < U_QM0 else T
            return raw[:, u % 2, 0:n], sq[:, u % 2, 0:n], rs[:, u % 2, 0:n], n

        block = ctx.enter_context(nc.Block())

        @block.sync
        def _(sp):
            sp.dma_start(memx, memT).then_inc(sem("mem_in"), 16)
            sp.dma_start(cst[:, :], consts).then_inc(sem("tables_in"), 16)
            sp.dma_start(par[:, :], params).then_inc(sem("tables_in"), 16)
            sp.dma_start(wmem, w_mem[0]).then_inc(sem("wmem_in"), 16)
            sp.dma_start(x[:, :, :], xT).then_inc(sem("x_in"), 16)

            def ring_tile(n, i, wide=False):
                w = SLOTW if wide else TILEW
                sp.dma_start(ring[:, i, 0:w], w_ring[bass.ds(n, 1), :, 0:w].rearrange("a p w -> (a p) w"))\
                  .then_inc(landed[i], 16)

            for n in range(SLOTS):
                ring_tile(n, n)
            sp.wait_ge(sem("mv_mm"), 2)
            sp.dma_start(wmem, w_mem[1]).then_inc(sem("wmem_in"), 16)
            sp.dma_start(ws, w_small[0].rearrange("p (a m) -> p a m", m=P)).then_inc(sem("ws_in"), 16)
            sp.wait_ge(used, N_OUTA)
            for i in range(3):
                sp.dma_start(ring[:, i, 0:TILEW], w_pairs[0, i]).then_inc(sem(f"wp_in{i}"), 16)
            with sp.Fori(1, PAIRS) as j:
                for i in range(3):
                    sp.wait_ge(sem("krv_mm"), 3 * j + (i - 2))
                    sp.dma_start(ring[:, i, 0:TILEW],
                                 w_pairs[bass.ds(j, 1), i, :, :].rearrange("a p w -> (a p) w"))\
                      .then_inc(sem(f"wp_in{i}"), 16)
                sp.wait_ge(sem("g_mm"), j)
                sp.dma_start(ws, w_small[bass.ds(j, 1)].rearrange("a p (b m) -> (a p) b m", m=P))\
                  .then_inc(sem("ws_in"), 16)
            for n in range(N_OUTA, N_OUTA + SLOTS):
                sp.wait_ge(sem("krv_mm"), 3 * (PAIRS - 1) + min(n - N_OUTA, 2) + 1)
                ring_tile(n, n % SLOTS)

            def stream(n0, n1):
                turns = (n1 - n0) // SLOTS
                if turns > 1:
                    with sp.Fori(0, turns) as i:
                        for b in range(SLOTS):
                            one(SLOTS * i + (n0 + b), n0 + b)
                    n0 += SLOTS * turns
                for n in range(n0, n1):
                    one(n, n)

            def one(n, like):
                sp.wait_ge(sem("w_lo"), n - (N_OUTA + SLOTS - 1))
                ring_tile(n, like % SLOTS, width(like) == SLOTW)

            stream(N_OUTA + SLOTS, N_MLP0)
            for half in range(2):
                up, down = mlp_tiles(0, half)
                stream(up, down)
                stream(down, down + KD)
            stream(N_K, N_K + SLOTS)
            sp.wait_ge(sem("x_up"), 3 * KD)
            sp.dma_start(rope[:, :, :], ropes).then_inc(sem("rope_in"), 16)
            stream(N_K + SLOTS, N_MLP1)
            sp.wait_ge(used, N_OUTB)
            sp.wait_ge(sem("rope_done"), 12)
            sp.dma_start(mask0[:, :, :], masks[:, 0:RES * T].rearrange("p (r t) -> p r t", t=T)).then_inc(sem("mask_in"), 16)
            sp.dma_start(mask12[:, :], masks[:, RES * T:RES * T + 2 * P]).then_inc(sem("mask_in"), 16)
            for half in range(2):
                up, down = mlp_tiles(1, half)
                stream(up, down)
                stream(down, down + KD)
            for m in range(KD):
                sp.wait_ge(sem("x_up"), 5 * KD + m + 1)
                sp.dma_start(outT[m], x[:, m, :]).then_inc(sem("out"), 16)
            sp.wait_ge(sem("out"), 16 * KD)

        @block.tensor
        def _(pe):
            def mm(out, lhsT, rhs, first=True, last=True):
                return nc.tensor.matmul(out, lhsT, rhs, start=first, stop=last, skip_group_check=True)

            def head_sum(u):
                _, sq, _, n = heads_of(u)
                pe.wait_ge(sem("hn_sqd"), u + 1)
                if u >= 2:
                    pe.wait_ge(sem("hn_sd"), u - 1)
                mm(bank[2 + u % 2][:, 0:n], blk, sq).then_inc(sem("hn_ss"), 1)

            def rope_turn(u):
                pe.wait_ge(sem("hn_done"), u + 1)
                if u >= U_K + 2:
                    pe.wait_ge(sem("rope_done"), u - U_K - 1)
                mm(bank[4 + u % 2][:, :], rot, hz[:, u % 2, :]).then_inc(sem("rope_mm"), 1)

            def split_product(out, n, hi, lo, kn, base=0, ready=None, between=lambda k: None):
                for k in range(kn):
                    between(k)
                    if ready:
                        pe.wait_ge(sem(ready[0]), ready[1] + k)
                    ks = slice(base + k * P, base + (k + 1) * P)
                    mm(out, w_hi[:, n % 2, ks], hi[:, k, :], k == 0, False)
                    mm(out, w_hi[:, n % 2, ks], lo[:, k, :], False, False)
                    i = mm(out, w_lo[:, n % 2, ks], hi[:, k, :], False, k == kn - 1)
                return i

            def ring_product(out, slot, rhs, kn, ready=None):
                for k in range(kn):
                    if ready:
                        pe.wait_ge(sem(ready[0]), ready[1] + k)
                    i = mm(out, ring[:, slot, k * P:(k + 1) * P], rhs(k), k == 0, k == kn - 1)
                return i

            def head_tile(u, n, src, h_at=None):
                pe.wait_ge(landed[n % SLOTS], 16 * (n // SLOTS + 1))
                if u >= 2:
                    pe.wait_ge(sem("hn_sqd"), u - 1)
                ring_product(bank[u % 2][:, :], n % SLOTS, lambda k: src[:, k, :], KD,
                             ready=("h_ready", h_at + 1) if h_at is not None else None).then_inc(used, 1)

            pe.wait_ge(sem("tables_in"), 32)
            for k in range(KD):
                pe.wait_ge(sem("msq"), k + 1)
                q = mm(bank[6][:, 0:NMEM], ones, memh[:, k, :], k == 0, k == KD - 1)
            q.then_inc(sem("mem_ss"), 1)
            for k in range(KD):
                pe.wait_ge(sem("xsq"), k + 1)
                q = mm(bank[7][:, :], ones, h[:, k, :], k == 0, k == KD - 1)
            q.then_inc(sem("x_ss"), 1)
            for l in range(2):
                pe.wait_ge(sem("wmem_in"), 16 * (l + 1))
                for i in range(2):
                    u = U_MK + 2 * l + i
                    if u >= 2:
                        pe.wait_ge(sem("hn_sqd"), u - 1)
                    for k in range(KD):
                        pe.wait_ge(sem("memh"), l * KD + k + 1)
                        q = mm(bank[u % 2][:, 0:NMEM], wmem[:, k, i * P:(i + 1) * P], memh[:, k, :], k == 0, k == KD - 1)
                    q.then_inc(sem("mk_mm"), 1)
                for i in range(2):
                    if l:
                        pe.wait_ge(sem("mv_out"), i + 1)
                    for k in range(KD):
                        q = mm(bank[4 + i][:, 0:NMEM], memh[:, k, i * P:(i + 1) * P],
                               wmem[:, k, 2 * P:4 * P], k == 0, k == KD - 1)
                    q.then_inc(sem("mv_mm"), 1)
                for i in range(2):
                    head_sum(U_MK + 2 * l + i)

            pe.wait_ge(sem("mv_out"), 4)
            for i in range(2):
                n = N_LORA + i
                pe.wait_ge(landed[n], 16)
                ring_product(bank[4 + i][:, :], n, lambda k: h[:, k, :], KD, ready=("h_ready", 1)).then_inc(used, 1)
            for i in range(2):
                head_tile(U_QM0 + i, N_QM0 + i, h)
            for i in range(2):
                head_sum(U_QM0 + i)
            pe.wait_ge(sem("shifted"), 2)

            def memory_attention(l):
                m = mem_attn[l]

                def scores(c, first):
                    g = 4 * l + c
                    pe.wait_ge(sem("ma_qs"), g + 1)
                    if not first:
                        pe.wait_ge(sem("ma_exp"), 4 * g)
                    for i in range(2):
                        mm(bank[i][:, :], m["qs"][:, i, :], mem_k[:, l, i, :, :].rearrange("p h t -> p (h t)"))\
                            .then_inc(sem("ma_sc"), 1)

                def token_tile(c, first, last):
                    g = 4 * l + c
                    if not last:
                        scores(c + 1, False)
                    pe.wait_ge(sem("ma_pn"), g + 1)
                    if not first:
                        pe.wait_ge(sem("ma_pt"), 2 * g)
                    for t in range(2):
                        for hh in range(MEMH):
                            q = nc.tensor.transpose(bank[2 + t][:, hh * P:(hh + 1) * P],
                                                    m["p"][:, hh, t * P:(t + 1) * P], ident)
                        q.then_inc(sem("ma_tr"), 1)

                scores(0, True)
                four_rounds(pe, token_tile)
                pe.wait_ge(sem("ma_pt"), 8 * l + 8)
                for hh in range(MEMH):
                    r = HD * (hh % 2)
                    for t in range(2):
                        q = mm(bank[4 + hh // 2][r:r + HD, :], mem_v[:, l, t, hh * HD:(hh + 1) * HD],
                               m["pt"][:, t, hh, :], t == 0, t == 1)
                    if hh % 2:
                        q.then_inc(sem("ma_o"), 1)

            memory_attention(0)

            def chain(j, c, hop):
                if hop == 0:
                    if c == 0:
                        pe.wait_ge(sem("dx_add"), ADDS * (j + 1))
                        pe.wait_ge(sem("v_tok"), j + 1)
                    else:
                        pe.wait_ge(sem("s_up"), 3 * j + c)
                    for hh in range(2):
                        o = bank[4][:, hh * P:(hh + 1) * P]
                        if c:
                            mm(o, AR[:, c, 2 * hh, :], S, True, False)
                        q = mm(o, KG[:, c, 2 * hh, :], diag(Vp, 2 * P * c), c == 0, True)
                    q.then_inc(sem("u_mm"), 1)
                elif hop == 1:
                    pe.wait_ge(sem("u_sb"), NCH * j + c + 1)
                    for hh in range(2):
                        q = mm(bank[4][:, hh * P:(hh + 1) * P], XT[:, hh, c, :], Usb)
                    q.then_inc(sem("sa_mm"), 1)
                else:
                    pe.wait_ge(sem("sa_sb"), NCH * j + c + 1)
                    o = bank[7][:, c * P:(c + 1) * P]
                    if c < NCH - 1:
                        q = mm(bank[5][:, 0:P], Btok[:, c, :], diag(SAp), True, False)
                        q = mm(bank[5][:, 0:P], Ktok[:, c, :], diag(Vp, 2 * P * c), False, True)
                    if c:
                        mm(o, S, AR[:, c, 1, :], True, False)
                        q = mm(o, S, AR[:, c, 3, :], False, False)
                    if c < NCH - 1:
                        q.then_inc(sem("st_mm"), 1)
                    for hh in range(2):
                        mm(o, SAp[:, hh * P:(hh + 1) * P], BG[:, c, 2 * hh + 1, :], c == 0 and hh == 0, False)
                        q = mm(o, Vp[:, 2 * P * c + hh * P:2 * P * c + (hh + 1) * P], KG[:, c, 2 * hh + 1, :],
                               False, hh == 1)
                    q.then_inc(sem("y_mm"), 1)

            def to_tokens(src, sig):
                for c in range(NCH):
                    q = nc.tensor.transpose(bank[5][:, c * P:(c + 1) * P], src[:, c * P:(c + 1) * P], ident)
                q.then_inc(sem(sig), 1)

            def mean_of(j):
                pe.wait_ge(sem("y_sb"), j + 1)
                mm(bank[6][:, :], blk, ysb).then_inc(sem("mean_mm"), 1)

            def variance_of(j):
                pe.wait_ge(sem("y_sq"), j + 1)
                mm(bank[7][:, :], blk, sc1).then_inc(sem("var_mm"), 1)

            def pair(j, first):
                pe.wait_ge(sem("ws_in"), 16 * (j + 1))
                if not first:
                    pe.wait_ge(sem("g_sb"), j)
                mm(bank[0][:, :], ws[:, 0, :], lora_w).then_inc(sem("w_mm"), 1)
                if not first:
                    pe.wait_ge(sem("bonus"), j)
                mm(bank[1][:, :], ws[:, 0, :], lora_a).then_inc(sem("a_mm"), 1)
                for g in range(12):
                    if not first:
                        chain(j - 1, g // 3, g % 3)
                    if g == 8:
                        pe.wait_ge(sem("kk_sq"), j + 1)
                        mm(bank[0][:, :], blk, sc1).then_inc(sem("kkss_mm"), 1)
                    t, b = g // 4, (0, 1, 1)[g // 4]
                    if g % 4 == 0:
                        pe.wait_ge(sem(f"wp_in{t}"), 16 * (j + 1))
                        pe.wait_ge(*((sem("w_sig"), j + 1), (sem("a_sig"), j + 1), (sem("shifted"), 3 * j + 4))[t])
                    for k in (2 * (g % 4), 2 * (g % 4) + 1):
                        q = mm(bank[b][:, :], ring[:, t, k * P:(k + 1) * P], h[:, k, :], k == 0, k == KD - 1)
                    if g % 4 == 3:
                        q.then_inc(sem("krv_mm"), 1)
                pe.wait_ge(sem("shifted"), 3 * j + 5)
                to_tokens(vx, "vt_mm")
                if not first:
                    mean_of(j - 1)
                pe.wait_ge(sem("kf"), j + 1)
                pe.wait_ge(sem("v_tok"), j + 1)
                to_tokens(flat(Kf), "kt_mm")
                pe.wait_ge(sem("bf"), j + 1)
                pe.wait_ge(sem("k_tok"), j + 1)
                to_tokens(flat(Bf), "bt_mm")
                if not first:
                    variance_of(j - 1)
                pe.wait_ge(sem("ar"), j + 1)
                for c in range(NCH):
                    if c:
                        pe.wait_ge(sem("kg_ev"), NCH * j + c)
                    mm(bank[2][:, :], Kf[:, c, :], flat(AR[:, c, :, :])).then_inc(sem("kg_mm"), 1)
                    if c:
                        pe.wait_ge(sem("bg_ev"), NCH * j + c)
                    mm(bank[3][:, :], Bf[:, c, :], flat(AR[:, c, :, :])).then_inc(sem("bg_mm"), 1)
                    if c:
                        pe.wait_ge(sem("x_l1"), NCH * j + c)
                    for hh in range(2):
                        q = mm(bank[4][:, hh * P:(hh + 1) * P], AR[:, c, 2 * hh, :], Bf[:, c, :])
                    q.then_inc(sem("m_mm"), 1)
                pe.wait_ge(sem("rk"), j + 1)
                mm(bank[1][:, :], blk, rrk).then_inc(sem("bonus_mm"), 1)
                pe.wait_ge(sem("kk_sd"), j + 1)
                mm(bank[0][:, :], ws[:, 1, :], sig_g).then_inc(sem("g_mm"), 1)
                pe.wait_ge(sem("kg_ev"), NCH * j + NCH)
                pe.wait_ge(sem("b_tok"), j + 1)
                if not first:
                    pe.wait_ge(sem("y_sd"), j)
                for v in range(LEVELS):
                    for hh in range(2):
                        pe.wait_ge(sem("ct"), MASKS * j + (2 * v + hh if v else 1))
                        if v == 0:
                            pe.wait_ge(sem("x_one"), j + 1)
                        else:
                            pe.wait_ge(sem("dx_add"), ADDS * j + (4 * (v - 1) + 2 * hh + 1))
                        for c in range(NCH):
                            q = mm(bank[2 + hh][:, c * P:(c + 1) * P], CT[:, hh, c, :], X[:, hh, c, :])
                        q.then_inc(sem("y1_mm"), 1)
                    for hh in range(2):
                        pe.wait_ge(sem("y1_sb"), 2 * LEVELS * j + (2 * v + hh + 1))
                        if v == 0:
                            pe.wait_ge(sem("xt_one"), j + 1)
                        else:
                            pe.wait_ge(sem("dx_add"), ADDS * j + (4 * (v - 1) + 2 * hh + 2))
                        for odd in range(v == LEVELS - 1, 2):
                            for c in range(NCH):
                                o = bank[4 + 2 * hh + odd][:, c * HP:(c + 1) * HP].rearrange("p (n b) -> p n b", b=2 << v)
                                if odd:
                                    q = mm(o, Y1[:, hh, c, :], blocks(XT[:, hh, c, :], v, 1))
                                else:
                                    q = mm(o, XT[:, hh, c, :], blocks(Y1[:, hh, c, :], v, 0))
                            q.then_inc(sem("dx_mm"), 1)

            pe.wait_ge(sem("lora_in"), 3)
            pe.wait_ge(sem("ma_y"), 2)
            rounds(pe, PAIRS, pair)
            for g in range(12):
                chain(PAIRS - 1, g // 3, g % 3)
            mean_of(PAIRS - 1)
            variance_of(PAIRS - 1)

            def split_ready(n, like=None):
                pe.wait_ge(sem("w_lo"), n - (N_OUTA - 1))

            def out_product(e, n0, kn, y_at, per_slot):
                for m in range(KD):
                    n, b = n0 + m // per_slot, m % per_slot
                    split_ready(n)
                    if m >= 2 or e:
                        pe.wait_ge(sem("x_up"), KD * e + m - 1)
                    q = split_product(bank[m % 2][:, :], n, in_hi, in_lo, kn, b * kn * P,
                                      ("y_split", y_at + 1) if m == 0 else None)
                    q.then_inc(used if b == per_slot - 1 else sem("out_half"), 1)
                square_sum(e // 3 * 2)

            def square_sum(q):
                pe.wait_ge(sem("sq_sum"), (KD - 2) * (q + 1))
                mm(bank[7][:, :], ones, y[:, 0, :], True, False)
                pe.wait_ge(sem("xsq"), KD * (q + 2))
                mm(bank[7][:, :], ones, y[:, KD - 1, :], False, True).then_inc(sem("x_ss"), 1)

            out_product(0, N_OUTA, KD, 0, 1)

            def mlp(l, h_at):
                for half in range(2):
                    up, down = mlp_tiles(l, half)
                    g0 = FT * l + HALF * half

                    def up_pair(p, q):
                        if isinstance(p, int) is False or g0 + p >= 2:
                            pe.wait_ge(sem("conv_done"), p + (g0 - 1))
                        for s in range(2):
                            n = up + 2 * q + s
                            split_ready(2 * p + (up + s))
                            b = 2 * ((g0 + q) % 2) + s
                            split_product(bank[b][:, :], n, in_hi, in_lo, KD,
                                          ready=("h_ready", h_at + 1) if q == 0 and s == 0 and half == 0 else None)\
                                .then_inc(used, 1)

                    mlp_pairs(pe, up_pair)
                    e = 3 * l + 1 + half
                    with pe.Fori(0, 2) as i:
                        for b in range(SLOTS):
                            split_ready(SLOTS * i + (down + b))
                            pe.wait_ge(sem("x_up"), SLOTS * i + (KD * e + b - 1))
                            for k in range(HALF):
                                if b == 0:
                                    pe.wait_ge(sem("z"), g0 + k + 1)
                                ks = slice(k * P, (k + 1) * P)
                                w = (down + b) % 2
                                o = bank[4 + b % 2][:, :]
                                mm(o, w_hi[:, w, ks], z_hi[:, k, :], k == 0, False)
                                mm(o, w_hi[:, w, ks], z_lo[:, k, :], False, False)
                                q = mm(o, w_lo[:, w, ks], z_hi[:, k, :], False, k == HALF - 1)
                            q.then_inc(used, 1)
                if l == 0:
                    square_sum(1)

            mlp(0, KD)

            pe.wait_ge(sem("kp_zero"), 1)
            for s in range(22):
                def behind(k):
                    if k == 2 and 6 <= s - 1 < 12:
                        i = s - 7
                        pe.wait_ge(sem("pos_read"), s)
                        if i >= 2:
                            pe.wait_ge(sem("v_ev"), i - 1)
                        src = by_residue(y[:, (s - 1) % 2, :])
                        for r in range(RES):
                            q = nc.tensor.transpose(bank[6 + i % 2][:, r * P:(r + 1) * P], src[:, r, :], ident)
                        q.then_inc(sem("v_mm2"), 1)
                    elif k == 2 and 0 <= s - 1 < 20:
                        head_sum(unit(s - 1))
                    if k == 3 and 0 <= s - 2 < 18 and not 6 <= s - 2 < 12:
                        rope_turn(unit(s - 2))

                if s < 20:
                    n = N_K + s
                    split_ready(n)
                    if s >= 2:
                        pe.wait_ge(sem("pos_read"), s - 1)
                    split_product(bank[s % 2][:, :], n, b_hi, b_lo, KD, between=behind,
                                  ready=("h_ready", (2 if s == 0 else 3) * KD + 1) if s in (0, 12) else None)\
                        .then_inc(used, 1)
                else:
                    behind(2)
                    behind(3)

            pe.wait_ge(sem("rope_done"), 12)
            pe.wait_ge(sem("hn_done"), U_END)
            pe.wait_ge(sem("v_ev"), 6)

            def scores(r, s, first):
                if not (first and s < 2):
                    pe.wait_ge(sem("da_sm"), 4 * r + (s - 1))
                if s == 0:
                    pe.wait_ge(sem("da_stage"), r + 1)
                rs, b = bass.ds(r * P, P), 2 * (s % 2)
                mm(bank[b][:, :], qS[:, s // 2, :], kp[:, s, :])
                mm(bank[b + 1][:, 0:P], qS[:, 2 + s // 2, :], kp[:, SLOTS + s, rs])
                mm(bank[b + 1][:, P:2 * P], qS[:, 4 + s // 2, :], kp[:, 2 * SLOTS + s, rs])\
                    .then_inc(sem("da_sc"), 1)

            def outputs(r, s, first):
                if s == 0:
                    pe.wait_ge(sem("da_vstage"), r + 1)
                pe.wait_ge(sem("da_pt"), 4 * r + (s + 1))
                if s == 3:
                    pe.wait_ge(sem("da_y"), 4 * r + 1)
                elif not first:
                    pe.wait_ge(sem("da_y"), 4 * r + (s - 3))
                o = bank[6 + s // 2][HD * (s % 2):HD * (s % 2) + HD, 0:P]
                for q in range(6):
                    at = ((q - RES) * 4 + s) * HD
                    v = vtok[:, q, s * HD:(s + 1) * HD] if q < RES else vS[:, at:at + HD]
                    i = mm(o, v, pT[:, s % 2, q * P:(q + 1) * P], q == 0, q == 5)
                i.then_inc(sem("da_o"), 1)

            def residue(r, first, last):
                for s in range(4):
                    if s < 2 or not last:
                        scores(r + (s + 2) // 4, (s + 2) % 4, first and s < 2)
                    if s:
                        outputs(r, s - 1, first)
                    elif not first:
                        outputs(r - 1, 3, False)
                    pe.wait_ge(sem("da_pn"), 4 * r + (s + 1))
                    if not (first and s == 0):
                        pe.wait_ge(sem("da_pt"), 4 * r + s)
                    for q in range(6):
                        i = nc.tensor.transpose(bank[4 + q // 4][:, (q % 4) * P:(q % 4 + 1) * P],
                                                pr[:, s % 2, q * P:(q + 1) * P], ident)
                    i.then_inc(sem("da_tr"), 1)

            scores(0, 0, True)
            scores(0, 1, True)
            four_rounds(pe, residue)
            outputs(RES - 1, 3, False)
            pe.wait_ge(sem("da_y"), 4 * RES)
            memory_attention(1)
            pe.wait_ge(sem("ma_y"), 4)
            out_product(3, N_OUTB, 4, KD, 2)
            mlp(1, 4 * KD)

        @block.scalar
        def _(act):
            def root(out, in_, count, eps):
                return nc.scalar.activation(out, in_, ACT.Sqrt, bias=eps, scale=1.0 / count)

            def copy(out, in_):
                return nc.scalar.activation(out, in_, ACT.Copy)

            act.wait_ge(sem("mem_in"), 16)
            for k in range(KD):
                nc.scalar.activation(memh[:, k, :], memx[:, k, :], ACT.Square).then_inc(sem("msq"), 1)
            act.wait_ge(sem("x_in"), 16)
            for k in range(KD):
                nc.scalar.activation(h[:, k, :], x[:, k, :], ACT.Square).then_inc(sem("xsq"), 1)
            act.wait_ge(sem("eps"), 2)
            act.wait_ge(sem("mem_ss"), 1)
            root(mem_rs, bank[6][:, 0:NMEM], D, rms_eps).then_inc(sem("mem_sd"), 1)

            def stream_root(e):
                act.wait_ge(sem("x_ss"), e + 1)
                root(rstd[:, :], bank[7][:, :], D, rms_eps).then_inc(sem("x_sd"), 1)

            stream_root(0)

            def head_out(u):
                raw, sq, _, n = heads_of(u)
                if u < U_QM0:
                    act.wait_ge(sem("mk_mm"), u + 1)
                else:
                    act.wait_ge(used, (N_QM0 + u - U_QM0 if u < U_K else N_K + u - U_K + 6 * (u >= U_Q)) + 1)
                if u >= 2:
                    act.wait_ge(sem("hn_done"), u - 1)
                    act.wait_ge(sem("hn_ss"), u - 1)
                if u >= U_K + 2:
                    act.wait_ge(sem("rope_done"), min(u - U_K - 1, 12))
                copy(raw, bank[u % 2][:, 0:n])
                nc.scalar.activation(sq, bank[u % 2][:, 0:n], ACT.Square).then_inc(sem("hn_sqd"), 1)
                if u >= U_K:
                    act.wait_ge(sem("hn_sqd"), u + 1)
                    act.sem_inc(sem("pos_read"), 1)

            def head_root(u):
                _, _, rs, n = heads_of(u)
                act.wait_ge(sem("hn_ss"), u + 1)
                if u >= 2:
                    act.wait_ge(sem("hn_done"), u - 1)
                if U_K + 2 <= u:
                    act.wait_ge(sem("rope_done"), min(u - U_K - 1, 12))
                root(rs, bank[2 + u % 2][:, 0:n], HD, rms_eps).then_inc(sem("hn_sd"), 1)

            for l in range(2):
                for i in range(2):
                    head_out(2 * l + i)
                for i in range(2):
                    act.wait_ge(sem("mv_mm"), 2 * l + i + 1)
                    copy(mem_v[:, l, i, :], bank[4 + i][:, 0:NMEM]).then_inc(sem("mv_out"), 1)
                for i in range(2):
                    head_root(2 * l + i)

            act.wait_ge(sem("derived"), 2)
            for i, dst in enumerate((kx, rx)):
                act.wait_ge(used, N_LORA + i + 1)
                nc.scalar.activation(dst, bank[4 + i][:, :], ACT.Identity,
                                     scale=derived[:, PAIRS * NPAR + i:PAIRS * NPAR + i + 1]).then_inc(sem("own"), 1)
            for i in range(2):
                head_out(U_QM0 + i)
            for i in range(2):
                head_root(U_QM0 + i)
            act.wait_ge(sem("shifted"), 2)
            act.wait_ge(sem("zeroed"), 2)
            nc.scalar.activation(lora_w[0:HD], kx[0:HD], ACT.Tanh).then_inc(sem("lora_in"), 1)
            copy(lora_a[HD:P], kx[HD:P]).then_inc(sem("lora_in"), 1)
            nc.scalar.activation(sig_g, rx, ACT.Sigmoid).then_inc(sem("lora_in"), 1)

            def memory_attention(l):
                m = mem_attn[l]

                def exps(c, first):
                    g = 4 * l + c
                    if not first:
                        act.wait_ge(sem("ma_tr"), 2 * g)
                    for i in range(2):
                        act.wait_ge(sem("ma_nb"), 2 * g + i + 1)
                        for hh in range(2):
                            k = 2 * i + hh
                            nc.scalar.activation(m["p"][:, k, :], bank[i][:, hh * NMEM:(hh + 1) * NMEM], ACT.Exp,
                                                 bias=stat[:, 4 + k:5 + k], scale=HD ** -0.5,
                                                 accum_out=stat[:, 8 + k:9 + k]).then_inc(sem("ma_exp"), 1)

                def token_tile(c, first, last):
                    g = 4 * l + c
                    if not last:
                        exps(c + 1, False)
                    for t in range(2):
                        act.wait_ge(sem("ma_tr"), 2 * g + t + 1)
                        copy(m["pt"][:, t, :, bass.ds(c * P, P)], bank[2 + t][:, :].rearrange("p (h t) -> p h t", t=P))\
                            .then_inc(sem("ma_pt"), 1)

                exps(0, True)
                four_rounds(act, token_tile)
                for i in range(2):
                    act.wait_ge(sem("ma_o"), 2 * l + i + 1)
                    copy(y[:, m["y"] + i, :], bank[4 + i][:, :]).then_inc(sem("ma_y"), 1)

            memory_attention(0)

            def bchunks(a):
                return a.rearrange("p (c t) -> p c t", t=CHUNK)

            def hop_u(j, c):
                act.wait_ge(sem("u_mm"), NCH * j + c + 1)
                copy(Usb.rearrange("p (h w) -> p h w", w=HD), diag(bank[4])).then_inc(sem("u_sb"), 1)

            def hop_sa(j, c):
                act.wait_ge(sem("sa_mm"), NCH * j + c + 1)
                copy(diag(SAp), diag(bank[4])).then_inc(sem("sa_sb"), 1)

            def y_read(j):
                act.wait_ge(sem("y_mm"), NCH * (j + 1))
                copy(ysb, bank[7][:, :]).then_inc(sem("y_sb"), 1)

            def y_square(j):
                act.wait_ge(sem("yc"), j + 1)
                nc.scalar.activation(sc1, ysb, ACT.Square).then_inc(sem("y_sq"), 1)

            def y_root(j):
                act.wait_ge(sem("var_mm"), j + 1)
                root(sc2, bank[7][:, :], HD, lnx_eps).then_inc(sem("y_sd"), 1)

            def y_affine(j):
                act.wait_ge(sem("yn"), j + 1)
                nc.scalar.activation(ysb, ysb, ACT.Identity, scale=pcol(j, LNW), bias=pcol(j, LNB))\
                    .then_inc(sem("y_ln"), 1)

            def own_part(dst, b, j, k, sig):
                nc.scalar.activation(dst, bank[b][:, :], ACT.Identity, scale=dcol(j, k)).then_inc(sem(sig), 1)

            def pair(j, first):
                act.wait_ge(sem("w_mm"), j + 1)
                nc.scalar.activation(lw[:, :, 1:], bchunks(bank[0][:, :]), ACT.Sigmoid, bias=pcol(j, PW0))\
                    .then_inc(sem("w_sig"), 1)
                act.wait_ge(sem("a_mm"), j + 1)
                nc.scalar.activation(aa, bank[1][:, :], ACT.Sigmoid, bias=pcol(j, PA0)).then_inc(sem("a_sig"), 1)
                act.wait_ge(sem("a_sig"), j + 1)
                nc.scalar.activation(fa, aa, ACT.Identity, scale=pcol(j, KAP), bias=dcol(j, KAP)).then_inc(sem("fa"), 1)
                if not first:
                    hop_u(j - 1, 0)
                    hop_sa(j - 1, 0)
                act.wait_ge(sem("cc"), j + 1)
                nc.scalar.activation(e_pos, cc, ACT.Exp, scale=DECAY)
                nc.scalar.activation(e_neg, cc, ACT.Exp, scale=-DECAY).then_inc(sem("e_neg"), 1)
                if not first:
                    hop_u(j - 1, 1)
                act.wait_ge(sem("krv_mm"), 3 * j + 1)
                own_part(kx, 0, j, MUK, "own")
                if not first:
                    hop_sa(j - 1, 1)
                    hop_u(j - 1, 2)
                act.wait_ge(sem("shifted"), 3 * j + 3)
                nc.scalar.activation(kkr, kx, ACT.Identity, scale=pcol(j, KKP)).then_inc(sem("kkr"), 1)
                act.wait_ge(sem("kkr"), j + 1)
                nc.scalar.activation(sc1, kkr, ACT.Square).then_inc(sem("kk_sq"), 1)
                if not first:
                    hop_sa(j - 1, 2)
                act.wait_ge(sem("krv_mm"), 3 * j + 2)
                own_part(rx, 1, j, MUR, "own")
                act.wait_ge(sem("kkss_mm"), j + 1)
                nc.scalar.activation(sc2, bank[0][:, :], ACT.Sqrt).then_inc(sem("kk_sd"), 1)
                if not first:
                    hop_u(j - 1, 3)
                    hop_sa(j - 1, 3)
                act.wait_ge(sem("krv_mm"), 3 * j + 3)
                own_part(vx, 1, j, MUV, "own")
                if not first:
                    y_read(j - 1)
                act.wait_ge(sem("vt_mm"), j + 1)
                v_to_tokens()
                act.wait_ge(sem("kt_mm"), j + 1)
                copy(flat(Ktok), bank[5][:, :]).then_inc(sem("k_tok"), 1)
                if not first:
                    y_square(j - 1)
                act.wait_ge(sem("bt_mm"), j + 1)
                copy(flat(Btok), bank[5][:, :]).then_inc(sem("b_tok"), 1)
                if not first:
                    act.wait_ge(sem("kk_n"), j + 1)
                    y_root(j - 1)
                for i in range(2 * LEVELS):
                    act.wait_ge(sem("y1_mm"), 2 * LEVELS * j + i + 1)
                    copy(flat(Y1[:, i % 2, :, :]), bank[2 + i % 2][:, :]).then_inc(sem("y1_sb"), 1)
                    if i == 1:
                        if not first:
                            y_affine(j - 1)
                    if i == 3:
                        if not first:
                            act.wait_ge(sem("y_out"), j)
                        act.wait_ge(sem("g_mm"), j + 1)
                        copy(gate, bank[0][:, :]).then_inc(sem("g_sb"), 1)

            def v_to_tokens():
                for hh in range(2):
                    dst = Vp[:, 0:NCH * 2 * P].rearrange("p (c w) -> p c w", w=2 * P)[:, :, 3 * HD * hh:3 * HD * hh + HD]
                    src = bank[5][:, :].rearrange("p (c w) -> p c w", w=P)[:, :, HD * hh:HD * (hh + 1)]
                    q = copy(dst, src)
                q.then_inc(sem("v_tok"), 1)

            act.wait_ge(sem("rw_zero"), 1)
            rounds(act, PAIRS, pair)
            j = PAIRS - 1
            for c in range(NCH):
                hop_u(j, c)
                hop_sa(j, c)
            y_read(j)
            y_square(j)
            y_root(j)
            y_affine(j)

            def split(n, like=None):
                like = n if like is None else like
                if isinstance(n, int) and n >= N_END:
                    return
                i, w = like % SLOTS, width(like)
                act.wait_ge(landed[i], 16 * ((n - like) // SLOTS + like // SLOTS + 1) if isinstance(n, int) else turns(n, like))
                if not isinstance(n, int) or n >= N_OUTA + 2:
                    act.wait_ge(used, n - 1)
                copy(w_hi[:, like % 2, 0:w], ring[:, i, 0:w]).then_inc(sem("w_hi"), 1)

            def input_split(k0, kn, src, at, hi, name):
                for k in range(kn):
                    act.wait_ge(sem(name), at + k + 1)
                    copy(hi[:, k, :], src(k)).then_inc(sem("in_hi"), 1)

            def squares(n0, e, slots):
                for m in range(KD):
                    if slots == 1 or m % 2 == 1:
                        split(n0 + int(slots * (m + 1)) + 1)
                    if e in (0, 2, 3):
                        act.wait_ge(sem("x_up"), KD * e + m + 1)
                        nc.scalar.activation(y[:, m, :], x[:, m, :], ACT.Square).then_inc(sem("xsq"), 1)

            act.wait_ge(sem("y_out"), PAIRS)
            for n in range(N_OUTA, N_OUTA + 2):
                split(n)
            for k in range(KD):
                copy(in_hi[:, k, :], y[:, k, :]).then_inc(sem("in_hi"), 1)
            squares(N_OUTA, 0, 1)
            stream_root(1)

            def norm_split(q, hi, raw):
                for k in range(KD):
                    act.wait_ge(sem("n_raw"), KD * q + k + 1)
                    copy(hi[:, k, :], raw[:, k % 2, :]).then_inc(sem("in_hi"), 1)

            def tap(l, tile, k):
                return par[:, bass.ds(4 * tile + (G_CONV + l * 2 * FT * 4 + k), 1)]

            def mlp(l):
                for half in range(2):
                    up, down = mlp_tiles(l, half)
                    g0 = FT * l + HALF * half

                    def up_pair(p, q):
                        b = (g0 + q) % 2
                        for s in range(2):
                            split_at(p, up + 2 + s, q)
                            act.wait_ge(used, 2 * p + (up + s + 1))
                            if s == 0 and (not isinstance(p, int) or g0 + p >= 2):
                                act.wait_ge(sem("z"), p + (g0 - 1))
                            tile = 2 * p + (2 * HALF * half + s)
                            nc.scalar.activation(conv[:, 2 * b + s, :], bank[2 * b + s][:, :], ACT.Identity,
                                                 scale=tap(l, tile, 2), bias=tap(l, tile, 3)).then_inc(sem("conv_own"), 1)
                        act.wait_ge(sem("conv_gate"), p + (g0 + 1))
                        nc.scalar.activation(silu[:, b, :], conv[:, 2 * b, :], ACT.Silu).then_inc(sem("silu"), 1)
                        act.wait_ge(sem("z_raw"), p + (g0 + 1))
                        copy(z_hi[:, bass.ds(p, 1), :], z_raw[:, b, :].unsqueeze(1)).then_inc(sem("z_hi"), 1)

                    mlp_pairs(act, up_pair)
                    squares(down, 3 * l + 1 + half, 1)

            def split_at(p, n0, q):
                n = n0 + 2 * q
                i, w = n % SLOTS, width(n)
                if isinstance(p, int):
                    return split(n)
                turn = (n0 + 2 * q) // SLOTS + 1
                act.wait_ge(landed[i], 8 * (p - q) + 16 * turn)
                act.wait_ge(used, 2 * p + (n0 - 1))
                copy(w_hi[:, n % 2, 0:w], ring[:, i, 0:w]).then_inc(sem("w_hi"), 1)

            norm_split(0, in_hi, in_raw)
            mlp(0)
            stream_root(2)
            norm_split(1, b_hi, b_raw)
            for s in range(21):
                if 6 <= s - 1 < 12:
                    i = s - 7
                    act.wait_ge(sem("v_mm2"), i + 1)
                    copy(vtok[:, :, i * P:(i + 1) * P], bank[6 + i % 2][:, :].rearrange("p (r f) -> p r f", f=P))\
                        .then_inc(sem("v_ev"), 1)
                elif s:
                    head_root(unit(s - 1))
                if s < 20:
                    if 6 <= s < 12:
                        act.wait_ge(used, N_K + s + 1)
                        copy(y[:, s % 2, :], bank[s % 2][:, :]).then_inc(sem("pos_read"), 1)
                    else:
                        head_out(unit(s))
                    split(N_K + s + 2)
                if s == 11:
                    act.wait_ge(used, N_Q)
                    norm_split(2, b_hi, b_raw)

            def exps(r, s, first):
                act.wait_ge(sem("da_nb"), 4 * r + (s + 1))
                if not (first and s < 2):
                    act.wait_ge(sem("da_tr"), 4 * r + (s - 1))
                nc.scalar.activation(pr[:, s % 2, :], sm[:, s % 2, :], ACT.Exp, bias=stat[:, 18 + s % 2:19 + s % 2],
                                     scale=HD ** -0.5, accum_out=stat[:, 20 + s % 2:21 + s % 2]).then_inc(sem("da_exp"), 1)

            def output(r, s):
                act.wait_ge(sem("da_o"), 4 * r + (s + 1))
                hs = slice(HD * (s % 2), HD * (s % 2) + HD)
                copy(by_residue(y[:, s // 2, :])[hs, bass.ds(r, 1), :],
                     bank[6 + s // 2][hs, 0:P].unsqueeze(1)).then_inc(sem("da_y"), 1)

            def residue(r, first, last):
                for s in range(4):
                    if s < 3 or not last:
                        exps(r + (s + 1) // 4, (s + 1) % 4, first and s < 3)
                    act.wait_ge(sem("da_tr"), 4 * r + (s + 1))
                    if not (first and s < 2):
                        act.wait_ge(sem("da_o"), 4 * r + (s - 1))
                    copy(pT[:, s % 2, 0:T], bank[4][:, :])
                    copy(pT[:, s % 2, T:6 * P], bank[5][:, 0:2 * P]).then_inc(sem("da_pt"), 1)
                    if s:
                        output(r, s - 1)
                    elif not first:
                        output(r - 1, 3)

            exps(0, 0, True)
            four_rounds(act, residue)
            output(RES - 1, 3)
            memory_attention(1)
            act.wait_ge(sem("ma_y"), 4)
            for k in range(4):
                copy(in_hi[:, k, :], y[:, k, :]).then_inc(sem("in_hi"), 1)
            squares(N_OUTB, 3, 0.5)
            stream_root(3)
            norm_split(3, in_hi, in_raw)
            mlp(1)

        @block.vector
        def _(dve):
            V = nc.vector
            V.memset(epsb[:, 0:1], RMS_EPS).then_inc(sem("eps"), 1)
            V.memset(epsb[:, 1:2], LNX_EPS).then_inc(sem("eps"), 1)
            dve.wait_ge(sem("tables_in"), 32)
            V.tensor_scalar(derived[:, 0:PAIRS * NPAR], par[:, G_PAIR:G_END], -1.0, 1.0, ALU.mult, ALU.add)\
                .then_inc(sem("derived"), 1)
            V.tensor_scalar(derived[:, PAIRS * NPAR:PAIRS * NPAR + 2], par[:, MU_WA:MU_WA + 2], -1.0, 1.0, ALU.mult, ALU.add)\
                .then_inc(sem("derived"), 1)

            dve.wait_ge(sem("mem_sd"), 1)
            V.reciprocal(mem_rs, mem_rs).then_inc(sem("mem_rc"), 1)
            dve.wait_ge(sem("mem_rc"), 1)
            dve.wait_ge(sem("zeroed"), 2)

            def scaled(dst, src, gain, by, sig):
                return V.scalar_tensor_tensor(out=dst, in0=src, scalar=gain, in1=by, op0=ALU.mult, op1=ALU.mult)\
                    .then_inc(sem(sig), 1)

            def stream_rstd(e):
                dve.wait_ge(sem("x_sd"), e + 1)
                V.reciprocal(rstd[:, :], rstd[:, :]).then_inc(sem("x_rc"), 1)
                dve.wait_ge(sem("x_rc"), e + 1)

            def lower(dst, src, high, sig):
                V.tensor_tensor(dst, src, high.bitcast(F32), ALU.subtract).then_inc(sem(sig), 1)

            def input_low(hi, lo, src, k, at, sig):
                dve.wait_ge(sem("in_hi"), at + k + 1)
                lower(lo[:, k, :], src, hi[:, k, :], sig)

            def norm_split(q, gain, hi, lo, raw, at):
                for k in range(KD + 1):
                    if 2 <= k < KD:
                        dve.wait_ge(sem("h_ready"), KD * (q + 1) + k - 1)
                    if k < KD:
                        scaled(raw[:, k % 2, :], x[:, k, :], col(gain + k), rstd[:, :], "n_raw")
                    if k:
                        input_low(hi, lo, raw[:, (k - 1) % 2, :], k - 1, at, "h_ready")

            def split(n, like=None):
                if isinstance(n, int) and n >= N_END:
                    return
                like = n if like is None else like
                w = width(like)
                dve.wait_ge(sem("w_hi"), n - (N_OUTA - 1))
                lower(w_lo[:, like % 2, 0:w], ring[:, like % SLOTS, 0:w], w_hi[:, like % 2, 0:w], "w_lo")

            def stream_norm(dst, gain):
                for k in range(KD):
                    scaled(dst[:, k, :], x[:, k, :], col(gain + k), rstd[:, :], "h_ready")

            def head_norm(u, gain):
                raw, _, rs, n = heads_of(u)
                dve.wait_ge(sem("hn_sd"), u + 1)
                V.reciprocal(rs, rs).then_inc(sem("hn_rc"), 1)
                dve.wait_ge(sem("hn_rc"), u + 1)
                if u < U_QM0:
                    l, i = u // 2, u % 2
                    for hh in range(2):
                        hs = slice(HD * hh, HD * hh + HD)
                        q = V.scalar_tensor_tensor(out=mem_k[hs, l, i, hh, :], in0=raw[hs], scalar=par[hs, gain:gain + 1],
                                                   in1=rs[hs], op0=ALU.mult, op1=ALU.mult)
                    q.then_inc(sem("hn_done"), 1)
                    return
                dst = qm_a[:, u % 2, :] if u < U_K else hz[:, u % 2, :] if u < U_QM1 else qm_b[:, u % 2, :]
                scaled(dst, raw, col(gain), rs, "hn_done")

            for k in range(KD):
                scaled(memh[:, k, :], memx[:, k, :], col(G_MEM0 + k), mem_rs, "memh")
            stream_rstd(0)
            stream_norm(h, G_ATTN0)
            for i in range(2):
                head_norm(i, G_MK0)
            dve.wait_ge(sem("mv_mm"), 2)
            for k in range(KD):
                scaled(memh[:, k, :], memx[:, k, :], col(G_MEM1 + k), mem_rs, "memh")
            for i in range(2):
                head_norm(2 + i, G_MK1)

            def shifted(dst, src, mu, sig):
                V.scalar_tensor_tensor(out=dst[:, 1:T], in0=src[:, 0:T - 1], scalar=mu, in1=dst[:, 1:T],
                                       op0=ALU.mult, op1=ALU.add).then_inc(sem(sig), 1)

            for i, dst in enumerate((kx, rx)):
                dve.wait_ge(sem("own"), i + 1)
                shifted(dst, bank[4 + i], col(MU_WA + i), "shifted")
            for i in range(2):
                head_norm(U_QM0 + i, G_MQ0)

            def memory_attention(l):
                m = mem_attn[l]

                def softmax_bound(c):
                    g = 4 * l + c
                    for i in range(2):
                        dve.wait_ge(sem("ma_sc"), 2 * g + i + 1)
                        V.tensor_reduce(stat[:, 2 * i:2 * i + 2], bank[i][:, :].rearrange("p (h t) -> p h t", t=NMEM),
                                        AX.X, ALU.max).then_inc(sem("ma_mx"), 1)
                        dve.wait_ge(sem("ma_mx"), 2 * g + i + 1)
                        V.tensor_scalar(stat[:, 4 + 2 * i:6 + 2 * i], stat[:, 2 * i:2 * i + 2], -HD ** -0.5, None, ALU.mult)\
                            .then_inc(sem("ma_nb"), 1)

                def token_tile(c, first, last):
                    g = 4 * l + c
                    dve.wait_ge(sem("ma_exp"), 4 * g + 4)
                    V.reciprocal(stat[:, 12:16], stat[:, 8:12]).then_inc(sem("ma_rd"), 1)
                    dve.wait_ge(sem("ma_rd"), g + 1)
                    V.tensor_tensor(m["p"], m["p"], stat[:, 12:16].unsqueeze(2).to_broadcast([P, MEMH, NMEM]), ALU.mult)\
                        .then_inc(sem("ma_pn"), 1)
                    if not last:
                        softmax_bound(c + 1)

                softmax_bound(0)
                four_rounds(dve, token_tile)

            memory_attention(0)

            def halves():
                return (slice(0, HD), 0), (slice(HD, P), 1)

            def state(j, c):
                if c:
                    dve.wait_ge(sem("s_up"), 3 * j + c)
                    V.tensor_scalar(Sf, S, fS[:, c:c + 1], None, ALU.mult).then_inc(sem("sf"), 1)
                dve.wait_ge(sem("st_mm"), 3 * j + c + 1)
                dve.wait_ge(sem("fs"), j + 1)
                if c:
                    dve.wait_ge(sem("sf"), 2 * j + c)
                for hs, hh in halves():
                    cs = slice(HD * hh, HD * hh + HD)
                    if c == 0:
                        q = V.tensor_scalar(S[hs, cs], bank[5][hs, cs], fS[hs, 0:1], None, ALU.mult)
                    else:
                        q = V.scalar_tensor_tensor(out=S[hs, cs], in0=bank[5][hs, cs], scalar=fS[hs, c:c + 1],
                                                   in1=Sf[hs, cs], op0=ALU.mult, op1=ALU.add)
                q.then_inc(sem("s_up"), 1)

            def centre(j):
                dve.wait_ge(sem("mean_mm"), j + 1)
                V.scalar_tensor_tensor(out=ysb, in0=bank[6][:, :], scalar=-1.0 / HD, in1=ysb, op0=ALU.mult, op1=ALU.add)\
                    .then_inc(sem("yc"), 1)

            def normalise(j):
                dve.wait_ge(sem("y_sd"), j + 1)
                V.reciprocal(sc2, sc2).then_inc(sem("y_rc"), 1)
                dve.wait_ge(sem("y_rc"), j + 1)
                V.tensor_tensor(ysb, ysb, sc2, ALU.mult).then_inc(sem("yn"), 1)

            def finish(j):
                dve.wait_ge(sem("y_ln"), j + 1)
                V.tensor_tensor(ysb, ysb, bonus, ALU.add).then_inc(sem("y_b"), 1)
                dve.wait_ge(sem("y_b"), j + 1)
                V.tensor_tensor(y[:, bass.ds(j, 1), :], ysb.unsqueeze(1), gate.unsqueeze(1), ALU.mult)\
                    .then_inc(sem("y_out"), 1)

            def pair(j, first):
                dve.wait_ge(sem("w_sig"), j + 1)
                V.tensor_tensor_scan(flat(lw), reset, flat(lw), 0.0, ALU.mult, ALU.add).then_inc(sem("cum"), 1)
                dve.wait_ge(sem("cum"), j + 1)
                V.tensor_tensor(cc, lw, lw[:, :, CHUNK // 2:CHUNK // 2 + 1].to_broadcast([P, NCH, PAD]), ALU.subtract)\
                    .then_inc(sem("cc"), 1)
                if not first:
                    state(j - 1, 0)
                dve.wait_ge(sem("own"), 3 * j + 3)
                shifted(kx, bank[0], pcol(j, MUK), "shifted")
                if not first:
                    state(j - 1, 1)
                dve.wait_ge(sem("fa"), j + 1)
                dve.wait_ge(sem("kkr"), j + 1)
                dve.wait_ge(sem("shifted"), 3 * j + 3)
                V.tensor_tensor(kx, kx, fa, ALU.mult).then_inc(sem("k2"), 1)
                dve.wait_ge(sem("own"), 3 * j + 4)
                shifted(rx, bank[1], pcol(j, MUR), "shifted")
                if not first:
                    state(j - 1, 2)
                dve.wait_ge(sem("shifted"), 3 * j + 4)
                dve.wait_ge(sem("k2"), j + 1)
                V.scalar_tensor_tensor(out=rrk, in0=rx, scalar=pcol(j, RKP), in1=kx, op0=ALU.mult, op1=ALU.mult)\
                    .then_inc(sem("rk"), 1)
                dve.wait_ge(sem("e_neg"), j + 1)
                V.tensor_tensor(Kf, kx.rearrange("p (c t) -> p c t", t=P), e_neg[:, :, 1:], ALU.mult).then_inc(sem("kf"), 1)
                dve.wait_ge(sem("kk_sd"), j + 1)
                V.tensor_scalar(sc2, sc2, 1e-12, None, ALU.max).then_inc(sem("kk_mx"), 1)
                dve.wait_ge(sem("kk_mx"), j + 1)
                V.reciprocal(sc2, sc2).then_inc(sem("kk_rc"), 1)
                dve.wait_ge(sem("kk_rc"), j + 1)
                V.tensor_tensor(kk, kkr, sc2, ALU.mult).then_inc(sem("kk_n"), 1)
                dve.wait_ge(sem("own"), 3 * j + 5)
                shifted(vx, bank[1], pcol(j, MUV), "shifted")
                dve.wait_ge(sem("bb"), j + 1)
                V.tensor_tensor(Bf, bb.rearrange("p (c t) -> p c t", t=P), e_neg[:, :, 1:], ALU.mult).then_inc(sem("bf"), 1)
                if not first:
                    dve.wait_ge(sem("y_mm"), NCH * j)
                    centre(j - 1)
                dve.wait_ge(sem("shifted"), 3 * j + 4)
                for hs, hh in halves():
                    V.scalar_tensor_tensor(out=AR[hs, :, 2 * hh, :], in0=kk[hs].rearrange("p (c t) -> p c t", t=P),
                                           scalar=-1.0, in1=e_pos[hs, :, 0:CHUNK], op0=ALU.mult, op1=ALU.mult)
                    q = V.tensor_tensor(AR[hs, :, 2 * hh + 1, :], rx[hs].rearrange("p (c t) -> p c t", t=P),
                                        e_pos[hs, :, 1:], ALU.mult)
                q.then_inc(sem("ar"), 1)
                tri2 = tri.unsqueeze(1).to_broadcast([P, 2, 2 * P])
                for c in range(NCH):
                    for G, b, n in ((KG, 2, "kg"), (BG, 3, "bg")):
                        dve.wait_ge(sem(n + "_mm"), NCH * j + c + 1)
                        V.tensor_tensor(flat(G[:, c, :, :]).rearrange("p (h w) -> p h w", w=2 * P),
                                        bank[b][:, :].rearrange("p (h w) -> p h w", w=2 * P), tri2, ALU.mult)\
                            .then_inc(sem(n + "_ev"), 1)
                    dve.wait_ge(sem("m_mm"), NCH * j + c + 1)
                    V.tensor_tensor(X[:, :, c, :], bank[4][:, 0:2 * P].rearrange("p (h t) -> p h t", t=P),
                                    level(LEVELS + 1).unsqueeze(1).to_broadcast([P, 2, P]), ALU.mult).then_inc(sem("x_l1"), 1)
                    dve.wait_ge(sem("x_l1"), NCH * j + c + 1)
                    q = V.tensor_tensor(X[:, :, c, :], X[:, :, c, :], ident.unsqueeze(1).to_broadcast([P, 2, P]), ALU.add)
                q.then_inc(sem("x_one"), 1)
                if not first:
                    normalise(j - 1)
                for v in range(LEVELS):
                    for hh in range(2):
                        for odd in range(v == LEVELS - 1, 2):
                            n = ADDS * j + (4 * v + hh + 1 if v == LEVELS - 1 else 4 * v + 2 * hh + odd + 1)
                            dve.wait_ge(sem("dx_mm"), n)
                            xf = blocks(flat((X, XT)[odd][:, hh, :, :]), v, odd)
                            V.tensor_tensor(xf, bank[4 + 2 * hh + odd][:, 0:NCH * HP].rearrange("p (n b) -> p n b", b=2 << v),
                                            xf, ALU.add).then_inc(sem("dx_add"), 1)
                    if v == 0:
                        if not first:
                            finish(j - 1)
                        dve.wait_ge(sem("bonus_mm"), j + 1)
                        V.tensor_tensor(bonus, bank[1][:, :], vx, ALU.mult).then_inc(sem("bonus"), 1)

            dve.wait_ge(sem("rw_zero"), 1)
            rounds(dve, PAIRS, pair)
            for c in range(NCH - 1):
                state(PAIRS - 1, c)
            centre(PAIRS - 1)
            normalise(PAIRS - 1)
            finish(PAIRS - 1)

            def residual(n0, e, b0, slots):
                for m in range(KD):
                    if slots == 1 or m % 2 == 1:
                        split(n0 + int(slots * (m + 1)) + 1)
                    if slots < 1 and m % 2 == 0:
                        dve.wait_ge(sem("out_half"), m // 2 + 1)
                    else:
                        dve.wait_ge(used, n0 + int(slots * (m + 1)))
                    if e:
                        dve.wait_ge(sem("x_up"), KD * (e - 1) + m + 1)
                    V.tensor_tensor(x[:, m, :], bank[b0 + m % 2][:, :], x[:, m, :], ALU.add).then_inc(sem("x_up"), 1)

            for n in range(N_OUTA, N_OUTA + 2):
                split(n)
            for k in range(KD):
                input_low(in_hi, in_lo, y[:, k, :], k, 0, "y_split")
            residual(N_OUTA, 0, 0, 1)
            stream_rstd(1)
            norm_split(0, G_FFN0, in_hi, in_lo, in_raw, KD)

            def tap(l, tile, k):
                return par[:, bass.ds(4 * tile + (G_CONV + l * 2 * FT * 4 + k), 1)]

            def mlp(l, in_at):
                for half in range(2):
                    up, down = mlp_tiles(l, half)
                    g0 = FT * l + HALF * half

                    def up_pair(p, q):
                        b = (g0 + q) % 2
                        for s in range(2):
                            c = conv[:, 2 * b + s, :]
                            split(2 * p + (up + 2 + s), up + 2 + s + 2 * q)
                            for lag in (1, 2):
                                if lag == 1:
                                    dve.wait_ge(sem("conv_own"), 2 * p + (2 * g0 + s + 1))
                                else:
                                    dve.wait_ge(sem("conv_one"), 2 * p + (2 * g0 + s + 1))
                                V.scalar_tensor_tensor(out=c[:, lag:T], in0=bank[2 * b + s][:, 0:T - lag],
                                                       scalar=tap(l, 2 * p + (2 * HALF * half + s), 2 - lag), in1=c[:, lag:T],
                                                       op0=ALU.mult, op1=ALU.add)\
                                    .then_inc(sem("conv_one" if lag == 1 else ("conv_gate", "conv_done")[s]), 1)
                        dve.wait_ge(sem("z_hi"), p + (g0 + 1))
                        lower(z_lo[:, bass.ds(p, 1), :], z_raw[:, b, :].unsqueeze(1), z_hi[:, bass.ds(p, 1), :], "z")

                    mlp_pairs(dve, up_pair)
                    residual(down, 3 * l + 1 + half, 4, 1)

            mlp(0, 2 * KD)
            stream_rstd(2)
            dve.wait_ge(sem("x_up"), 3 * KD)
            norm_split(1, G_KV, b_hi, b_lo, b_raw, 2 * KD)

            def turn(u):
                v = u - U_K
                dve.wait_ge(sem("rope_mm"), v + 1)
                dve.wait_ge(sem("rope_in"), 16)
                rz = heads_of(u)[2]
                V.tensor_tensor(rz, bank[4 + u % 2][:, :], sinT, ALU.mult).then_inc(sem("rope_sin"), 1)
                dve.wait_ge(sem("rope_sin"), v + 1)
                dve.wait_ge(sem("rope_cos"), v + 1)
                if u < U_Q:
                    for hs, hh in halves():
                        q = V.tensor_tensor(kp[hs, 2 * v + hh, :].rearrange("p (r u) -> p r u", r=RES),
                                            by_residue(t1[hs, u % 2, :]), by_residue(rz[hs]), ALU.add)
                else:
                    q = V.tensor_tensor(qT[:, v - 6, :].rearrange("p (r u) -> p r u", r=RES),
                                        by_residue(t1[:, u % 2, :]), by_residue(rz), ALU.add)
                q.then_inc(sem("rope_done"), 1)

            dve.wait_ge(sem("kp_zero"), 1)
            for s in range(22):
                if 0 <= s - 2 < 18 and not 6 <= s - 2 < 12:
                    turn(unit(s - 2))
                if 0 <= s - 1 < 20 and not 6 <= s - 1 < 12:
                    u = unit(s - 1)
                    head_norm(u, G_KN if u < U_Q else G_QN if u < U_QM1 else G_MQ1)
                if s == 11:
                    norm_split(2, G_ATTN1, b_hi, b_lo, b_raw, 3 * KD)

            def softmax_bound(r, s, first):
                g, b = 4 * r + s, s % 2
                dve.wait_ge(sem("da_sc"), g + 1)
                if not (first and s < 2):
                    dve.wait_ge(sem("da_exp"), g - 1)
                V.tensor_tensor(sm[:, b, 0:T].unsqueeze(1), bank[2 * b][:, :].unsqueeze(1), mask0[:, bass.ds(r, 1), :], ALU.add)
                V.tensor_tensor(sm[:, b, T:6 * P], bank[2 * b + 1][:, 0:2 * P], mask12[:, :], ALU.add).then_inc(sem("da_sm"), 1)
                dve.wait_ge(sem("da_sm"), g + 1)
                V.tensor_reduce(stat[:, 16 + b:17 + b], sm[:, b, :], AX.X, ALU.max).then_inc(sem("da_mx"), 1)
                dve.wait_ge(sem("da_mx"), g + 1)
                V.tensor_scalar(stat[:, 18 + b:19 + b], stat[:, 16 + b:17 + b], -HD ** -0.5, None, ALU.mult)\
                    .then_inc(sem("da_nb"), 1)

            def residue(r, first, last):
                for s in range(4):
                    if s < 3 or not last:
                        softmax_bound(r + (s + 1) // 4, (s + 1) % 4, first and s < 3)
                    g, b = 4 * r + s, s % 2
                    dve.wait_ge(sem("da_exp"), g + 1)
                    V.reciprocal(stat[:, 22 + b:23 + b], stat[:, 20 + b:21 + b]).then_inc(sem("da_rd"), 1)
                    dve.wait_ge(sem("da_rd"), g + 1)
                    V.tensor_scalar(pr[:, b, :], pr[:, b, :], stat[:, 22 + b:23 + b], None, ALU.mult).then_inc(sem("da_pn"), 1)

            dve.wait_ge(sem("mask_in"), 32)
            softmax_bound(0, 0, True)
            four_rounds(dve, residue)
            dve.wait_ge(sem("w_lo"), N_OUTB + 2 - N_OUTA)
            memory_attention(1)
            for k in range(4):
                input_low(in_hi, in_lo, y[:, k, :], k, 4 * KD, "y_split")
            residual(N_OUTB, 3, 0, 0.5)
            stream_rstd(3)
            norm_split(3, G_FFN1, in_hi, in_lo, in_raw, 4 * KD + 4)
            mlp(1, 0)

        @block.gpsimd
        def _(pool):
            G = nc.gpsimd

            G.memset(mem_k[:, :, :, :, :], 0.0).then_inc(sem("zeroed"), 1)
            G.memset(arena[:, 0:2 * T], 0.0).then_inc(sem("zeroed"), 1)

            def memory_attention(l):
                m = mem_attn[l]

                def token_tile(c, first):
                    g = 4 * l + c
                    if not first:
                        pool.wait_ge(sem("ma_sc"), 2 * g)
                    G.tensor_copy(m["qs"], m["q"][:, :, bass.ds(c * P, P)]).then_inc(sem("ma_qs"), 1)

                pool.wait_ge(sem("hn_done"), (U_K, U_END)[l])
                rounds(pool, RES, token_tile)

            memory_attention(0)
            pool.wait_ge(sem("ma_y"), 2)
            G.memset(flat(lw)[:, 0:NCH * PAD:PAD], 0.0)
            G.memset(AR, 0.0)
            G.memset(Vp, 0.0)
            G.memset(SAp, 0.0)
            G.memset(S, 0.0).then_inc(sem("rw_zero"), 1)

            def pair(j, first):
                pool.wait_ge(sem("kk_n"), j + 1)
                G.tensor_tensor(bb, kk, aa, ALU.mult).then_inc(sem("bb"), 1)
                pool.wait_ge(sem("e_neg"), j + 1)
                if not first:
                    pool.wait_ge(sem("s_up"), 3 * j)
                G.tensor_tensor(fS[:, 0:NCH - 1].unsqueeze(2), e_pos[:, 0:NCH - 1, CHUNK:PAD], e_neg[:, 1:NCH, 0:1], ALU.mult)\
                    .then_inc(sem("fs"), 1)
                for c in range(NCH):
                    pool.wait_ge(sem("bg_ev"), NCH * j + c + 1)
                    b = BG[:, c, 0:4:2, :]
                    G.tensor_tensor(XT[:, :, c, :], b, both(level(0)), ALU.mult).then_inc(sem("xt_l1"), 1)
                    q = G.tensor_tensor(CT[:, :, c, :], b, both(level(1)), ALU.mult)
                    if c == NCH - 1:
                        q.then_inc(sem("ct"), 1)
                    pool.wait_ge(sem("xt_l1"), NCH * j + c + 1)
                    q = G.tensor_tensor(XT[:, :, c, :], XT[:, :, c, :], both(ident), ALU.add)
                q.then_inc(sem("xt_one"), 1)
                for v in range(1, LEVELS):
                    for hh in range(2):
                        pool.wait_ge(sem("y1_mm"), 2 * LEVELS * j + (2 * (v - 1) + hh + 1))
                        G.tensor_tensor(CT[:, hh, :, :], BG[:, :, 2 * hh, :],
                                        level(v + 1).unsqueeze(1).to_broadcast([P, NCH, P]), ALU.mult).then_inc(sem("ct"), 1)

            def both(a):
                return a.unsqueeze(1).to_broadcast([P, 2, P])

            rounds(pool, PAIRS, pair)

            def sum_squares(q):
                for m in range(1, KD - 1):
                    pool.wait_ge(sem("xsq"), KD * (q + 1) + m + 1)
                    if m > 1:
                        pool.wait_ge(sem("sq_sum"), (KD - 2) * q + m - 1)
                    G.tensor_tensor(y[:, 0, :], y[:, 0, :], y[:, m, :], ALU.add).then_inc(sem("sq_sum"), 1)

            def mlp(l):
                for half in range(2):
                    g0 = FT * l + HALF * half

                    def up_pair(p, q):
                        b = (g0 + q) % 2
                        pool.wait_ge(sem("silu"), p + (g0 + 1))
                        pool.wait_ge(sem("conv_done"), p + (g0 + 1))
                        if not isinstance(p, int) or g0 + p >= 2:
                            pool.wait_ge(sem("z"), p + (g0 - 1))
                        G.tensor_tensor(z_raw[:, b, :], silu[:, b, :], conv[:, 2 * b + 1, :], ALU.mult).then_inc(sem("z_raw"), 1)

                    mlp_pairs(pool, up_pair)

            sum_squares(0)
            mlp(0)
            sum_squares(1)
            pool.wait_ge(sem("x_up"), 3 * KD)
            G.memset(kp[:, :, :], 0.0).then_inc(sem("kp_zero"), 1)
            pool.wait_ge(sem("w_lo"), N_K + 2 - N_OUTA)
            for s in range(21):
                if s < 20:
                    n = N_K + s + 2
                    w = width(n)
                    pool.wait_ge(sem("w_hi"), n - (N_OUTA - 1))
                    G.tensor_tensor(w_lo[:, n % 2, 0:w], ring[:, n % SLOTS, 0:w], w_hi[:, n % 2, 0:w].bitcast(F32),
                                    ALU.subtract).then_inc(sem("w_lo"), 1)
                if s and unit(s - 1) < U_QM1 and not 6 <= s - 1 < 12:
                    u = unit(s - 1)
                    pool.wait_ge(sem("rope_in"), 16)
                    pool.wait_ge(sem("hn_done"), u + 1)
                    if u >= U_K + 2:
                        pool.wait_ge(sem("rope_done"), u - U_K - 1)
                    G.tensor_tensor(t1[:, u % 2, :], hz[:, u % 2, :], cosT, ALU.mult).then_inc(sem("rope_cos"), 1)

            def queries(r):
                G.tensor_copy(qS[:, :, :], qT[:, :, bass.ds(r * P, P)]).then_inc(sem("da_stage"), 1)

            def values(r):
                G.tensor_copy(vS[:, :].unsqueeze(1), vtok[:, bass.ds(r, 1), 2 * P:6 * P]).then_inc(sem("da_vstage"), 1)

            def residue(r, first):
                if not first:
                    pool.wait_ge(sem("da_o"), 4 * r)
                    values(r)
                pool.wait_ge(sem("da_sc"), 4 * r + 4)
                queries(r + 1)

            pool.wait_ge(used, N_OUTB)
            pool.wait_ge(sem("v_ev"), 6)
            pool.wait_ge(sem("rope_done"), 12)
            queries(0)
            values(0)
            rounds(pool, RES - 1, residue)
            pool.wait_ge(sem("da_o"), 4 * (RES - 1))
            values(RES - 1)
            pool.wait_ge(sem("da_y"), 4 * RES)
            memory_attention(1)
            sum_squares(2)
            mlp(1)


def shape_constants():
    i = np.arange(P)
    cst = np.zeros((P, C_END), np.float32)
    cst[:, C_ID:C_ID + P] = np.eye(P)
    cst[:, C_ONE:C_ONE + P] = 1
    cst[:, C_BLK:C_BLK + P] = i[:, None] // HD == i[None] // HD
    half = HD // 2
    turn = np.zeros((P, P), np.float32)
    for m in range(P):
        if m % HD < half:
            turn[m + half, m] = -1
        else:
            turn[m - half, m] = 1
    cst[:, C_ROT:C_ROT + P] = turn
    s, t = i[:, None], i[None]
    cst[:, C_TRI:C_TRI + P] = s < t
    cst[:, C_TRI + P:C_TRI + 2 * P] = s <= t
    for v in range(LEVELS + 1):
        b = 1 << v
        cst[:, C_LEV + v * P:C_LEV + (v + 1) * P] = (s // b + 1 == t // b) & (t // b % 2 == 1)
    cst[:, C_LEV + (LEVELS + 1) * P:C_RESET] = cst[:, C_LEV:C_LEV + P].T
    cst[:, C_RESET:C_END] = np.tile((np.arange(PAD) > 0).astype(np.float32), NCH)
    inv = (10000.0 ** (-np.arange(0, HD, 2, dtype=np.float32) / np.float32(HD))).astype(np.float32)
    ang = np.arange(T, dtype=np.float32)[:, None] * inv[None, :]
    rope = np.stack([np.tile(f(ang).T, (4, 1)) for f in (np.cos, np.sin)], axis=1).astype(np.float32)
    tok = np.arange(T).reshape(P, RES).T
    keys = tok.reshape(-1)
    masks = np.zeros((P, RES * T + 2 * P), np.float32)
    for r in range(RES):
        dist = tok[r][:, None] - keys[None]
        masks[:, r * T:(r + 1) * T] = np.where((dist >= 0) & (dist <= 128), 0, -1e30)
    d = i[:, None] - i[None]
    masks[:, RES * T:RES * T + P] = np.where(d >= 0, 0, -1e30)
    masks[:, RES * T + P:] = np.where((d >= 0) & (d % 4 == 0), 0, -1e30)
    return cst, rope, masks


def tiles_of(w):
    k, n = w.shape
    return w.reshape(k // P, P, n // P, P).transpose(2, 1, 0, 3).reshape(n // P, P, k)


def columns(v):
    return v.reshape(-1, P).T


def kernel(**inputs):
    import concourse.bacc as _bacc
    from concourse.bass_utils import run_bass_kernel_spmd as _run

    a = {k: np.asarray(v) for k, v in inputs.items()}
    f32 = np.float32
    cst, rope, masks = shape_constants()
    W = PAIRS * P

    w_in = tiles_of(a["a_w_in"][0])
    w_pairs = np.stack([np.stack([w_in[6 + j], w_in[j], w_in[12 + j]]) for j in range(PAIRS)])
    w_small = np.zeros((PAIRS, P, 2 * P), f32)
    for j in range(PAIRS):
        js = slice(j * P, (j + 1) * P)
        w_small[j, 0:HD, 0:P] = a["a_w2"][0][:, js]
        w_small[j, HD:P, 0:P] = a["a_a2"][0][:, js]
        w_small[j, :, P:2 * P] = a["a_g2"][0][:, js]

    w_ring = np.zeros((N_END, P, SLOTW), f32)
    w_ring[N_LORA:N_LORA + 2, :, 0:TILEW] = w_in[18:20]
    w_ring[N_QM0:N_QM0 + 2, :, 0:TILEW] = w_in[20:22]
    w_ring[N_OUTA:N_OUTA + KD, :, 0:TILEW] = tiles_of(a["a_w_out"][0])
    kv = tiles_of(a["kv_w"])
    w_ring[N_K:N_K + 6, :, 0:TILEW] = kv[0:6]
    w_ring[N_V:N_V + 6, :, 0:TILEW] = kv[6:12]
    b_in = tiles_of(a["b_w_in"][0])
    w_ring[N_Q:N_Q + 8, :, 0:TILEW] = b_in
    out_b = tiles_of(a["b_w_out"][0])
    w_ring[N_OUTB:N_OUTB + 4, :, 0:TILEW] = out_b.reshape(4, 2, P, 4 * P).transpose(0, 2, 1, 3).reshape(4, P, TILEW)
    for l in range(2):
        u = tiles_of(a["ffn_w_up"][l])
        dn = tiles_of(a["ffn_w_down"][l])
        for half in range(2):
            up, down = mlp_tiles(l, half)
            hs = slice(HALF * half, HALF * (half + 1))
            w_ring[up:down:2, :, 0:TILEW] = u[0:FT][hs]
            w_ring[up + 1:down:2, :, 0:TILEW] = u[FT:2 * FT][hs]
            w_ring[down:down + KD] = dn[:, :, SLOTW * half:SLOTW * (half + 1)]
    w_mem = np.ascontiguousarray(a["mem_w_kv"].reshape(2, KD, P, 2 * MEMH * HD).transpose(0, 2, 1, 3))

    par = np.zeros((P, G_END), f32)
    for l in range(2):
        par[:, (G_ATTN0, G_ATTN1)[l]:][:, 0:KD] = columns(a["attn_norm"][l])
        par[:, (G_FFN0, G_FFN1)[l]:][:, 0:KD] = columns(a["ffn_norm"][l])
        par[:, (G_MEM0, G_MEM1)[l]:][:, 0:KD] = columns(a["mem_norm"][l])
        par[:, (G_MQ0, G_MQ1)[l]] = np.tile(a["mem_q_norm"][l], 2)
        par[:, (G_MK0, G_MK1)[l]] = np.tile(a["mem_k_norm"][l], 2)
        taps = np.concatenate([a["ffn_conv_w"][l], a["ffn_conv_b"][l][None]])
        taps = taps.reshape(4, 2, FT, P).transpose(3, 2, 1, 0)
        par[:, G_CONV + l * 2 * FT * 4:][:, 0:2 * FT * 4] = taps.reshape(P, -1)
    par[:, G_KV:G_KV + KD] = columns(a["kv_norm"])
    par[:, G_KN] = np.tile(a["kv_k_norm"], 2)
    par[:, G_QN] = np.tile(a["b_q_norm"][0], 2)
    mu = a["a_mu"][0]
    par[:, MU_WA] = mu[3 * W:3 * W + P]
    par[:, MU_G] = mu[3 * W + P:3 * W + 2 * P]
    per_pair = (mu[W:2 * W], mu[0:W], mu[2 * W:3 * W], a["a_w0"][0], a["a_a0"][0], a["a_k_k"][0], a["a_k_a"][0],
                a["a_r_k"][0].reshape(-1), a["a_lnx_w"][0], a["a_lnx_b"][0])
    par[:, G_PAIR:G_END] = np.stack([columns(v) for v in per_pair], axis=2).reshape(P, -1)

    arrays = {
        "xT": np.ascontiguousarray(a["x"][0].T.reshape(KD, P, T).transpose(1, 0, 2)),
        "memT": np.ascontiguousarray(a["mem"][0].T.reshape(KD, P, NMEM).transpose(1, 0, 2)),
        "consts": cst, "params": par, "ropes": rope, "masks": masks, "w_small": w_small, "w_mem": w_mem,
        "w_pairs": w_pairs, "w_ring": w_ring,
    }
    nc = _bacc.Bacc("TRN2", target_bir_lowering=False, num_devices=1)
    args = [nc.dram_tensor(k, v.shape, mybir.dt.from_np(v.dtype), kind="ExternalInput").ap() for k, v in arrays.items()]
    args.append(nc.dram_tensor("outT", [KD, P, T], F32, kind="ExternalOutput").ap())
    trunk(nc, *args)
    r = _run(nc, [arrays], core_ids=[0])
    return np.ascontiguousarray(r.results[0]["outT"].reshape(D, T).T).reshape(1, T, D)
```

```python
from contextlib import ExitStack

import numpy as np

import concourse.bass as bass
from concourse import mybir

F32 = mybir.dt.float32
F32R = mybir.dt.float32r
ALU = mybir.AluOpType
ACT = mybir.ActivationFunctionType
AX = mybir.AxisListType

P = 128
HP = P // 2
T = 512
D = 1024
KD = D // P
HD = 64
NMEM = 256
MEMH = 4
PAIRS = 6
CHUNK = 128
NCH = T // CHUNK
PAD = CHUNK + 1
LEVELS = 6
ADDS = 4 * LEVELS - 2
MASKS = NCH + 2 * (LEVELS - 1)
FF = 2816
FT = FF // P
RES = 4
SLOTS = 4
SLOTW = FT // 2 * P
TILEW = KD * P
LNX_EPS = 64e-5
RMS_EPS = 1e-6
DECAY = -float(np.exp(-0.5))
KRV_BANKS = 2, 3, 1
NPAR = 10
MUK, MUR, MUV, PW0, PA0, KKP, KAP, RKP, LNW, LNB = range(NPAR)
N_LORA, N_QM0, N_OUTA, N_MLP0, N_K, N_V, N_Q, N_QM1, N_OUTB, N_MLP1, N_END = 0, 2, 4, 12, 72, 78, 84, 90, 92, 96, 156
N_SPLIT = N_OUTA + SLOTS
QW = TILEW // 4
QSLOTS = 3
Q0 = 4 * N_OUTA
HALF = FT // 2
UPS = 2 * HALF
U_MK0, U_QM0, U_MK1, U_K, U_Q, U_QM1, U_END = 0, 2, 4, 6, 12, 18, 20
C_ID, C_ONE, C_BLK, C_ROT, C_TRI, C_LEV = 0, 128, 256, 384, 512, 768
C_RESET = C_LEV + (LEVELS + 2) * P
C_END = C_RESET + NCH * PAD
G_ATTN0, G_ATTN1, G_KV, G_FFN0, G_FFN1, G_MEM0, G_MEM1 = range(0, 56, 8)
G_KN, G_QN, G_MQ0, G_MQ1, G_MK0, G_MK1, MU_WA, MU_G = range(56, 64)
G_CONV = 64
G_PAIR = G_CONV + 2 * 2 * FT * 4
G_END = G_PAIR + PAIRS * NPAR
ARENA = 26320


def memory_key(u):
    return u < U_QM0 or U_MK1 <= u < U_K


def mlp_tiles(l, half):
    n = (N_MLP0, N_MLP1)[l] + half * (UPS + KD)
    return n, n + UPS


def width(n):
    down = any(mlp_tiles(l, f)[1] <= n < mlp_tiles(l, f)[1] + KD for l in range(2) for f in range(2))
    return SLOTW if down else TILEW


def mlp_pairs(eng, step):
    step(0, 0)
    with eng.Fori(0, (HALF - 3) // 2) as i:
        step(2 * i + 1, 1)
        step(2 * i + 2, 2)
    for p in range(HALF - 2, HALF):
        step(p, p)


def rounds(eng, n, body):
    body(0, True)
    with eng.Fori(1, n) as i:
        body(i, False)


def four_rounds(eng, body):
    body(0, True, False)
    with eng.Fori(1, RES - 1) as r:
        body(r, False, False)
    body(RES - 1, False, True)


def trunk(nc, xT, memT, consts, params, ropes, masks, w_small, w_mem, w_pairs, w_ring, outT):
    ctx = ExitStack()
    with ctx:
        def sb(name, shape):
            return ctx.enter_context(nc.sbuf_tensor(name, shape, F32))

        made = {}

        def sem(name):
            if name not in made:
                made[name] = ctx.enter_context(nc.semaphore(name))
            return made[name]

        y = sb("y", [P, KD, T])
        ring = sb("ring", [P, SLOTS, SLOTW])
        cst = sb("cst", [P, C_END])
        par = sb("par", [P, G_END])
        derived = sb("derived", [P, PAIRS * NPAR + 2])
        rstd = sb("rstd", [P, T])
        mem_k = sb("mem_k", [P, 2, 2, 2, NMEM])
        mem_v = sb("mem_v", [P, 2, 2, MEMH * HD])
        stat = sb("stat", [P, 32])
        epsb = sb("epsb", [P, 2])

        def tensor(group, name, shape, dt=F32):
            return group.enter_context(nc.sbuf_tensor(name, shape, dt))

        with ExitStack() as start:
            x0 = tensor(start, "x0", [P, KD, T])
        with ExitStack() as rwkv_layer:
            h_lo = tensor(rwkv_layer, "h_lo", [P, KD, T], F32R)
            h_hi = tensor(rwkv_layer, "h_hi", [P, KD, T], F32R)
            q_hi = tensor(rwkv_layer, "q_hi", [P, QSLOTS, QW], F32R)
            q_lo = tensor(rwkv_layer, "q_lo", [P, QSLOTS, QW], F32R)
            arena = tensor(rwkv_layer, "arena", [P, ARENA])
        x = tensor(ctx, "x", [P, KD, T])
        w_hi = tensor(ctx, "w_hi", [P, 2, SLOTW], F32R)
        w_lo = tensor(ctx, "w_lo", [P, 2, SLOTW], F32R)
        with ExitStack() as mlp_layer:
            in_hi = tensor(mlp_layer, "in_hi", [P, KD, T], F32R)
            in_lo = tensor(mlp_layer, "in_lo", [P, KD, T], F32R)
            in_raw = tensor(mlp_layer, "in_raw", [P, 2, T])
            z_hi = tensor(mlp_layer, "z_hi", [P, HALF, T], F32R)
            z_lo = tensor(mlp_layer, "z_lo", [P, HALF, T], F32R)
            z_raw = tensor(mlp_layer, "z_raw", [P, 2, T])
            conv = tensor(mlp_layer, "conv", [P, 4, T])
            silu = tensor(mlp_layer, "silu", [P, 2, T])
        with ExitStack() as dilated_layer:
            kp = tensor(dilated_layer, "kp", [P, 12, T])
            qT = tensor(dilated_layer, "qT", [P, 6, T])
            vtok = tensor(dilated_layer, "vtok", [P, RES, 6 * P])
            qm_b = tensor(dilated_layer, "qm_b", [P, 2, T])
            with ExitStack() as projections:
                rope = tensor(projections, "rope", [P, 2, T])
                b_hi = tensor(projections, "b_hi", [P, KD, T], F32R)
                b_lo = tensor(projections, "b_lo", [P, KD, T], F32R)
                b_raw = tensor(projections, "b_raw", [P, 2, T])
                hz = tensor(projections, "hz", [P, 2, T])
                t1 = tensor(projections, "t1", [P, 2, T])
            with ExitStack() as attention:
                mask0 = tensor(attention, "mask0", [P, RES, T])
                mask12 = tensor(attention, "mask12", [P, 2 * P])
                qS = tensor(attention, "qS", [P, 6, P])
                vS = tensor(attention, "vS", [P, T])
                sm = tensor(attention, "sm", [P, 2, 6 * P])
                pr = tensor(attention, "pr", [P, 2, 6 * P])
                pT = tensor(attention, "pT", [P, 2, 6 * P])
            with ExitStack() as memory:
                qs_b = tensor(memory, "qs_b", [P, 2, P])
                pm_b = tensor(memory, "pm_b", [P, MEMH, NMEM])
                pt_b = tensor(memory, "pt_b", [P, 2, MEMH, T])
        cosT, sinT = rope[:, 0, :], rope[:, 1, :]

        ident = cst[:, C_ID:C_ID + P]
        ones = cst[:, C_ONE:C_ONE + P]
        blk = cst[:, C_BLK:C_BLK + P]
        rot = cst[:, C_ROT:C_ROT + P]
        tri = cst[:, C_TRI:C_TRI + 2 * P]
        reset = cst[:, C_RESET:C_RESET + NCH * PAD]
        rms_eps, lnx_eps = epsb[:, 0:1], epsb[:, 1:2]

        def level(v):
            return cst[:, C_LEV + v * P:C_LEV + (v + 1) * P]

        def col(i):
            return par[:, i:i + 1]

        def pcol(j, k):
            return par[:, bass.ds(NPAR * j + (G_PAIR + k), 1)]

        def dcol(j, k):
            return derived[:, bass.ds(NPAR * j + k, 1)]

        at = [0]

        def part(*shape):
            n = int(np.prod(shape))
            a = arena[:, at[0]:at[0] + n]
            at[0] += n
            assert at[0] <= ARENA, at[0]
            if len(shape) == 2:
                a = a.rearrange("p (a b) -> p a b", b=shape[1])
            if len(shape) == 3:
                a = a.rearrange("p (a b c) -> p a b c", b=shape[1], c=shape[2])
            return a

        lora_w, lora_a = part(T), part(T)
        sig_g = part(T)
        ws = part(2, P)
        kx, rx, vx, aa = part(T), part(T), part(T), part(T)
        lw, cc = part(NCH, PAD), part(NCH, PAD)
        e_pos, e_neg = part(NCH, PAD), part(NCH, PAD)
        rw_late = at[0]
        kk, kkr, sc1, sc2 = part(T), part(T), part(T), part(T)
        fa, bb, rrk = part(T), part(T), part(T)
        Bf, Kf = part(NCH, P), part(NCH, P)
        bonus, gate, ysb = part(T), part(T), part(T)
        Btok, Ktok = part(NCH, P), part(NCH, P)
        BG, KG = part(NCH, 4, P), part(NCH, 4, P)
        X, XT, CT, Y1 = part(2, NCH, P), part(2, NCH, P), part(2, NCH, P), part(2, NCH, P)
        Usb = part(P)
        Sf = part(P)
        fS = part(4)
        AR = part(NCH, 4, P)
        Vp = part(NCH * 2 * P + P)
        SAp = part(3 * P)
        S = part(P)

        at[0] = rw_late
        hn_a = (part(2, T), part(2, T), part(2, T))
        qm_a = part(2, T)
        memx, memh, mem_rs = part(KD, NMEM), part(KD, NMEM), part(NMEM)
        wmem = part(KD, 2 * MEMH * HD)
        at[0] = rw_late + 8 * T
        qs_a, pm_a, pt_a = part(2, P), part(MEMH, NMEM), part(2, MEMH, T)
        bank = [ctx.enter_context(nc.psum_tensor(f"bank{i}", [P, T], F32)) for i in range(8)]
        mem_attn = [dict(q=qm_a, qs=qs_a, p=pm_a, pt=pt_a, y=6),
                    dict(q=qm_b, qs=qs_b[:, :, :], p=pm_b[:, :, :], pt=pt_b[:, :, :, :], y=2)]
        landed = [sem(f"landed{i}") for i in range(SLOTS)]
        used = sem("ring_used")

        def flat(a):
            return a.rearrange("p a b -> p (a b)")

        def out_bank(e, m):
            return m % (KD - 1) if e == 0 else m % 2 if e == 3 else 4 + m % 2

        def blocks(a, v, odd):
            return a.rearrange("p (n w b) -> p n w b", w=2, b=2 << v)[:, :, odd, :]

        def diag(a, base=0):
            return a[:, base:base + 3 * P].rearrange("p (h w) -> p h w", w=3 * HD)[:, :, 0:HD]

        def by_residue(a):
            return a.rearrange("p (u r) -> p r u", r=RES)

        def unit(s):
            return U_K + s if s < 6 else U_K + s - 6

        def heads_of(u):
            raw, sq, rs = (hz, y[:, 0:2, :], y[:, 2:4, :]) if u >= U_K else hn_a
            n = NMEM if memory_key(u) else T
            return raw[:, u % 2, 0:n], sq[:, u % 2, 0:n], rs[:, u % 2, 0:n], n

        block = ctx.enter_context(nc.Block())

        @block.sync
        def _(sp):
            sp.dma_start(memx, memT).then_inc(sem("mem_in"), 16)
            sp.dma_start(cst[:, :], consts).then_inc(sem("tables_in"), 16)
            sp.dma_start(par[:, :], params).then_inc(sem("tables_in"), 16)
            sp.dma_start(wmem, w_mem[0]).then_inc(sem("wmem_in"), 16)
            sp.dma_start(x0[:, :, :], xT).then_inc(sem("x_in"), 16)

            def ring_tile(n, i, wide=False):
                w = SLOTW if wide else TILEW
                sp.dma_start(ring[:, i, 0:w], w_ring[bass.ds(n, 1), :, 0:w].rearrange("a p w -> (a p) w"))\
                  .then_inc(landed[i], 16)

            for n in range(SLOTS):
                ring_tile(n, n)
            sp.wait_ge(sem("mv_mm"), 2)
            sp.dma_start(wmem, w_mem[1]).then_inc(sem("wmem_in"), 16)
            sp.dma_start(ws, w_small[0].rearrange("p (a m) -> p a m", m=P)).then_inc(sem("ws_in"), 16)
            sp.wait_ge(used, N_OUTA)
            for i in range(3):
                sp.dma_start(ring[:, i, 0:TILEW], w_pairs[0, i]).then_inc(sem(f"wp_in{i}"), 16)
            with sp.Fori(1, PAIRS) as j:
                for i in range(3):
                    sp.wait_ge(sem("krv_mm"), 3 * j + (i - 2))
                    sp.dma_start(ring[:, i, 0:TILEW],
                                 w_pairs[bass.ds(j, 1), i, :, :].rearrange("a p w -> (a p) w"))\
                      .then_inc(sem(f"wp_in{i}"), 16)
                sp.wait_ge(sem("g_mm"), j)
                sp.dma_start(ws, w_small[bass.ds(j, 1)].rearrange("a p (b m) -> (a p) b m", m=P))\
                  .then_inc(sem("ws_in"), 16)
            for n in range(N_OUTA, N_OUTA + SLOTS):
                sp.wait_ge(sem("krv_mm"), 3 * (PAIRS - 1) + min(n - N_OUTA, 2) + 1)
                ring_tile(n, n % SLOTS)
            sp.dma_start(x[:, :, :], xT).then_inc(sem("x_in"), 16)

            def stream(n0, n1):
                turns = (n1 - n0) // SLOTS
                if turns > 1:
                    with sp.Fori(0, turns) as i:
                        for b in range(SLOTS):
                            one(SLOTS * i + (n0 + b), n0 + b)
                    n0 += SLOTS * turns
                for n in range(n0, n1):
                    one(n, n)

            def one(n, like):
                if isinstance(n, int) and n < N_SPLIT + SLOTS:
                    sp.wait_ge(used, n - SLOTS + 1)
                else:
                    sp.wait_ge(sem("w_lo"), n - (N_SPLIT + SLOTS - 1))
                ring_tile(n, like % SLOTS, width(like) == SLOTW)

            for n in range(N_SPLIT, N_MLP0):
                one(n, n)
            for half in range(2):
                up, down = mlp_tiles(0, half)
                stream(up, down)
                stream(down, down + KD)
            stream(N_K, N_K + SLOTS)
            sp.wait_ge(sem("x_up"), 3 * KD)
            sp.dma_start(rope[:, :, :], ropes).then_inc(sem("rope_in"), 16)
            stream(N_K + SLOTS, N_MLP1)
            sp.wait_ge(used, N_OUTB)
            sp.wait_ge(sem("rope_done"), 12)
            sp.dma_start(mask0[:, :, :], masks[:, 0:RES * T].rearrange("p (r t) -> p r t", t=T)).then_inc(sem("mask_in"), 16)
            sp.dma_start(mask12[:, :], masks[:, RES * T:RES * T + 2 * P]).then_inc(sem("mask_in"), 16)
            for half in range(2):
                up, down = mlp_tiles(1, half)
                stream(up, down)
                stream(down, down + KD)
            for m in range(KD):
                sp.wait_ge(sem("x_up"), 5 * KD + m + 1)
                sp.dma_start(outT[m], x[:, m, :]).then_inc(sem("out"), 16)
            sp.wait_ge(sem("out"), 16 * KD)

        @block.tensor
        def _(pe):
            def mm(out, lhsT, rhs, first=True, last=True):
                return nc.tensor.matmul(out, lhsT, rhs, start=first, stop=last, skip_group_check=True)

            def head_sum(u):
                _, sq, _, n = heads_of(u)
                pe.wait_ge(sem("hn_sqd"), u + 1)
                if u >= 2:
                    pe.wait_ge(sem("hn_sd"), u - 1)
                mm(bank[2 + u % 2][:, 0:n], blk, sq).then_inc(sem("hn_ss"), 1)

            def rope_turn(u):
                pe.wait_ge(sem("hn_done"), u + 1)
                if u >= U_K + 2:
                    pe.wait_ge(sem("rope_done"), u - U_K - 1)
                mm(bank[4 + u % 2][:, :], rot, hz[:, u % 2, :]).then_inc(sem("rope_mm"), 1)

            def split_product(out, n, hi, lo, kn, base=0, ready=None, between=lambda k: None):
                for k in range(kn):
                    between(k)
                    if ready:
                        pe.wait_ge(sem(ready[0]), ready[1] + k)
                    ks = slice(base + k * P, base + (k + 1) * P)
                    mm(out, w_hi[:, n % 2, ks], hi[:, k, :], k == 0, False)
                    mm(out, w_hi[:, n % 2, ks], lo[:, k, :], False, False)
                    i = mm(out, w_lo[:, n % 2, ks], hi[:, k, :], False, k == kn - 1)
                return i

            def quarter(out, j, g, first, last):
                n = g if j is None else Q0 + 12 * j + g
                w = (g if j is None else Q0 + g) % QSLOTS
                pe.wait_ge(sem("q_split"), n + 1)
                for b in range(2):
                    k, ks = 2 * (g % 4) + b, slice(b * P, (b + 1) * P)
                    if j is None and g < 4:
                        pe.wait_ge(sem("h_ready"), k + 1)
                    mm(out, q_hi[:, w, ks], h_hi[:, k, :], first and b == 0, False)
                    mm(out, q_hi[:, w, ks], h_lo[:, k, :], False, False)
                    q = mm(out, q_lo[:, w, ks], h_hi[:, k, :], False, last and b == 1)
                return q

            def quartered_tile(out, n):
                for g in range(4 * n, 4 * n + 4):
                    quarter(out, None, g, g % 4 == 0, g % 4 == 3).then_inc(used if g % 4 == 3 else sem("q_used"), 1)

            pe.wait_ge(sem("tables_in"), 32)
            for k in range(KD):
                pe.wait_ge(sem("msq"), k + 1)
                q = mm(bank[6][:, 0:NMEM], ones, memh[:, k, :], k == 0, k == KD - 1)
            q.then_inc(sem("mem_ss"), 1)
            for k in range(KD):
                pe.wait_ge(sem("xsq"), k + 1)
                q = mm(bank[7][:, :], ones, y[:, k, :], k == 0, k == KD - 1)
            q.then_inc(sem("x_ss"), 1)

            def memory_keys_values(l):
                pe.wait_ge(sem("wmem_in"), 16 * (l + 1))
                for i in range(2):
                    u = (U_MK0, U_MK1)[l] + i
                    if u >= 2:
                        pe.wait_ge(sem("hn_sqd"), u - 1)
                    for k in range(KD):
                        pe.wait_ge(sem("memh"), l * KD + k + 1)
                        q = mm(bank[u % 2][:, 0:NMEM], wmem[:, k, i * P:(i + 1) * P], memh[:, k, :], k == 0, k == KD - 1)
                    q.then_inc(sem("mk_mm"), 1)
                if l:
                    pe.wait_ge(sem("shifted"), 2)
                for i in range(2):
                    for k in range(KD):
                        q = mm(bank[4 + i][:, 0:NMEM], memh[:, k, i * P:(i + 1) * P],
                               wmem[:, k, 2 * P:4 * P], k == 0, k == KD - 1)
                    q.then_inc(sem("mv_mm"), 1)
                    if i == 0:
                        for u in range(2):
                            head_sum((U_MK0, U_MK1)[l] + u)

            memory_keys_values(0)
            pe.wait_ge(sem("mv_out"), 2)
            for i in range(2):
                quartered_tile(bank[4 + i][:, :], N_LORA + i)
            for i in range(2):
                pe.wait_ge(sem("hn_sqd"), i + 1)
                quartered_tile(bank[i][:, :], N_QM0 + i)
            for i in range(2):
                head_sum(U_QM0 + i)
            memory_keys_values(1)
            pe.wait_ge(sem("mv_out"), 4)

            def memory_attention(l):
                m = mem_attn[l]

                def scores(c, first):
                    g = 4 * l + c
                    pe.wait_ge(sem("ma_qs"), g + 1)
                    if not first:
                        pe.wait_ge(sem("ma_exp"), 4 * g)
                    for i in range(2):
                        mm(bank[i][:, :], m["qs"][:, i, :], mem_k[:, l, i, :, :].rearrange("p h t -> p (h t)"))\
                            .then_inc(sem("ma_sc"), 1)

                def token_tile(c, first, last):
                    g = 4 * l + c
                    if not last:
                        scores(c + 1, False)
                    pe.wait_ge(sem("ma_pn"), g + 1)
                    if not first:
                        pe.wait_ge(sem("ma_pt"), 2 * g)
                    for t in range(2):
                        for hh in range(MEMH):
                            q = nc.tensor.transpose(bank[2 + t][:, hh * P:(hh + 1) * P],
                                                    m["p"][:, hh, t * P:(t + 1) * P], ident)
                        q.then_inc(sem("ma_tr"), 1)

                scores(0, True)
                four_rounds(pe, token_tile)
                pe.wait_ge(sem("ma_pt"), 8 * l + 8)
                for hh in range(MEMH):
                    r = HD * (hh % 2)
                    for t in range(2):
                        q = mm(bank[4 + hh // 2][r:r + HD, :], mem_v[:, l, t, hh * HD:(hh + 1) * HD],
                               m["pt"][:, t, hh, :], t == 0, t == 1)
                    if hh % 2:
                        q.then_inc(sem("ma_o"), 1)

            memory_attention(0)

            def chain(j, c, hop):
                if hop == 0:
                    if c == 0:
                        pe.wait_ge(sem("dx_add"), ADDS * (j + 1))
                        pe.wait_ge(sem("v_tok"), j + 1)
                    else:
                        pe.wait_ge(sem("s_up"), 3 * j + c)
                    for hh in range(2):
                        o = bank[4][:, hh * P:(hh + 1) * P]
                        if c:
                            mm(o, AR[:, c, 2 * hh, :], S, True, False)
                        q = mm(o, KG[:, c, 2 * hh, :], diag(Vp, 2 * P * c), c == 0, True)
                    q.then_inc(sem("u_mm"), 1)
                elif hop == 1:
                    pe.wait_ge(sem("u_sb"), NCH * j + c + 1)
                    for hh in range(2):
                        q = mm(bank[4][:, hh * P:(hh + 1) * P], XT[:, hh, c, :], Usb)
                    q.then_inc(sem("sa_mm"), 1)
                else:
                    pe.wait_ge(sem("sa_sb"), NCH * j + c + 1)
                    o = bank[7][:, c * P:(c + 1) * P]
                    if c < NCH - 1:
                        q = mm(bank[5][:, 0:P], Btok[:, c, :], diag(SAp), True, False)
                        q = mm(bank[5][:, 0:P], Ktok[:, c, :], diag(Vp, 2 * P * c), False, True)
                    if c:
                        mm(o, S, AR[:, c, 1, :], True, False)
                        q = mm(o, S, AR[:, c, 3, :], False, False)
                    if c < NCH - 1:
                        q.then_inc(sem("st_mm"), 1)
                    for hh in range(2):
                        mm(o, SAp[:, hh * P:(hh + 1) * P], BG[:, c, 2 * hh + 1, :], c == 0 and hh == 0, False)
                        q = mm(o, Vp[:, 2 * P * c + hh * P:2 * P * c + (hh + 1) * P], KG[:, c, 2 * hh + 1, :],
                               False, hh == 1)
                    q.then_inc(sem("y_mm"), 1)

            def to_tokens(src, sig):
                for c in range(NCH):
                    q = nc.tensor.transpose(bank[5][:, c * P:(c + 1) * P], src[:, c * P:(c + 1) * P], ident)
                q.then_inc(sem(sig), 1)

            def mean_of(j):
                pe.wait_ge(sem("y_sb"), j + 1)
                mm(bank[6][:, :], blk, ysb).then_inc(sem("mean_mm"), 1)

            def variance_of(j):
                pe.wait_ge(sem("y_sq"), j + 1)
                mm(bank[7][:, :], blk, sc1).then_inc(sem("var_mm"), 1)

            def pair(j, first):
                pe.wait_ge(sem("ws_in"), 16 * (j + 1))
                if not first:
                    pe.wait_ge(sem("g_sb"), j)
                mm(bank[0][:, :], ws[:, 0, :], lora_w).then_inc(sem("w_mm"), 1)
                if not first:
                    pe.wait_ge(sem("bonus"), j)
                mm(bank[1][:, :], ws[:, 0, :], lora_a).then_inc(sem("a_mm"), 1)
                for g in range(12):
                    if not first:
                        chain(j - 1, g // 3, g % 3)
                    if g == 8:
                        pe.wait_ge(sem("kk_sq"), j + 1)
                        pe.wait_ge(sem("w_sig"), j + 1)
                        mm(bank[0][:, :], blk, sc1).then_inc(sem("kkss_mm"), 1)
                    t, b = g // 4, KRV_BANKS[g // 4]
                    if g % 4 == 0:
                        if t == 2:
                            pe.wait_ge(sem("a_sig"), j + 1)
                    quarter(bank[b][:, :], j, g, g % 4 == 0, g % 4 == 3)\
                        .then_inc(sem("krv_mm" if g % 4 == 3 else "q_used"), 1)
                pe.wait_ge(sem("kf"), j + 1)
                to_tokens(flat(Kf), "kt_mm")
                pe.wait_ge(sem("kk_sd"), j + 1)
                mm(bank[0][:, :], ws[:, 1, :], sig_g).then_inc(sem("g_mm"), 1)
                if not first:
                    mean_of(j - 1)
                pe.wait_ge(sem("shifted"), 3 * j + 5)
                pe.wait_ge(sem("k_tok"), j + 1)
                to_tokens(vx, "vt_mm")
                pe.wait_ge(sem("rk"), j + 1)
                mm(bank[1][:, :], blk, rrk).then_inc(sem("bonus_mm"), 1)
                pe.wait_ge(sem("bf"), j + 1)
                pe.wait_ge(sem("v_tok"), j + 1)
                to_tokens(flat(Bf), "bt_mm")
                if not first:
                    variance_of(j - 1)
                pe.wait_ge(sem("ar"), j + 1)
                for c in range(NCH):
                    if c:
                        pe.wait_ge(sem("kg_ev"), NCH * j + c)
                    mm(bank[2][:, :], Kf[:, c, :], flat(AR[:, c, :, :])).then_inc(sem("kg_mm"), 1)
                    if c:
                        pe.wait_ge(sem("bg_ev"), NCH * j + c)
                    mm(bank[3][:, :], Bf[:, c, :], flat(AR[:, c, :, :])).then_inc(sem("bg_mm"), 1)
                    if c:
                        pe.wait_ge(sem("x_l1"), NCH * j + c)
                    for hh in range(2):
                        q = mm(bank[4][:, hh * P:(hh + 1) * P], AR[:, c, 2 * hh, :], Bf[:, c, :])
                    q.then_inc(sem("m_mm"), 1)
                pe.wait_ge(sem("kg_ev"), NCH * j + NCH)
                pe.wait_ge(sem("b_tok"), j + 1)
                if not first:
                    pe.wait_ge(sem("y_sd"), j)
                for v in range(LEVELS):
                    for hh in range(2):
                        if v:
                            pe.wait_ge(sem("ct"), MASKS * j + (NCH + 2 * (v - 1) + hh + 1))
                            pe.wait_ge(sem("dx_add"), ADDS * j + (4 * (v - 1) + 2 * hh + 1))
                        for c in range(NCH):
                            if v == 0 and hh == 0:
                                pe.wait_ge(sem("ct"), MASKS * j + (c + 1))
                                pe.wait_ge(sem("x_one"), NCH * j + (c + 1))
                            q = mm(bank[2 + hh][:, c * P:(c + 1) * P], CT[:, hh, c, :], X[:, hh, c, :])
                        q.then_inc(sem("y1_mm"), 1)
                    for hh in range(2):
                        pe.wait_ge(sem("y1_sb"), 2 * LEVELS * j + (2 * v + hh + 1))
                        if v == 0:
                            pe.wait_ge(sem("xt_one"), j + 1)
                        else:
                            pe.wait_ge(sem("dx_add"), ADDS * j + (4 * (v - 1) + 2 * hh + 2))
                        for odd in range(v == LEVELS - 1, 2):
                            for c in range(NCH):
                                o = bank[4 + 2 * hh + odd][:, c * HP:(c + 1) * HP].rearrange("p (n b) -> p n b", b=2 << v)
                                if odd:
                                    q = mm(o, Y1[:, hh, c, :], blocks(XT[:, hh, c, :], v, 1))
                                else:
                                    q = mm(o, XT[:, hh, c, :], blocks(Y1[:, hh, c, :], v, 0))
                            q.then_inc(sem("dx_mm"), 1)

            pe.wait_ge(sem("lora_in"), 3)
            pe.wait_ge(sem("ma_y"), 2)
            rounds(pe, PAIRS, pair)

            pe.wait_ge(sem("g_sb"), PAIRS)
            pe.wait_ge(sem("bonus"), PAIRS)
            pe.wait_ge(sem("y_out"), PAIRS - 1)
            ready_k = [k for k in range(KD) if k != PAIRS - 1]

            def early(a, b):
                for m, k in [(m, k) for m in range(SLOTS) for k in ready_k][a:b]:
                    if k == 0:
                        pe.wait_ge(landed[m], 16 * ((N_OUTA + m) // SLOTS + 1))
                    mm(bank[m][:, :], ring[:, m, k * P:(k + 1) * P], y[:, k, :], k == 0, False)

            for g in range(12):
                chain(PAIRS - 1, g // 3, g % 3)
                early(g, g + 1)
            early(12, 14)
            mean_of(PAIRS - 1)
            early(14, 18)
            variance_of(PAIRS - 1)
            early(18, SLOTS * len(ready_k))
            pe.wait_ge(sem("y_out"), PAIRS)
            for m in range(SLOTS):
                k = PAIRS - 1
                mm(bank[m][:, :], ring[:, m, k * P:(k + 1) * P], y[:, k, :], False, True).then_inc(used, 1)

            def split_ready(n):
                pe.wait_ge(sem("w_lo"), n - (N_SPLIT - 1))

            def out_product(e, n0, m0, kn, y_at, per_slot):
                for m in range(m0, KD):
                    n, b = n0 + m // per_slot, m % per_slot
                    split_ready(n)
                    if e:
                        pe.wait_ge(sem("x_up"), KD * e + m - 1)
                    elif m == KD - 1:
                        pe.wait_ge(sem("x_up"), 1)
                    q = split_product(bank[out_bank(e, m)][:, :], n, in_hi, in_lo, kn, b * kn * P,
                                      ("y_split", y_at + 1) if m == m0 else None)
                    q.then_inc(used if b == per_slot - 1 else sem("out_half"), 1)
                square_sum(e // 3 * 2)

            def square_sum(q):
                pe.wait_ge(sem("sq_sum"), (KD - 2) * (q + 1))
                mm(bank[7][:, :], ones, y[:, 0, :], True, False)
                pe.wait_ge(sem("xsq"), KD * (q + 2))
                mm(bank[7][:, :], ones, y[:, KD - 1, :], False, True).then_inc(sem("x_ss"), 1)

            out_product(0, N_OUTA, SLOTS, KD, 0, 1)

            def mlp(l, h_at):
                for half in range(2):
                    up, down = mlp_tiles(l, half)
                    g0 = FT * l + HALF * half

                    def up_pair(p, q):
                        if not isinstance(p, int) or g0 + p >= 2:
                            pe.wait_ge(sem("conv_done"), p + (g0 - 1))
                        for s in range(2):
                            n = up + 2 * q + s
                            split_ready(2 * p + (up + s))
                            b = 2 * ((g0 + q) % 2) + s
                            split_product(bank[b][:, :], n, in_hi, in_lo, KD,
                                          ready=("h_ready", h_at + 1) if q == 0 and s == 0 and half == 0 else None)\
                                .then_inc(used, 1)

                    mlp_pairs(pe, up_pair)
                    e = 3 * l + 1 + half
                    with pe.Fori(0, 2) as i:
                        for b in range(SLOTS):
                            split_ready(SLOTS * i + (down + b))
                            pe.wait_ge(sem("x_up"), SLOTS * i + (KD * e + b - 1))
                            for k in range(HALF):
                                if b == 0:
                                    pe.wait_ge(sem("z"), g0 + k + 1)
                                ks = slice(k * P, (k + 1) * P)
                                w = (down + b) % 2
                                o = bank[4 + b % 2][:, :]
                                mm(o, w_hi[:, w, ks], z_hi[:, k, :], k == 0, False)
                                mm(o, w_hi[:, w, ks], z_lo[:, k, :], False, False)
                                q = mm(o, w_lo[:, w, ks], z_hi[:, k, :], False, k == HALF - 1)
                            q.then_inc(used, 1)
                if l == 0:
                    square_sum(1)

            mlp(0, KD)

            pe.wait_ge(sem("zeroed"), 4)
            for s in range(22):
                def behind(k):
                    if k == 2 and 6 <= s - 1 < 12:
                        i = s - 7
                        pe.wait_ge(sem("pos_read"), s)
                        if i >= 2:
                            pe.wait_ge(sem("v_ev"), i - 1)
                        src = by_residue(y[:, (s - 1) % 2, :])
                        for r in range(RES):
                            q = nc.tensor.transpose(bank[6 + i % 2][:, r * P:(r + 1) * P], src[:, r, :], ident)
                        q.then_inc(sem("v_mm2"), 1)
                    elif k == 2 and 0 <= s - 1 < 20:
                        head_sum(unit(s - 1))
                    if k == 3 and 0 <= s - 2 < 18 and not 6 <= s - 2 < 12:
                        rope_turn(unit(s - 2))

                if s < 20:
                    n = N_K + s
                    split_ready(n)
                    if s >= 2:
                        pe.wait_ge(sem("pos_read"), s - 1)
                    split_product(bank[s % 2][:, :], n, b_hi, b_lo, KD, between=behind,
                                  ready=("h_ready", (2 if s == 0 else 3) * KD + 1) if s in (0, 12) else None)\
                        .then_inc(used, 1)
                else:
                    behind(2)
                    behind(3)

            pe.wait_ge(sem("rope_done"), 12)
            pe.wait_ge(sem("hn_done"), U_END)
            pe.wait_ge(sem("v_ev"), 6)

            def scores(r, s, first):
                if not (first and s < 2):
                    pe.wait_ge(sem("da_sm"), 4 * r + (s - 1))
                if s == 0:
                    pe.wait_ge(sem("da_stage"), r + 1)
                rs, b = bass.ds(r * P, P), 2 * (s % 2)
                mm(bank[b][:, :], qS[:, s // 2, :], kp[:, s, :])
                mm(bank[b + 1][:, 0:P], qS[:, 2 + s // 2, :], kp[:, SLOTS + s, rs])
                mm(bank[b + 1][:, P:2 * P], qS[:, 4 + s // 2, :], kp[:, 2 * SLOTS + s, rs])\
                    .then_inc(sem("da_sc"), 1)

            def outputs(r, s, first):
                if s == 0:
                    pe.wait_ge(sem("da_vstage"), r + 1)
                pe.wait_ge(sem("da_pt"), 4 * r + (s + 1))
                if s == 3:
                    pe.wait_ge(sem("da_y"), 4 * r + 1)
                elif not first:
                    pe.wait_ge(sem("da_y"), 4 * r + (s - 3))
                o = bank[6 + s // 2][HD * (s % 2):HD * (s % 2) + HD, 0:P]
                for q in range(6):
                    at = ((q - RES) * 4 + s) * HD
                    v = vtok[:, q, s * HD:(s + 1) * HD] if q < RES else vS[:, at:at + HD]
                    i = mm(o, v, pT[:, s % 2, q * P:(q + 1) * P], q == 0, q == 5)
                i.then_inc(sem("da_o"), 1)

            def residue(r, first, last):
                for s in range(4):
                    if s < 2 or not last:
                        scores(r + (s + 2) // 4, (s + 2) % 4, first and s < 2)
                    if s:
                        outputs(r, s - 1, first)
                    elif not first:
                        outputs(r - 1, 3, False)
                    pe.wait_ge(sem("da_pn"), 4 * r + (s + 1))
                    if not (first and s == 0):
                        pe.wait_ge(sem("da_pt"), 4 * r + s)
                    for q in range(6):
                        i = nc.tensor.transpose(bank[4 + q // 4][:, (q % 4) * P:(q % 4 + 1) * P],
                                                pr[:, s % 2, q * P:(q + 1) * P], ident)
                    i.then_inc(sem("da_tr"), 1)

            scores(0, 0, True)
            scores(0, 1, True)
            four_rounds(pe, residue)
            outputs(RES - 1, 3, False)
            pe.wait_ge(sem("da_y"), 4 * RES)
            memory_attention(1)
            pe.wait_ge(sem("ma_y"), 4)
            out_product(3, N_OUTB, 0, 4, KD, 2)
            mlp(1, 4 * KD)

        @block.scalar
        def _(act):
            def root(out, in_, count, eps):
                return nc.scalar.activation(out, in_, ACT.Sqrt, bias=eps, scale=1.0 / count)

            def copy(out, in_):
                return nc.scalar.activation(out, in_, ACT.Copy)

            act.wait_ge(sem("mem_in"), 16)
            for k in range(KD):
                nc.scalar.activation(memh[:, k, :], memx[:, k, :], ACT.Square).then_inc(sem("msq"), 1)
            act.wait_ge(sem("x_in"), 16)
            for k in range(KD):
                nc.scalar.activation(y[:, k, :], x0[:, k, :], ACT.Square).then_inc(sem("xsq"), 1)
            act.wait_ge(sem("derived"), 2)
            act.wait_ge(sem("mem_ss"), 1)
            root(mem_rs, bank[6][:, 0:NMEM], D, rms_eps).then_inc(sem("mem_sd"), 1)

            def stream_root(e):
                act.wait_ge(sem("x_ss"), e + 1)
                root(rstd[:, :], bank[7][:, :], D, rms_eps).then_inc(sem("x_sd"), 1)

            stream_root(0)

            def norm_split(q, hi, raw):
                for k in range(KD):
                    act.wait_ge(sem("n_raw"), KD * (q + 1) + k + 1)
                    copy(hi[:, k, :], raw[:, k % 2, :]).then_inc(sem("in_hi"), 1)

            def head_out(u):
                raw, sq, _, n = heads_of(u)
                if memory_key(u):
                    act.wait_ge(sem("mk_mm"), u + 1 if u < U_QM0 else u - 1)
                else:
                    act.wait_ge(used, (N_QM0 + u - U_QM0 if u < U_K else N_K + u - U_K + 6 * (u >= U_Q)) + 1)
                if u >= 2:
                    act.wait_ge(sem("hn_done"), u - 1)
                    act.wait_ge(sem("hn_ss"), u - 1)
                if u >= U_K + 2:
                    act.wait_ge(sem("rope_done"), min(u - U_K - 1, 12))
                copy(raw, bank[u % 2][:, 0:n])
                nc.scalar.activation(sq, bank[u % 2][:, 0:n], ACT.Square).then_inc(sem("hn_sqd"), 1)
                if u >= U_K:
                    act.wait_ge(sem("hn_sqd"), u + 1)
                    act.sem_inc(sem("pos_read"), 1)

            def head_root(u):
                _, _, rs, n = heads_of(u)
                act.wait_ge(sem("hn_ss"), u + 1)
                if u >= 2:
                    act.wait_ge(sem("hn_done"), u - 1)
                if U_K + 2 <= u:
                    act.wait_ge(sem("rope_done"), min(u - U_K - 1, 12))
                root(rs, bank[2 + u % 2][:, 0:n], HD, rms_eps).then_inc(sem("hn_sd"), 1)

            def memory_keys_values(l):
                for i in range(2):
                    head_out((U_MK0, U_MK1)[l] + i)
                if l == 0:
                    norm_split(-1, h_hi, y)
                for i in range(2):
                    act.wait_ge(sem("mv_mm"), 2 * l + i + 1)
                    copy(mem_v[:, l, i, :], bank[4 + i][:, 0:NMEM]).then_inc(sem("mv_out"), 1)
                    if i == 0:
                        for u in range(2):
                            head_root((U_MK0, U_MK1)[l] + u)

            memory_keys_values(0)

            act.wait_ge(sem("derived"), 4)
            for i, dst in enumerate((kx, rx)):
                act.wait_ge(used, N_LORA + i + 1)
                nc.scalar.activation(dst, bank[4 + i][:, :], ACT.Identity,
                                     scale=derived[:, PAIRS * NPAR + i:PAIRS * NPAR + i + 1]).then_inc(sem("own"), 1)
            for i in range(2):
                head_out(U_QM0 + i)
            for i in range(2):
                head_root(U_QM0 + i)
            memory_keys_values(1)
            act.wait_ge(sem("shifted"), 2)
            act.wait_ge(sem("zeroed"), 2)
            nc.scalar.activation(lora_w[0:HD], kx[0:HD], ACT.Tanh).then_inc(sem("lora_in"), 1)
            copy(lora_a[HD:P], kx[HD:P]).then_inc(sem("lora_in"), 1)
            nc.scalar.activation(sig_g, rx, ACT.Sigmoid).then_inc(sem("lora_in"), 1)

            def memory_attention(l):
                m = mem_attn[l]

                def exps(c, first):
                    g = 4 * l + c
                    if not first:
                        act.wait_ge(sem("ma_tr"), 2 * g)
                    for i in range(2):
                        act.wait_ge(sem("ma_nb"), 2 * g + i + 1)
                        for hh in range(2):
                            k = 2 * i + hh
                            nc.scalar.activation(m["p"][:, k, :], bank[i][:, hh * NMEM:(hh + 1) * NMEM], ACT.Exp,
                                                 bias=stat[:, 4 + k:5 + k], scale=HD ** -0.5,
                                                 accum_out=stat[:, 8 + k:9 + k]).then_inc(sem("ma_exp"), 1)

                def token_tile(c, first, last):
                    g = 4 * l + c
                    if not last:
                        exps(c + 1, False)
                    for t in range(2):
                        act.wait_ge(sem("ma_tr"), 2 * g + t + 1)
                        copy(m["pt"][:, t, :, bass.ds(c * P, P)], bank[2 + t][:, :].rearrange("p (h t) -> p h t", t=P))\
                            .then_inc(sem("ma_pt"), 1)

                exps(0, True)
                four_rounds(act, token_tile)
                for i in range(2):
                    act.wait_ge(sem("ma_o"), 2 * l + i + 1)
                    copy(y[:, m["y"] + i, :], bank[4 + i][:, :]).then_inc(sem("ma_y"), 1)

            memory_attention(0)

            def bchunks(a):
                return a.rearrange("p (c t) -> p c t", t=CHUNK)

            def hop_u(j, c):
                act.wait_ge(sem("u_mm"), NCH * j + c + 1)
                copy(Usb.rearrange("p (h w) -> p h w", w=HD), diag(bank[4])).then_inc(sem("u_sb"), 1)

            def hop_sa(j, c):
                act.wait_ge(sem("sa_mm"), NCH * j + c + 1)
                copy(diag(SAp), diag(bank[4])).then_inc(sem("sa_sb"), 1)

            def y_read(j):
                act.wait_ge(sem("y_mm"), NCH * (j + 1))
                copy(ysb, bank[7][:, :]).then_inc(sem("y_sb"), 1)

            def y_square(j):
                act.wait_ge(sem("yc"), j + 1)
                nc.scalar.activation(sc1, ysb, ACT.Square).then_inc(sem("y_sq"), 1)

            def y_root(j):
                act.wait_ge(sem("var_mm"), j + 1)
                root(sc2, bank[7][:, :], HD, lnx_eps).then_inc(sem("y_sd"), 1)

            def y_affine(j):
                act.wait_ge(sem("yn"), j + 1)
                nc.scalar.activation(ysb, ysb, ACT.Identity, scale=pcol(j, LNW), bias=pcol(j, LNB))\
                    .then_inc(sem("y_ln"), 1)

            def own_part(dst, b, j, k, sig):
                nc.scalar.activation(dst, bank[b][:, :], ACT.Identity, scale=dcol(j, k)).then_inc(sem(sig), 1)

            def pair(j, first):
                act.wait_ge(sem("w_mm"), j + 1)
                nc.scalar.activation(lw[:, :, 1:], bchunks(bank[0][:, :]), ACT.Sigmoid, bias=pcol(j, PW0))\
                    .then_inc(sem("w_sig"), 1)
                act.wait_ge(sem("a_mm"), j + 1)
                nc.scalar.activation(aa, bank[1][:, :], ACT.Sigmoid, bias=pcol(j, PA0)).then_inc(sem("a_sig"), 1)
                if not first:
                    hop_u(j - 1, 0)
                act.wait_ge(sem("a_sig"), j + 1)
                nc.scalar.activation(fa, aa, ACT.Identity, scale=pcol(j, KAP), bias=dcol(j, KAP)).then_inc(sem("fa"), 1)
                if not first:
                    hop_sa(j - 1, 0)
                act.wait_ge(sem("cc"), j + 1)
                nc.scalar.activation(e_pos, cc, ACT.Exp, scale=DECAY)
                nc.scalar.activation(e_neg, cc, ACT.Exp, scale=-DECAY).then_inc(sem("e_neg"), 1)
                if not first:
                    hop_u(j - 1, 1)
                act.wait_ge(sem("krv_mm"), 3 * j + 1)
                own_part(kx, KRV_BANKS[0], j, MUK, "own")
                if not first:
                    hop_sa(j - 1, 1)
                    hop_u(j - 1, 2)
                act.wait_ge(sem("shifted"), 3 * j + 3)
                nc.scalar.activation(kkr, kx, ACT.Identity, scale=pcol(j, KKP)).then_inc(sem("kkr"), 1)
                act.wait_ge(sem("kkr"), j + 1)
                nc.scalar.activation(sc1, kkr, ACT.Square).then_inc(sem("kk_sq"), 1)
                if not first:
                    hop_sa(j - 1, 2)
                act.wait_ge(sem("krv_mm"), 3 * j + 2)
                own_part(rx, KRV_BANKS[1], j, MUR, "own")
                act.wait_ge(sem("kkss_mm"), j + 1)
                nc.scalar.activation(sc2, bank[0][:, :], ACT.Sqrt).then_inc(sem("kk_sd"), 1)
                if not first:
                    hop_u(j - 1, 3)
                    hop_sa(j - 1, 3)
                act.wait_ge(sem("krv_mm"), 3 * j + 3)
                own_part(vx, KRV_BANKS[2], j, MUV, "own")
                if not first:
                    y_read(j - 1)
                act.wait_ge(sem("kt_mm"), j + 1)
                copy(flat(Ktok), bank[5][:, :]).then_inc(sem("k_tok"), 1)
                act.wait_ge(sem("vt_mm"), j + 1)
                v_to_tokens()
                if not first:
                    y_square(j - 1)
                act.wait_ge(sem("bt_mm"), j + 1)
                copy(flat(Btok), bank[5][:, :]).then_inc(sem("b_tok"), 1)
                if not first:
                    act.wait_ge(sem("kk_n"), j + 1)
                    y_root(j - 1)
                for i in range(2 * LEVELS):
                    act.wait_ge(sem("y1_mm"), 2 * LEVELS * j + i + 1)
                    copy(flat(Y1[:, i % 2, :, :]), bank[2 + i % 2][:, :]).then_inc(sem("y1_sb"), 1)
                    if i == 1:
                        if not first:
                            y_affine(j - 1)
                    if i == 3:
                        if not first:
                            act.wait_ge(sem("y_out"), j)
                        act.wait_ge(sem("g_mm"), j + 1)
                        copy(gate, bank[0][:, :]).then_inc(sem("g_sb"), 1)

            def v_to_tokens():
                for hh in range(2):
                    dst = Vp[:, 0:NCH * 2 * P].rearrange("p (c w) -> p c w", w=2 * P)[:, :, 3 * HD * hh:3 * HD * hh + HD]
                    src = bank[5][:, :].rearrange("p (c w) -> p c w", w=P)[:, :, HD * hh:HD * (hh + 1)]
                    q = copy(dst, src)
                q.then_inc(sem("v_tok"), 1)

            act.wait_ge(sem("zeroed"), 3)
            rounds(act, PAIRS, pair)
            j = PAIRS - 1
            for c in range(NCH):
                hop_u(j, c)
                hop_sa(j, c)
            y_read(j)
            y_square(j)
            y_root(j)
            y_affine(j)

            def split(n):
                if n >= N_END:
                    return
                i, w = n % SLOTS, width(n)
                act.wait_ge(landed[i], 16 * (n // SLOTS + 1))
                if n >= N_SPLIT + 2:
                    act.wait_ge(used, n - 1)
                copy(w_hi[:, n % 2, 0:w], ring[:, i, 0:w]).then_inc(sem("w_hi"), 1)

            def squares(n0, e, slots):
                for m in range(KD):
                    n = n0 + int(slots * (m + 1)) + 1
                    due = (slots == 1 or m % 2 == 1) and n >= N_SPLIT + 2
                    if due and m == KD - 1:
                        split(n)
                    if e in (0, 2, 3):
                        act.wait_ge(sem("x_up"), KD * e + m + 1)
                        nc.scalar.activation(y[:, m, :], x[:, m, :], ACT.Square).then_inc(sem("xsq"), 1)
                    if due and m < KD - 1:
                        split(n)

            act.wait_ge(sem("y_out"), PAIRS)
            split(N_SPLIT)
            for k in range(KD):
                copy(in_hi[:, k, :], y[:, k, :]).then_inc(sem("in_hi"), 1)
            split(N_SPLIT + 1)
            squares(N_OUTA, 0, 1)
            stream_root(1)

            def tap(l, tile, k):
                return par[:, bass.ds(4 * tile + (G_CONV + l * 2 * FT * 4 + k), 1)]

            def mlp(l):
                for half in range(2):
                    up, down = mlp_tiles(l, half)
                    g0 = FT * l + HALF * half

                    def up_pair(p, q):
                        b = (g0 + q) % 2
                        for s in range(2):
                            split_at(p, up + 2 + s, q)
                            act.wait_ge(used, 2 * p + (up + s + 1))
                            if s == 0 and (not isinstance(p, int) or g0 + p >= 2):
                                act.wait_ge(sem("z"), p + (g0 - 1))
                            tile = 2 * p + (2 * HALF * half + s)
                            nc.scalar.activation(conv[:, 2 * b + s, :], bank[2 * b + s][:, :], ACT.Identity,
                                                 scale=tap(l, tile, 2), bias=tap(l, tile, 3)).then_inc(sem("conv_own"), 1)
                        act.wait_ge(sem("conv_gate"), p + (g0 + 1))
                        nc.scalar.activation(silu[:, b, :], conv[:, 2 * b, :], ACT.Silu).then_inc(sem("silu"), 1)
                        act.wait_ge(sem("z_raw"), p + (g0 + 1))
                        copy(z_hi[:, bass.ds(p, 1), :], z_raw[:, b, :].unsqueeze(1)).then_inc(sem("z_hi"), 1)

                    mlp_pairs(act, up_pair)
                    squares(down, 3 * l + 1 + half, 1)

            def split_at(p, n0, q):
                n = n0 + 2 * q
                i, w = n % SLOTS, width(n)
                if isinstance(p, int):
                    return split(n)
                turn = (n0 + 2 * q) // SLOTS + 1
                act.wait_ge(landed[i], 8 * (p - q) + 16 * turn)
                act.wait_ge(used, 2 * p + (n0 - 1))
                copy(w_hi[:, n % 2, 0:w], ring[:, i, 0:w]).then_inc(sem("w_hi"), 1)

            norm_split(0, in_hi, in_raw)
            mlp(0)
            stream_root(2)
            norm_split(1, b_hi, b_raw)
            for s in range(21):
                if 6 <= s - 1 < 12:
                    i = s - 7
                    act.wait_ge(sem("v_mm2"), i + 1)
                    copy(vtok[:, :, i * P:(i + 1) * P], bank[6 + i % 2][:, :].rearrange("p (r f) -> p r f", f=P))\
                        .then_inc(sem("v_ev"), 1)
                elif s:
                    head_root(unit(s - 1))
                if s < 20:
                    if 6 <= s < 12:
                        act.wait_ge(used, N_K + s + 1)
                        copy(y[:, s % 2, :], bank[s % 2][:, :]).then_inc(sem("pos_read"), 1)
                    else:
                        head_out(unit(s))
                    split(N_K + s + 2)
                if s == 11:
                    act.wait_ge(used, N_Q)
                    norm_split(2, b_hi, b_raw)

            def exps(r, s, first):
                act.wait_ge(sem("da_nb"), 4 * r + (s + 1))
                if not (first and s < 2):
                    act.wait_ge(sem("da_tr"), 4 * r + (s - 1))
                nc.scalar.activation(pr[:, s % 2, :], sm[:, s % 2, :], ACT.Exp, bias=stat[:, 18 + s % 2:19 + s % 2],
                                     scale=HD ** -0.5, accum_out=stat[:, 20 + s % 2:21 + s % 2]).then_inc(sem("da_exp"), 1)

            def output(r, s):
                act.wait_ge(sem("da_o"), 4 * r + (s + 1))
                hs = slice(HD * (s % 2), HD * (s % 2) + HD)
                copy(by_residue(y[:, s // 2, :])[hs, bass.ds(r, 1), :],
                     bank[6 + s // 2][hs, 0:P].unsqueeze(1)).then_inc(sem("da_y"), 1)

            def residue(r, first, last):
                for s in range(4):
                    if s < 3 or not last:
                        exps(r + (s + 1) // 4, (s + 1) % 4, first and s < 3)
                    act.wait_ge(sem("da_tr"), 4 * r + (s + 1))
                    if not (first and s < 2):
                        act.wait_ge(sem("da_o"), 4 * r + (s - 1))
                    copy(pT[:, s % 2, 0:T], bank[4][:, :])
                    copy(pT[:, s % 2, T:6 * P], bank[5][:, 0:2 * P]).then_inc(sem("da_pt"), 1)
                    if s:
                        output(r, s - 1)
                    elif not first:
                        output(r - 1, 3)

            exps(0, 0, True)
            four_rounds(act, residue)
            output(RES - 1, 3)
            act.wait_ge(sem("da_y"), 4 * RES)
            for k in range(2):
                copy(in_hi[:, k, :], y[:, k, :]).then_inc(sem("in_hi"), 1)
            memory_attention(1)
            act.wait_ge(sem("ma_y"), 4)
            for k in range(2, 4):
                copy(in_hi[:, k, :], y[:, k, :]).then_inc(sem("in_hi"), 1)
            squares(N_OUTB, 3, 0.5)
            stream_root(3)
            norm_split(3, in_hi, in_raw)
            mlp(1)

        @block.vector
        def _(dve):
            V = nc.vector
            V.memset(epsb[:, 0:1], RMS_EPS).then_inc(sem("derived"), 1)
            V.memset(epsb[:, 1:2], LNX_EPS).then_inc(sem("derived"), 1)
            dve.wait_ge(sem("tables_in"), 32)
            V.tensor_scalar(derived[:, 0:PAIRS * NPAR], par[:, G_PAIR:G_END], -1.0, 1.0, ALU.mult, ALU.add)\
                .then_inc(sem("derived"), 1)
            V.tensor_scalar(derived[:, PAIRS * NPAR:PAIRS * NPAR + 2], par[:, MU_WA:MU_WA + 2], -1.0, 1.0, ALU.mult, ALU.add)\
                .then_inc(sem("derived"), 1)

            dve.wait_ge(sem("mem_sd"), 1)
            V.reciprocal(mem_rs, mem_rs).then_inc(sem("mem_rc"), 1)
            dve.wait_ge(sem("mem_rc"), 1)
            dve.wait_ge(sem("zeroed"), 2)

            def scaled(dst, src, gain, by, sig):
                return V.scalar_tensor_tensor(out=dst, in0=src, scalar=gain, in1=by, op0=ALU.mult, op1=ALU.mult)\
                    .then_inc(sem(sig), 1)

            def stream_rstd(e):
                dve.wait_ge(sem("x_sd"), e + 1)
                V.reciprocal(rstd[:, :], rstd[:, :]).then_inc(sem("x_rc"), 1)
                dve.wait_ge(sem("x_rc"), e + 1)

            def lower(dst, src, high, sig):
                V.tensor_tensor(dst, src, high.bitcast(F32), ALU.subtract).then_inc(sem(sig), 1)

            def input_low(hi, lo, src, k, at, sig):
                dve.wait_ge(sem("in_hi"), KD + at + k + 1)
                lower(lo[:, k, :], src, hi[:, k, :], sig)

            def norm_split(q, gain, hi, lo, raw, at, x=x):
                for k in range(KD + 1):
                    if 2 <= k < KD:
                        dve.wait_ge(sem("h_ready"), KD * (q + 1) + k - 1)
                    if k < KD:
                        scaled(raw[:, k % 2, :], x[:, k, :], col(gain + k), rstd[:, :], "n_raw")
                    if k:
                        input_low(hi, lo, raw[:, (k - 1) % 2, :], k - 1, at, "h_ready")

            def split(n, like=None):
                if isinstance(n, int) and n >= N_END:
                    return
                like = n if like is None else like
                w = width(like)
                dve.wait_ge(sem("w_hi"), n - (N_SPLIT - 1))
                lower(w_lo[:, like % 2, 0:w], ring[:, like % SLOTS, 0:w], w_hi[:, like % 2, 0:w], "w_lo")

            def head_norm(u, gain):
                raw, _, rs, n = heads_of(u)
                dve.wait_ge(sem("hn_sd"), u + 1)
                V.reciprocal(rs, rs).then_inc(sem("hn_rc"), 1)
                dve.wait_ge(sem("hn_rc"), u + 1)
                if memory_key(u):
                    l, i = u // U_MK1, u % 2
                    for hh in range(2):
                        hs = slice(HD * hh, HD * hh + HD)
                        q = V.scalar_tensor_tensor(out=mem_k[hs, l, i, hh, :], in0=raw[hs], scalar=par[hs, gain:gain + 1],
                                                   in1=rs[hs], op0=ALU.mult, op1=ALU.mult)
                    q.then_inc(sem("hn_done"), 1)
                    return
                dst = qm_a[:, u % 2, :] if u < U_K else hz[:, u % 2, :] if u < U_QM1 else qm_b[:, u % 2, :]
                scaled(dst, raw, col(gain), rs, "hn_done")

            for k in range(KD):
                scaled(memh[:, k, :], memx[:, k, :], col(G_MEM0 + k), mem_rs, "memh")
            stream_rstd(0)
            norm_split(-1, G_ATTN0, h_hi, h_lo, y, -KD, x0)
            for i in range(2):
                head_norm(i, G_MK0)
            dve.wait_ge(sem("mv_mm"), 2)
            for k in range(KD):
                scaled(memh[:, k, :], memx[:, k, :], col(G_MEM1 + k), mem_rs, "memh")

            def shifted(dst, src, mu, sig):
                V.scalar_tensor_tensor(out=dst[:, 1:T], in0=src[:, 0:T - 1], scalar=mu, in1=dst[:, 1:T],
                                       op0=ALU.mult, op1=ALU.add).then_inc(sem(sig), 1)

            for i, dst in enumerate((kx, rx)):
                dve.wait_ge(sem("own"), i + 1)
                shifted(dst, bank[4 + i], col(MU_WA + i), "shifted")
            for i in range(2):
                head_norm(U_QM0 + i, G_MQ0)
            for i in range(2):
                head_norm(U_MK1 + i, G_MK1)

            def memory_attention(l):
                m = mem_attn[l]

                def softmax_bound(c):
                    g = 4 * l + c
                    for i in range(2):
                        dve.wait_ge(sem("ma_sc"), 2 * g + i + 1)
                        V.tensor_reduce(stat[:, 2 * i:2 * i + 2], bank[i][:, :].rearrange("p (h t) -> p h t", t=NMEM),
                                        AX.X, ALU.max).then_inc(sem("ma_mx"), 1)
                        dve.wait_ge(sem("ma_mx"), 2 * g + i + 1)
                        V.tensor_scalar(stat[:, 4 + 2 * i:6 + 2 * i], stat[:, 2 * i:2 * i + 2], -HD ** -0.5, None, ALU.mult)\
                            .then_inc(sem("ma_nb"), 1)

                def token_tile(c, first, last):
                    g = 4 * l + c
                    dve.wait_ge(sem("ma_exp"), 4 * g + 4)
                    V.reciprocal(stat[:, 12:16], stat[:, 8:12]).then_inc(sem("ma_rd"), 1)
                    dve.wait_ge(sem("ma_rd"), g + 1)
                    V.tensor_tensor(m["p"], m["p"], stat[:, 12:16].unsqueeze(2).to_broadcast([P, MEMH, NMEM]), ALU.mult)\
                        .then_inc(sem("ma_pn"), 1)
                    if not last:
                        softmax_bound(c + 1)

                softmax_bound(0)
                four_rounds(dve, token_tile)

            memory_attention(0)

            def halves():
                return (slice(0, HD), 0), (slice(HD, P), 1)

            def state(j, c):
                if c:
                    dve.wait_ge(sem("s_up"), 3 * j + c)
                    V.tensor_scalar(Sf, S, fS[:, c:c + 1], None, ALU.mult).then_inc(sem("sf"), 1)
                dve.wait_ge(sem("st_mm"), 3 * j + c + 1)
                dve.wait_ge(sem("fs"), j + 1)
                if c:
                    dve.wait_ge(sem("sf"), 2 * j + c)
                for hs, hh in halves():
                    cs = slice(HD * hh, HD * hh + HD)
                    if c == 0:
                        q = V.tensor_scalar(S[hs, cs], bank[5][hs, cs], fS[hs, 0:1], None, ALU.mult)
                    else:
                        q = V.scalar_tensor_tensor(out=S[hs, cs], in0=bank[5][hs, cs], scalar=fS[hs, c:c + 1],
                                                   in1=Sf[hs, cs], op0=ALU.mult, op1=ALU.add)
                q.then_inc(sem("s_up"), 1)

            def centre(j):
                dve.wait_ge(sem("mean_mm"), j + 1)
                V.scalar_tensor_tensor(out=ysb, in0=bank[6][:, :], scalar=-1.0 / HD, in1=ysb, op0=ALU.mult, op1=ALU.add)\
                    .then_inc(sem("yc"), 1)

            def normalise(j):
                dve.wait_ge(sem("y_sd"), j + 1)
                V.reciprocal(sc2, sc2).then_inc(sem("y_rc"), 1)
                dve.wait_ge(sem("y_rc"), j + 1)
                V.tensor_tensor(ysb, ysb, sc2, ALU.mult).then_inc(sem("yn"), 1)

            def finish(j):
                dve.wait_ge(sem("y_ln"), j + 1)
                V.tensor_tensor(ysb, ysb, bonus, ALU.add).then_inc(sem("y_b"), 1)
                dve.wait_ge(sem("y_b"), j + 1)
                V.tensor_tensor(y[:, bass.ds(j, 1), :], ysb.unsqueeze(1), gate.unsqueeze(1), ALU.mult)\
                    .then_inc(sem("y_out"), 1)

            def pair(j, first):
                dve.wait_ge(sem("w_sig"), j + 1)
                V.tensor_tensor_scan(flat(lw), reset, flat(lw), 0.0, ALU.mult, ALU.add).then_inc(sem("cum"), 1)
                dve.wait_ge(sem("cum"), j + 1)
                V.tensor_tensor(cc, lw, lw[:, :, CHUNK // 2:CHUNK // 2 + 1].to_broadcast([P, NCH, PAD]), ALU.subtract)\
                    .then_inc(sem("cc"), 1)
                if not first:
                    state(j - 1, 0)
                dve.wait_ge(sem("own"), 3 * j + 3)
                shifted(kx, bank[KRV_BANKS[0]], pcol(j, MUK), "shifted")
                if not first:
                    state(j - 1, 1)
                dve.wait_ge(sem("fa"), j + 1)
                dve.wait_ge(sem("kkr"), j + 1)
                dve.wait_ge(sem("shifted"), 3 * j + 3)
                V.tensor_tensor(kx, kx, fa, ALU.mult).then_inc(sem("k2"), 1)
                dve.wait_ge(sem("own"), 3 * j + 4)
                shifted(rx, bank[KRV_BANKS[1]], pcol(j, MUR), "shifted")
                if not first:
                    state(j - 1, 2)
                dve.wait_ge(sem("shifted"), 3 * j + 4)
                dve.wait_ge(sem("k2"), j + 1)
                V.scalar_tensor_tensor(out=rrk, in0=rx, scalar=pcol(j, RKP), in1=kx, op0=ALU.mult, op1=ALU.mult)\
                    .then_inc(sem("rk"), 1)
                dve.wait_ge(sem("e_neg"), j + 1)
                V.tensor_tensor(Kf, kx.rearrange("p (c t) -> p c t", t=P), e_neg[:, :, 1:], ALU.mult).then_inc(sem("kf"), 1)
                dve.wait_ge(sem("kk_sd"), j + 1)
                V.tensor_scalar(sc2, sc2, 1e-12, None, ALU.max).then_inc(sem("kk_mx"), 1)
                dve.wait_ge(sem("kk_mx"), j + 1)
                V.reciprocal(sc2, sc2).then_inc(sem("kk_rc"), 1)
                dve.wait_ge(sem("kk_rc"), j + 1)
                V.tensor_tensor(kk, kkr, sc2, ALU.mult).then_inc(sem("kk_n"), 1)
                dve.wait_ge(sem("own"), 3 * j + 5)
                shifted(vx, bank[KRV_BANKS[2]], pcol(j, MUV), "shifted")
                dve.wait_ge(sem("bb"), j + 1)
                V.tensor_tensor(Bf, bb.rearrange("p (c t) -> p c t", t=P), e_neg[:, :, 1:], ALU.mult).then_inc(sem("bf"), 1)
                if not first:
                    dve.wait_ge(sem("y_mm"), NCH * j)
                    centre(j - 1)
                dve.wait_ge(sem("shifted"), 3 * j + 4)
                for hs, hh in halves():
                    V.scalar_tensor_tensor(out=AR[hs, :, 2 * hh, :], in0=kk[hs].rearrange("p (c t) -> p c t", t=P),
                                           scalar=-1.0, in1=e_pos[hs, :, 0:CHUNK], op0=ALU.mult, op1=ALU.mult)
                    q = V.tensor_tensor(AR[hs, :, 2 * hh + 1, :], rx[hs].rearrange("p (c t) -> p c t", t=P),
                                        e_pos[hs, :, 1:], ALU.mult)
                q.then_inc(sem("ar"), 1)
                tri2 = tri.unsqueeze(1).to_broadcast([P, 2, 2 * P])
                for c in range(NCH):
                    for G, b, n in ((KG, 2, "kg"), (BG, 3, "bg")):
                        dve.wait_ge(sem(n + "_mm"), NCH * j + c + 1)
                        V.tensor_tensor(flat(G[:, c, :, :]).rearrange("p (h w) -> p h w", w=2 * P),
                                        bank[b][:, :].rearrange("p (h w) -> p h w", w=2 * P), tri2, ALU.mult)\
                            .then_inc(sem(n + "_ev"), 1)
                    dve.wait_ge(sem("m_mm"), NCH * j + c + 1)
                    V.tensor_tensor(X[:, :, c, :], bank[4][:, 0:2 * P].rearrange("p (h t) -> p h t", t=P),
                                    level(LEVELS + 1).unsqueeze(1).to_broadcast([P, 2, P]), ALU.mult).then_inc(sem("x_l1"), 1)
                    dve.wait_ge(sem("x_l1"), NCH * j + c + 1)
                    V.tensor_tensor(X[:, :, c, :], X[:, :, c, :], ident.unsqueeze(1).to_broadcast([P, 2, P]), ALU.add)\
                        .then_inc(sem("x_one"), 1)
                if not first:
                    normalise(j - 1)
                for v in range(LEVELS):
                    for hh in range(2):
                        for odd in range(v == LEVELS - 1, 2):
                            n = ADDS * j + (4 * v + hh + 1 if v == LEVELS - 1 else 4 * v + 2 * hh + odd + 1)
                            dve.wait_ge(sem("dx_mm"), n)
                            xf = blocks(flat((X, XT)[odd][:, hh, :, :]), v, odd)
                            V.tensor_tensor(xf, bank[4 + 2 * hh + odd][:, 0:NCH * HP].rearrange("p (n b) -> p n b", b=2 << v),
                                            xf, ALU.add).then_inc(sem("dx_add"), 1)
                    if v == 0:
                        if not first:
                            finish(j - 1)
                        dve.wait_ge(sem("bonus_mm"), j + 1)
                        V.tensor_tensor(bonus, bank[1][:, :], vx, ALU.mult).then_inc(sem("bonus"), 1)

            dve.wait_ge(sem("zeroed"), 3)
            rounds(dve, PAIRS, pair)
            for c in range(NCH - 1):
                state(PAIRS - 1, c)
            centre(PAIRS - 1)
            normalise(PAIRS - 1)
            finish(PAIRS - 1)

            def residual(n0, e, slots):
                for m in range(KD):
                    if slots < 1 and m % 2 == 0:
                        dve.wait_ge(sem("out_half"), m // 2 + 1)
                    else:
                        dve.wait_ge(used, n0 + int(slots * (m + 1)))
                    if e:
                        dve.wait_ge(sem("x_up"), KD * (e - 1) + m + 1)
                    elif m == 0:
                        dve.wait_ge(sem("x_in"), 32)
                    V.tensor_tensor(x[:, m, :], bank[out_bank(e, m)][:, :], x[:, m, :], ALU.add).then_inc(sem("x_up"), 1)
                    n = n0 + int(slots * (m + 1)) + 1
                    if (slots == 1 or m % 2 == 1) and n >= N_SPLIT + 2:
                        split(n)

            split(N_SPLIT)
            for k in range(KD):
                input_low(in_hi, in_lo, y[:, k, :], k, 0, "y_split")
            split(N_SPLIT + 1)
            residual(N_OUTA, 0, 1)
            stream_rstd(1)
            norm_split(0, G_FFN0, in_hi, in_lo, in_raw, KD)

            def tap(l, tile, k):
                return par[:, bass.ds(4 * tile + (G_CONV + l * 2 * FT * 4 + k), 1)]

            def mlp(l, in_at):
                for half in range(2):
                    up, down = mlp_tiles(l, half)
                    g0 = FT * l + HALF * half

                    def up_pair(p, q):
                        b = (g0 + q) % 2
                        for s in range(2):
                            c = conv[:, 2 * b + s, :]
                            split(2 * p + (up + 2 + s), up + 2 + s + 2 * q)
                            for lag in (1, 2):
                                if lag == 1:
                                    dve.wait_ge(sem("conv_own"), 2 * p + (2 * g0 + s + 1))
                                else:
                                    dve.wait_ge(sem("conv_one"), 2 * p + (2 * g0 + s + 1))
                                V.scalar_tensor_tensor(out=c[:, lag:T], in0=bank[2 * b + s][:, 0:T - lag],
                                                       scalar=tap(l, 2 * p + (2 * HALF * half + s), 2 - lag), in1=c[:, lag:T],
                                                       op0=ALU.mult, op1=ALU.add)\
                                    .then_inc(sem("conv_one" if lag == 1 else ("conv_gate", "conv_done")[s]), 1)
                        dve.wait_ge(sem("z_hi"), p + (g0 + 1))
                        lower(z_lo[:, bass.ds(p, 1), :], z_raw[:, b, :].unsqueeze(1), z_hi[:, bass.ds(p, 1), :], "z")

                    mlp_pairs(dve, up_pair)
                    residual(down, 3 * l + 1 + half, 1)

            mlp(0, 2 * KD)
            stream_rstd(2)
            dve.wait_ge(sem("x_up"), 3 * KD)
            norm_split(1, G_KV, b_hi, b_lo, b_raw, 2 * KD)

            def turn(u):
                v = u - U_K
                dve.wait_ge(sem("rope_mm"), v + 1)
                dve.wait_ge(sem("rope_in"), 16)
                rz = heads_of(u)[2]
                V.tensor_tensor(rz, bank[4 + u % 2][:, :], sinT, ALU.mult).then_inc(sem("rope_sin"), 1)
                dve.wait_ge(sem("rope_sin"), v + 1)
                dve.wait_ge(sem("rope_cos"), v + 1)
                if u < U_Q:
                    for hs, hh in halves():
                        q = V.tensor_tensor(kp[hs, 2 * v + hh, :].rearrange("p (r u) -> p r u", r=RES),
                                            by_residue(t1[hs, u % 2, :]), by_residue(rz[hs]), ALU.add)
                else:
                    q = V.tensor_tensor(qT[:, v - 6, :].rearrange("p (r u) -> p r u", r=RES),
                                        by_residue(t1[:, u % 2, :]), by_residue(rz), ALU.add)
                q.then_inc(sem("rope_done"), 1)

            dve.wait_ge(sem("zeroed"), 4)
            for s in range(22):
                if 0 <= s - 2 < 18 and not 6 <= s - 2 < 12:
                    turn(unit(s - 2))
                if 0 <= s - 1 < 20 and not 6 <= s - 1 < 12:
                    u = unit(s - 1)
                    head_norm(u, G_KN if u < U_Q else G_QN if u < U_QM1 else G_MQ1)
                if s == 11:
                    norm_split(2, G_ATTN1, b_hi, b_lo, b_raw, 3 * KD)

            def softmax_bound(r, s, first):
                g, b = 4 * r + s, s % 2
                dve.wait_ge(sem("da_sc"), g + 1)
                if not (first and s < 2):
                    dve.wait_ge(sem("da_exp"), g - 1)
                V.tensor_tensor(sm[:, b, 0:T].unsqueeze(1), bank[2 * b][:, :].unsqueeze(1), mask0[:, bass.ds(r, 1), :], ALU.add)
                V.tensor_tensor(sm[:, b, T:6 * P], bank[2 * b + 1][:, 0:2 * P], mask12[:, :], ALU.add).then_inc(sem("da_sm"), 1)
                dve.wait_ge(sem("da_sm"), g + 1)
                V.tensor_reduce(stat[:, 16 + b:17 + b], sm[:, b, :], AX.X, ALU.max).then_inc(sem("da_mx"), 1)
                dve.wait_ge(sem("da_mx"), g + 1)
                V.tensor_scalar(stat[:, 18 + b:19 + b], stat[:, 16 + b:17 + b], -HD ** -0.5, None, ALU.mult)\
                    .then_inc(sem("da_nb"), 1)

            def residue(r, first, last):
                for s in range(4):
                    if s < 3 or not last:
                        softmax_bound(r + (s + 1) // 4, (s + 1) % 4, first and s < 3)
                    g, b = 4 * r + s, s % 2
                    dve.wait_ge(sem("da_exp"), g + 1)
                    V.reciprocal(stat[:, 22 + b:23 + b], stat[:, 20 + b:21 + b]).then_inc(sem("da_rd"), 1)
                    dve.wait_ge(sem("da_rd"), g + 1)
                    V.tensor_scalar(pr[:, b, :], pr[:, b, :], stat[:, 22 + b:23 + b], None, ALU.mult).then_inc(sem("da_pn"), 1)

            dve.wait_ge(sem("mask_in"), 32)
            softmax_bound(0, 0, True)
            four_rounds(dve, residue)
            dve.wait_ge(sem("w_lo"), N_OUTB + 2 - N_SPLIT)
            for k in range(2):
                input_low(in_hi, in_lo, y[:, k, :], k, 4 * KD, "y_split")
            memory_attention(1)
            for k in range(2, 4):
                input_low(in_hi, in_lo, y[:, k, :], k, 4 * KD, "y_split")
            residual(N_OUTB, 3, 0.5)
            stream_rstd(3)
            norm_split(3, G_FFN1, in_hi, in_lo, in_raw, 4 * KD + 4)
            mlp(1, 0)

        @block.gpsimd
        def _(pool):
            G = nc.gpsimd

            G.memset(mem_k[:, :, :, :, :], 0.0).then_inc(sem("zeroed"), 1)
            G.memset(arena[:, 0:2 * T], 0.0).then_inc(sem("zeroed"), 1)

            def memory_attention(l):
                m = mem_attn[l]

                def token_tile(c, first):
                    g = 4 * l + c
                    if not first:
                        pool.wait_ge(sem("ma_sc"), 2 * g)
                    G.tensor_copy(m["qs"], m["q"][:, :, bass.ds(c * P, P)]).then_inc(sem("ma_qs"), 1)

                pool.wait_ge(sem("hn_done"), (U_K, U_END)[l])
                rounds(pool, RES, token_tile)

            def split_quarter(j, g):
                t = g // 4
                w = (g if j is None else Q0 + g) % QSLOTS
                if g % 4 == 0:
                    if j is None:
                        pool.wait_ge(landed[t], 16)
                    else:
                        pool.wait_ge(sem(f"wp_in{t}"), 16 * (j + 1))
                if j is None:
                    o = g - QSLOTS
                    if o >= 0 and o % 4 == 3:
                        pool.wait_ge(used, o // 4 + 1)
                    elif o >= 0:
                        pool.wait_ge(sem("q_used"), 3 * (o // 4) + o % 4 + 1)
                elif g == QSLOTS - 1 and isinstance(j, int):
                    pool.wait_ge(used, N_OUTA)
                elif g == QSLOTS - 1:
                    pool.wait_ge(sem("krv_mm"), 3 * j)
                elif (g - QSLOTS) % 4 == 3:
                    pool.wait_ge(sem("krv_mm"), 3 * j + (g - QSLOTS) // 4 + 1)
                else:
                    o = g - QSLOTS
                    pool.wait_ge(sem("q_used"), 9 * j + (3 * N_OUTA + 3 * (o // 4) + o % 4 + 1))
                src = ring[:, t, (g % 4) * QW:(g % 4 + 1) * QW]
                n = g if j is None else Q0 + 12 * j + g
                G.tensor_tensor(q_hi[:, w, :], src, ones[:, 0:1].to_broadcast([P, QW]), ALU.mult)\
                    .then_inc(sem("q_high"), 1)
                pool.wait_ge(sem("q_high"), n + 1)
                G.tensor_tensor(q_lo[:, w, :], src, q_hi[:, w, :].bitcast(F32), ALU.subtract).then_inc(sem("q_split"), 1)

            for g in range(Q0):
                split_quarter(None, g)
            memory_attention(0)
            for g in range(QSLOTS):
                split_quarter(0, g)
            pool.wait_ge(sem("ma_y"), 2)
            G.memset(flat(lw)[:, 0:NCH * PAD:PAD], 0.0)
            G.memset(AR, 0.0)
            G.memset(Vp, 0.0)
            G.memset(SAp, 0.0)
            G.memset(S, 0.0).then_inc(sem("zeroed"), 1)

            def pair(j, first):
                for g in range(QSLOTS if first else 0, 12):
                    split_quarter(j, g)
                pool.wait_ge(sem("kk_n"), j + 1)
                G.tensor_tensor(bb, kk, aa, ALU.mult).then_inc(sem("bb"), 1)
                pool.wait_ge(sem("e_neg"), j + 1)
                if not first:
                    pool.wait_ge(sem("s_up"), 3 * j)
                G.tensor_tensor(fS[:, 0:NCH - 1].unsqueeze(2), e_pos[:, 0:NCH - 1, CHUNK:PAD], e_neg[:, 1:NCH, 0:1], ALU.mult)\
                    .then_inc(sem("fs"), 1)
                for c in range(NCH):
                    pool.wait_ge(sem("bg_ev"), NCH * j + c + 1)
                    b = BG[:, c, 0:4:2, :]
                    G.tensor_tensor(CT[:, :, c, :], b, both(level(1)), ALU.mult).then_inc(sem("ct"), 1)
                    G.tensor_tensor(XT[:, :, c, :], b, both(level(0)), ALU.mult).then_inc(sem("xt_l1"), 1)
                    pool.wait_ge(sem("xt_l1"), NCH * j + c + 1)
                    q = G.tensor_tensor(XT[:, :, c, :], XT[:, :, c, :], both(ident), ALU.add)
                q.then_inc(sem("xt_one"), 1)
                for v in range(1, LEVELS):
                    for hh in range(2):
                        pool.wait_ge(sem("y1_mm"), 2 * LEVELS * j + (2 * (v - 1) + hh + 1))
                        G.tensor_tensor(CT[:, hh, :, :], BG[:, :, 2 * hh, :],
                                        level(v + 1).unsqueeze(1).to_broadcast([P, NCH, P]), ALU.mult).then_inc(sem("ct"), 1)

            def both(a):
                return a.unsqueeze(1).to_broadcast([P, 2, P])

            rounds(pool, PAIRS, pair)

            def sum_squares(q):
                for m in range(1, KD - 1):
                    pool.wait_ge(sem("xsq"), KD * (q + 1) + m + 1)
                    if m > 1:
                        pool.wait_ge(sem("sq_sum"), (KD - 2) * q + m - 1)
                    G.tensor_tensor(y[:, 0, :], y[:, 0, :], y[:, m, :], ALU.add).then_inc(sem("sq_sum"), 1)

            def mlp(l):
                for half in range(2):
                    g0 = FT * l + HALF * half

                    def up_pair(p, q):
                        b = (g0 + q) % 2
                        pool.wait_ge(sem("silu"), p + (g0 + 1))
                        pool.wait_ge(sem("conv_done"), p + (g0 + 1))
                        if not isinstance(p, int) or g0 + p >= 2:
                            pool.wait_ge(sem("z"), p + (g0 - 1))
                        G.tensor_tensor(z_raw[:, b, :], silu[:, b, :], conv[:, 2 * b + 1, :], ALU.mult).then_inc(sem("z_raw"), 1)

                    mlp_pairs(pool, up_pair)

            sum_squares(0)
            mlp(0)
            sum_squares(1)
            pool.wait_ge(sem("x_up"), 3 * KD)
            G.memset(kp[:, :, :], 0.0).then_inc(sem("zeroed"), 1)
            pool.wait_ge(sem("w_lo"), N_K + 2 - N_SPLIT)
            for s in range(21):
                if s < 20:
                    n = N_K + s + 2
                    w = width(n)
                    pool.wait_ge(sem("w_hi"), n - (N_SPLIT - 1))
                    G.tensor_tensor(w_lo[:, n % 2, 0:w], ring[:, n % SLOTS, 0:w], w_hi[:, n % 2, 0:w].bitcast(F32),
                                    ALU.subtract).then_inc(sem("w_lo"), 1)
                if s and unit(s - 1) < U_QM1 and not 6 <= s - 1 < 12:
                    u = unit(s - 1)
                    pool.wait_ge(sem("rope_in"), 16)
                    pool.wait_ge(sem("hn_done"), u + 1)
                    if u >= U_K + 2:
                        pool.wait_ge(sem("rope_done"), u - U_K - 1)
                    G.tensor_tensor(t1[:, u % 2, :], hz[:, u % 2, :], cosT, ALU.mult).then_inc(sem("rope_cos"), 1)

            def queries(r):
                G.tensor_copy(qS[:, :, :], qT[:, :, bass.ds(r * P, P)]).then_inc(sem("da_stage"), 1)

            def values(r):
                G.tensor_copy(vS[:, :].unsqueeze(1), vtok[:, bass.ds(r, 1), 2 * P:6 * P]).then_inc(sem("da_vstage"), 1)

            def residue(r, first):
                if not first:
                    pool.wait_ge(sem("da_o"), 4 * r)
                    values(r)
                pool.wait_ge(sem("da_sc"), 4 * r + 4)
                queries(r + 1)

            pool.wait_ge(used, N_OUTB)
            pool.wait_ge(sem("v_ev"), 6)
            pool.wait_ge(sem("rope_done"), 12)
            queries(0)
            values(0)
            rounds(pool, RES - 1, residue)
            pool.wait_ge(sem("da_o"), 4 * (RES - 1))
            values(RES - 1)
            pool.wait_ge(sem("da_y"), 4 * RES)
            memory_attention(1)
            sum_squares(2)
            mlp(1)


def shape_constants():
    i = np.arange(P)
    cst = np.zeros((P, C_END), np.float32)
    cst[:, C_ID:C_ID + P] = np.eye(P)
    cst[:, C_ONE:C_ONE + P] = 1
    cst[:, C_BLK:C_BLK + P] = i[:, None] // HD == i[None] // HD
    half = HD // 2
    turn = np.zeros((P, P), np.float32)
    for m in range(P):
        if m % HD < half:
            turn[m + half, m] = -1
        else:
            turn[m - half, m] = 1
    cst[:, C_ROT:C_ROT + P] = turn
    s, t = i[:, None], i[None]
    cst[:, C_TRI:C_TRI + P] = s < t
    cst[:, C_TRI + P:C_TRI + 2 * P] = s <= t
    for v in range(LEVELS + 1):
        b = 1 << v
        cst[:, C_LEV + v * P:C_LEV + (v + 1) * P] = (s // b + 1 == t // b) & (t // b % 2 == 1)
    cst[:, C_LEV + (LEVELS + 1) * P:C_RESET] = cst[:, C_LEV:C_LEV + P].T
    cst[:, C_RESET:C_END] = np.tile((np.arange(PAD) > 0).astype(np.float32), NCH)
    inv = (10000.0 ** (-np.arange(0, HD, 2, dtype=np.float32) / np.float32(HD))).astype(np.float32)
    ang = np.arange(T, dtype=np.float32)[:, None] * inv[None, :]
    rope = np.stack([np.tile(f(ang).T, (4, 1)) for f in (np.cos, np.sin)], axis=1).astype(np.float32)
    tok = np.arange(T).reshape(P, RES).T
    keys = tok.reshape(-1)
    masks = np.zeros((P, RES * T + 2 * P), np.float32)
    for r in range(RES):
        dist = tok[r][:, None] - keys[None]
        masks[:, r * T:(r + 1) * T] = np.where((dist >= 0) & (dist <= 128), 0, -1e30)
    d = i[:, None] - i[None]
    masks[:, RES * T:RES * T + P] = np.where(d >= 0, 0, -1e30)
    masks[:, RES * T + P:] = np.where((d >= 0) & (d % 4 == 0), 0, -1e30)
    return cst, rope, masks


def tiles_of(w):
    k, n = w.shape
    return w.reshape(k // P, P, n // P, P).transpose(2, 1, 0, 3).reshape(n // P, P, k)


def columns(v):
    return v.reshape(-1, P).T


def kernel(**inputs):
    import concourse.bacc as _bacc
    from concourse.bass_utils import run_bass_kernel_spmd as _run

    a = {k: np.asarray(v) for k, v in inputs.items()}
    f32 = np.float32
    cst, rope, masks = shape_constants()
    W = PAIRS * P

    w_in = tiles_of(a["a_w_in"][0])
    w_pairs = np.stack([np.stack([w_in[6 + j], w_in[j], w_in[12 + j]]) for j in range(PAIRS)])
    w_small = np.zeros((PAIRS, P, 2 * P), f32)
    for j in range(PAIRS):
        js = slice(j * P, (j + 1) * P)
        w_small[j, 0:HD, 0:P] = a["a_w2"][0][:, js]
        w_small[j, HD:P, 0:P] = a["a_a2"][0][:, js]
        w_small[j, :, P:2 * P] = a["a_g2"][0][:, js]

    w_ring = np.zeros((N_END, P, SLOTW), f32)
    w_ring[N_LORA:N_LORA + 2, :, 0:TILEW] = w_in[18:20]
    w_ring[N_QM0:N_QM0 + 2, :, 0:TILEW] = w_in[20:22]
    w_ring[N_OUTA:N_OUTA + KD, :, 0:TILEW] = tiles_of(a["a_w_out"][0])
    kv = tiles_of(a["kv_w"])
    w_ring[N_K:N_K + 6, :, 0:TILEW] = kv[0:6]
    w_ring[N_V:N_V + 6, :, 0:TILEW] = kv[6:12]
    b_in = tiles_of(a["b_w_in"][0])
    w_ring[N_Q:N_Q + 8, :, 0:TILEW] = b_in
    out_b = tiles_of(a["b_w_out"][0])
    w_ring[N_OUTB:N_OUTB + 4, :, 0:TILEW] = out_b.reshape(4, 2, P, 4 * P).transpose(0, 2, 1, 3).reshape(4, P, TILEW)
    for l in range(2):
        u = tiles_of(a["ffn_w_up"][l])
        dn = tiles_of(a["ffn_w_down"][l])
        for half in range(2):
            up, down = mlp_tiles(l, half)
            hs = slice(HALF * half, HALF * (half + 1))
            w_ring[up:down:2, :, 0:TILEW] = u[0:FT][hs]
            w_ring[up + 1:down:2, :, 0:TILEW] = u[FT:2 * FT][hs]
            w_ring[down:down + KD] = dn[:, :, SLOTW * half:SLOTW * (half + 1)]
    w_mem = np.ascontiguousarray(a["mem_w_kv"].reshape(2, KD, P, 2 * MEMH * HD).transpose(0, 2, 1, 3))

    par = np.zeros((P, G_END), f32)
    for l in range(2):
        par[:, (G_ATTN0, G_ATTN1)[l]:][:, 0:KD] = columns(a["attn_norm"][l])
        par[:, (G_FFN0, G_FFN1)[l]:][:, 0:KD] = columns(a["ffn_norm"][l])
        par[:, (G_MEM0, G_MEM1)[l]:][:, 0:KD] = columns(a["mem_norm"][l])
        par[:, (G_MQ0, G_MQ1)[l]] = np.tile(a["mem_q_norm"][l], 2)
        par[:, (G_MK0, G_MK1)[l]] = np.tile(a["mem_k_norm"][l], 2)
        taps = np.concatenate([a["ffn_conv_w"][l], a["ffn_conv_b"][l][None]])
        taps = taps.reshape(4, 2, FT, P).transpose(3, 2, 1, 0)
        par[:, G_CONV + l * 2 * FT * 4:][:, 0:2 * FT * 4] = taps.reshape(P, -1)
    par[:, G_KV:G_KV + KD] = columns(a["kv_norm"])
    par[:, G_KN] = np.tile(a["kv_k_norm"], 2)
    par[:, G_QN] = np.tile(a["b_q_norm"][0], 2)
    mu = a["a_mu"][0]
    par[:, MU_WA] = mu[3 * W:3 * W + P]
    par[:, MU_G] = mu[3 * W + P:3 * W + 2 * P]
    per_pair = (mu[W:2 * W], mu[0:W], mu[2 * W:3 * W], a["a_w0"][0], a["a_a0"][0], a["a_k_k"][0], a["a_k_a"][0],
                a["a_r_k"][0].reshape(-1), a["a_lnx_w"][0], a["a_lnx_b"][0])
    par[:, G_PAIR:G_END] = np.stack([columns(v) for v in per_pair], axis=2).reshape(P, -1)

    arrays = {
        "xT": np.ascontiguousarray(a["x"][0].T.reshape(KD, P, T).transpose(1, 0, 2)),
        "memT": np.ascontiguousarray(a["mem"][0].T.reshape(KD, P, NMEM).transpose(1, 0, 2)),
        "consts": cst, "params": par, "ropes": rope, "masks": masks, "w_small": w_small, "w_mem": w_mem,
        "w_pairs": w_pairs, "w_ring": w_ring,
    }
    nc = _bacc.Bacc("TRN2", target_bir_lowering=False, num_devices=1)
    args = [nc.dram_tensor(k, v.shape, mybir.dt.from_np(v.dtype), kind="ExternalInput").ap() for k, v in arrays.items()]
    args.append(nc.dram_tensor("outT", [KD, P, T], F32, kind="ExternalOutput").ap())
    trunk(nc, *args)
    r = _run(nc, [arrays], core_ids=[0])
    return np.ascontiguousarray(r.results[0]["outT"].reshape(D, T).T).reshape(1, T, D)
```
